# Optimizing a Trainium2 kernel written in Bass

```python
import math
import jax, jax.numpy as jnp
from jax import lax
import numpy as np

D_MODEL = 1024
BATCH = 1
SEQ = 512
DEPTH = 2

N_MIXERS = 2
N_LRU_LAYERS = (DEPTH + 1) // 2
N_FOX_LAYERS = DEPTH // 2
EPS = 1e-6
LRU_WIDTH = 1536
LRU_BLOCKS = 12
LRU_BLOCK_W = LRU_WIDTH // LRU_BLOCKS
CONV_WIDTH = 4
LRU_C = 8.0
FOX_HEADS = 16
FOX_HEAD_DIM = 64
FOX_WIDTH = FOX_HEADS * FOX_HEAD_DIM
Q_BLOCK = 128
NEG_INF = -1e30


def rms_norm(x, g):
    xf = x.astype(jnp.float32)
    y = xf * lax.rsqrt(jnp.mean(xf * xf, axis=-1, keepdims=True) + EPS)
    return (y * g.astype(jnp.float32)).astype(x.dtype)

def causal_depthwise_conv(x, w, b):
    c = x.shape[-1]
    y = lax.conv_general_dilated(
        x, w[:, None, :].astype(x.dtype), window_strides=(1,),
        padding=[(CONV_WIDTH - 1, 0)],
        dimension_numbers=("NWC", "WIO", "NWC"),
        feature_group_count=c)
    return y + b.astype(x.dtype)

def block_diag_linear(x, w, b):
    bsz, s, _ = x.shape
    xb = x.reshape(bsz, s, LRU_BLOCKS, LRU_BLOCK_W)
    y = jnp.einsum("bsnc,ncd->bsnd", xb, w.astype(x.dtype))
    return y.reshape(bsz, s, LRU_WIDTH) + b.astype(x.dtype)

def lru_mixer(h, w_in, conv_w, conv_b, wa, ba, wx, bx, a_param, w_out):
    u = h @ w_in.astype(h.dtype)
    xb, gate = u[..., :LRU_WIDTH], u[..., LRU_WIDTH:]
    xc = causal_depthwise_conv(xb, conv_w, conv_b)
    r = jax.nn.sigmoid(block_diag_linear(xc, wa, ba).astype(jnp.float32))
    i = jax.nn.sigmoid(block_diag_linear(xc, wx, bx).astype(jnp.float32))
    log_a = -LRU_C * r * jax.nn.softplus(-a_param.astype(jnp.float32))
    a = jnp.exp(log_a)
    mult = jnp.sqrt(-jnp.expm1(2.0 * log_a))
    bterm = mult * (i * xc.astype(jnp.float32))

    def combine(lhs, rhs):
        a1, b1 = lhs
        a2, b2 = rhs
        return a1 * a2, a2 * b1 + b2

    _, hs = lax.associative_scan(combine, (a, bterm), axis=1)
    y = hs.astype(h.dtype) * jax.nn.silu(gate)
    return y @ w_out.astype(h.dtype)

def fox_mixer(h, w_in, b_f, w_out):
    bsz, s, _ = h.shape
    u = h @ w_in.astype(h.dtype)
    q = u[..., 0 * FOX_WIDTH:1 * FOX_WIDTH].reshape(bsz, s, FOX_HEADS, FOX_HEAD_DIM)
    k = u[..., 1 * FOX_WIDTH:2 * FOX_WIDTH].reshape(bsz, s, FOX_HEADS, FOX_HEAD_DIM)
    v = u[..., 2 * FOX_WIDTH:3 * FOX_WIDTH].reshape(bsz, s, FOX_HEADS, FOX_HEAD_DIM)
    gate = u[..., 3 * FOX_WIDTH:4 * FOX_WIDTH]
    f_logit = u[..., 4 * FOX_WIDTH:].astype(jnp.float32) + b_f.astype(jnp.float32)
    cum = jnp.cumsum(jax.nn.log_sigmoid(f_logit), axis=1)
    ck = jnp.transpose(cum, (0, 2, 1))
    scale = 1.0 / math.sqrt(FOX_HEAD_DIM)
    n_blocks = s // Q_BLOCK
    qb = jnp.transpose(q.reshape(bsz, n_blocks, Q_BLOCK, FOX_HEADS, FOX_HEAD_DIM), (1, 0, 2, 3, 4))
    cqb = jnp.transpose(cum.reshape(bsz, n_blocks, Q_BLOCK, FOX_HEADS), (1, 0, 3, 2))
    starts = jnp.arange(n_blocks, dtype=jnp.int32) * Q_BLOCK
    kpos = jnp.arange(s, dtype=jnp.int32)
    kf = k.astype(jnp.float32)
    vf = v.astype(jnp.float32)

    def one_block(args):
        q_blk, cq_blk, start = args
        qpos = start + jnp.arange(Q_BLOCK, dtype=jnp.int32)
        logits = jnp.einsum("bqhd,bkhd->bhqk", q_blk.astype(jnp.float32), kf) * scale
        logits = logits + (cq_blk[..., :, None] - ck[:, :, None, :])
        mask = kpos[None, :] <= qpos[:, None]
        logits = jnp.where(mask[None, None], logits, NEG_INF)
        p = jax.nn.softmax(logits, axis=-1)
        return jnp.einsum("bhqk,bkhd->bqhd", p, vf)

    o = lax.map(one_block, (qb, cqb, starts))
    o = jnp.transpose(o, (1, 0, 2, 3, 4)).reshape(bsz, s, FOX_WIDTH).astype(h.dtype)
    y = o * jax.nn.silu(gate)
    return y @ w_out.astype(h.dtype)

def first_inputs(seed: int = 0) -> dict:
    key = jax.random.key(seed)
    ks = jax.random.split(key, 16)
    f32 = jnp.float32
    nl, nf = N_LRU_LAYERS, N_FOX_LAYERS
    x = jax.random.normal(ks[0], (BATCH, SEQ, D_MODEL), f32)
    norm_g = 1.0 + 0.05 * jax.random.normal(ks[1], (DEPTH, D_MODEL), f32)
    final_g = 1.0 + 0.05 * jax.random.normal(ks[2], (D_MODEL,), f32)
    lru_w_in = jax.random.normal(ks[3], (nl, D_MODEL, 2 * LRU_WIDTH), f32) * D_MODEL ** -0.5
    lru_conv_w = jax.random.normal(ks[4], (nl, CONV_WIDTH, LRU_WIDTH), f32) * CONV_WIDTH ** -0.5
    lru_conv_b = 0.02 * jax.random.normal(ks[5], (nl, LRU_WIDTH), f32)
    lru_wa = jax.random.normal(ks[6], (nl, LRU_BLOCKS, LRU_BLOCK_W, LRU_BLOCK_W), f32) * LRU_BLOCK_W ** -0.5
    lru_ba = 0.02 * jax.random.normal(ks[7], (nl, LRU_WIDTH), f32)
    lru_wx = jax.random.normal(ks[8], (nl, LRU_BLOCKS, LRU_BLOCK_W, LRU_BLOCK_W), f32) * LRU_BLOCK_W ** -0.5
    lru_bx = 0.02 * jax.random.normal(ks[9], (nl, LRU_WIDTH), f32)
    a_c = jax.random.uniform(ks[10], (nl, LRU_WIDTH), f32, minval=0.9, maxval=0.999)
    a0 = a_c ** (1.0 / LRU_C)
    lru_a_param = jnp.log(a0) - jnp.log1p(-a0)
    lru_w_out = jax.random.normal(ks[11], (nl, LRU_WIDTH, D_MODEL), f32) * LRU_WIDTH ** -0.5
    fox_w_in = jax.random.normal(ks[12], (nf, D_MODEL, 4 * FOX_WIDTH + FOX_HEADS), f32) * D_MODEL ** -0.5
    fox_b_f = 3.0 + 0.5 * jax.random.normal(ks[13], (nf, FOX_HEADS), f32)
    fox_w_out = jax.random.normal(ks[14], (nf, FOX_WIDTH, D_MODEL), f32) * FOX_WIDTH ** -0.5
    return {"x": x, "norm_g": norm_g, "final_g": final_g,
            "lru_w_in": lru_w_in, "lru_conv_w": lru_conv_w, "lru_conv_b": lru_conv_b,
            "lru_wa": lru_wa, "lru_ba": lru_ba, "lru_wx": lru_wx, "lru_bx": lru_bx,
            "lru_a_param": lru_a_param, "lru_w_out": lru_w_out,
            "fox_w_in": fox_w_in, "fox_b_f": fox_b_f, "fox_w_out": fox_w_out}

def first_block(x, norm_g, final_g, lru_w_in, lru_conv_w, lru_conv_b, lru_wa, lru_ba,
              lru_wx, lru_bx, lru_a_param, lru_w_out, fox_w_in, fox_b_f, fox_w_out):
    for i in range(DEPTH):
        h = rms_norm(x, norm_g[i])
        j = i // N_MIXERS
        if i % N_MIXERS == 0:
            x = x + lru_mixer(h, lru_w_in[j], lru_conv_w[j], lru_conv_b[j], lru_wa[j], lru_ba[j],
                              lru_wx[j], lru_bx[j], lru_a_param[j], lru_w_out[j])
        else:
            x = x + fox_mixer(h, fox_w_in[j], fox_b_f[j], fox_w_out[j])
    return rms_norm(x, final_g)


D_CONV = D_MODEL
CONV_WIDTH_2 = 3
RET_HEADS = 4
RET_QK_DIM = 128
RET_V_DIM = 256
RET_QK = RET_HEADS * RET_QK_DIM
RET_V = RET_HEADS * RET_V_DIM
CHUNK = 128
ROPE_BASE = 10000.0
D_FF = 4 * D_MODEL
MAX_START = 1024

IN_SIZES = (D_CONV, D_CONV, D_CONV, RET_QK, RET_QK, RET_V, RET_V, D_MODEL, D_MODEL)
D_IN = 3 * D_CONV + 2 * RET_QK + 2 * RET_V + 2 * D_MODEL


def rmsnorm(x, g):
    xf = x.astype(jnp.float32)
    xf = xf * lax.rsqrt(jnp.mean(xf * xf, axis=-1, keepdims=True) + EPS)
    return (xf * g.astype(jnp.float32)).astype(x.dtype)

def rotary(t, positions):
    half = t.shape[-1] // 2
    inv_freq = ROPE_BASE ** (-jnp.arange(half, dtype=jnp.float32) / half)
    ang = positions.astype(jnp.float32)[..., None] * inv_freq
    cos = jnp.cos(ang)[:, :, None, :].astype(t.dtype)
    sin = jnp.sin(ang)[:, :, None, :].astype(t.dtype)
    t1, t2 = t[..., :half], t[..., half:]
    return jnp.concatenate([t1 * cos - t2 * sin, t1 * sin + t2 * cos], axis=-1)

def short_conv_mixer(b, c, u, conv_w, w_out):
    z = c * u
    z = lax.conv_general_dilated(
        z, conv_w[:, None, :].astype(z.dtype), window_strides=(1,),
        padding=[(CONV_WIDTH_2 - 1, 0)], dimension_numbers=("NWC", "WIO", "NWC"),
        feature_group_count=D_CONV)
    return (b * z) @ w_out

def retention_core(q, k, v, positions):
    bsz, seq = q.shape[0], q.shape[1]
    n_chunks = seq // CHUNK
    q = rotary(q, positions) * (RET_QK_DIM ** -0.5)
    k = rotary(k, positions)

    def to_chunks(t):
        return t.astype(jnp.float32).reshape(bsz, n_chunks, CHUNK, RET_HEADS, t.shape[-1]).swapaxes(0, 1)

    qc, kc, vc = to_chunks(q), to_chunks(k), to_chunks(v)
    log_gamma = jnp.log1p(-jnp.exp2(-5.0 - jnp.arange(RET_HEADS, dtype=jnp.float32)))
    pos = jnp.arange(CHUNK, dtype=jnp.float32)
    rel = pos[:, None] - pos[None, :]
    decay_intra = jnp.where(rel >= 0, jnp.exp(log_gamma[:, None, None] * jnp.maximum(rel, 0.0)), 0.0)
    decay_q = jnp.exp((pos[:, None] + 1.0) * log_gamma)
    decay_k = jnp.exp((CHUNK - 1.0 - pos[:, None]) * log_gamma)
    decay_chunk = jnp.exp(CHUNK * log_gamma)

    scores = jnp.einsum("nbqhd,nbkhd->nbhqk", qc, kc) * decay_intra
    o_intra = jnp.einsum("nbhqk,nbkhv->nbqhv", scores, vc)

    def step(state, inp):
        q_i, k_i, v_i = inp
        o_inter = jnp.einsum("bqhd,bhdv->bqhv", q_i, state) * decay_q[None, :, :, None]
        state = state * decay_chunk[None, :, None, None] + jnp.einsum("bkhd,kh,bkhv->bhdv", k_i, decay_k, v_i)
        return state, o_inter

    state0 = jnp.zeros((bsz, RET_HEADS, RET_QK_DIM, RET_V_DIM), jnp.float32)
    _, o_inter = lax.scan(step, state0, (qc, kc, vc))
    return (o_intra + o_inter).swapaxes(0, 1).reshape(bsz, seq, RET_HEADS, RET_V_DIM)

def retention_mixer(q, k, v, g, positions, ret_norm, w_out):
    bsz, seq = q.shape[0], q.shape[1]
    o = retention_core(q.reshape(bsz, seq, RET_HEADS, RET_QK_DIM),
                       k.reshape(bsz, seq, RET_HEADS, RET_QK_DIM),
                       v.reshape(bsz, seq, RET_HEADS, RET_V_DIM), positions)
    mu = jnp.mean(o, axis=-1, keepdims=True)
    var = jnp.mean(jnp.square(o - mu), axis=-1, keepdims=True)
    o = ((o - mu) * lax.rsqrt(var + EPS)).reshape(bsz, seq, RET_V) * ret_norm.astype(jnp.float32)
    o = o.astype(g.dtype)
    return (jax.nn.silu(g) * o) @ w_out

def hybrid_layer(x, positions, norm_mix, w_in, conv_w, w_conv_out, ret_norm, w_ret_out, w_o,
                 norm_mlp, w_up, w_down):
    h = rmsnorm(x, norm_mix)
    proj = h @ w_in
    split_points = np.cumsum(IN_SIZES)[:-1].tolist()
    cb, cc, cu, q, k, v, g, ga, gb = jnp.split(proj, split_points, axis=-1)
    y_conv = short_conv_mixer(cb, cc, cu, conv_w, w_conv_out)
    y_ret = retention_mixer(q, k, v, g, positions, ret_norm, w_ret_out)
    merged = jax.nn.sigmoid(ga) * y_conv + jax.nn.sigmoid(gb) * y_ret
    x = x + merged @ w_o
    h2 = rmsnorm(x, norm_mlp)
    return x + jnp.square(jax.nn.relu(h2 @ w_up)) @ w_down

def second_inputs(seed: int = 0) -> dict:
    key = jax.random.key(seed)
    ks = jax.random.split(key, 14)
    f32 = jnp.float32

    def dense(k, fan_in, fan_out):
        return jax.random.normal(k, (DEPTH, fan_in, fan_out), f32) * (fan_in ** -0.5)

    def gain(k, shape):
        return 1.0 + 0.02 * jax.random.normal(k, shape, f32)

    x = jax.random.normal(ks[0], (BATCH, SEQ, D_MODEL), f32)
    start = jax.random.randint(ks[1], (BATCH, 1), 0, MAX_START, dtype=jnp.int32)
    positions = (start + jnp.arange(SEQ, dtype=jnp.int32)[None, :]).astype(jnp.int32)
    return {
        "x": x,
        "positions": positions,
        "norm_mix": gain(ks[2], (DEPTH, D_MODEL)),
        "w_in": dense(ks[3], D_MODEL, D_IN),
        "conv_w": jax.random.normal(ks[4], (DEPTH, CONV_WIDTH_2, D_CONV), f32) * (CONV_WIDTH_2 ** -0.5),
        "w_conv_out": dense(ks[5], D_CONV, D_MODEL),
        "ret_norm": gain(ks[6], (DEPTH, RET_V)),
        "w_ret_out": dense(ks[7], RET_V, D_MODEL),
        "w_o": dense(ks[8], D_MODEL, D_MODEL),
        "norm_mlp": gain(ks[9], (DEPTH, D_MODEL)),
        "w_up": dense(ks[10], D_MODEL, D_FF),
        "w_down": dense(ks[11], D_FF, D_MODEL),
        "norm_final": gain(ks[12], (D_MODEL,)),
    }

def second_block(x, positions, norm_mix, w_in, conv_w, w_conv_out, ret_norm, w_ret_out, w_o,
              norm_mlp, w_up, w_down, norm_final):
    for i in range(DEPTH):
        x = hybrid_layer(x, positions, norm_mix[i], w_in[i], conv_w[i], w_conv_out[i], ret_norm[i],
                         w_ret_out[i], w_o[i], norm_mlp[i], w_up[i], w_down[i])
    return rmsnorm(x, norm_final)


def setup_inputs(seed=0):
    out = dict(first_inputs(seed))
    for name, value in second_inputs(seed + 1).items():
        if name != "x":
            out[name + "_2"] = value
    return out


def reference(
    x, norm_g, final_g, lru_w_in, lru_conv_w, lru_conv_b, lru_wa, lru_ba, lru_wx, lru_bx,
    lru_a_param, lru_w_out, fox_w_in, fox_b_f, fox_w_out, positions_2, norm_mix_2, w_in_2,
    conv_w_2, w_conv_out_2, ret_norm_2, w_ret_out_2, w_o_2, norm_mlp_2, w_up_2, w_down_2,
    norm_final_2,
):
    x = first_block(
        x, norm_g, final_g, lru_w_in, lru_conv_w, lru_conv_b, lru_wa, lru_ba, lru_wx, lru_bx,
        lru_a_param, lru_w_out, fox_w_in, fox_b_f, fox_w_out,
    )
    return second_block(
        x, positions_2, norm_mix_2, w_in_2, conv_w_2, w_conv_out_2, ret_norm_2, w_ret_out_2,
        w_o_2, norm_mlp_2, w_up_2, w_down_2, norm_final_2,
    )


_drawn_inputs = setup_inputs


def setup_inputs(seed=0):
    import zlib

    import numpy as np

    out = dict(_drawn_inputs(seed))
    spreads = {}
    factors = {'lru_ba': 8.0,
     'lru_bx': 8.0,
     'ret_norm_2': 7.135,
     'norm_final_2': 8.05,
     'norm_mlp_2': 3.457}
    for name, (base, spread) in spreads.items():
        noise = np.random.default_rng([zlib.crc32(name.encode()), seed]).standard_normal(out[name].shape)
        drawn = base * np.exp(spread * noise) if base else spread * noise
        out[name] = __import__('jax').numpy.asarray(drawn.astype(out[name].dtype))
    for name, factor in factors.items():
        out[name] = (out[name] * factor).astype(out[name].dtype)
    return out
```

```python
import math
from contextlib import ExitStack

import numpy as np

import concourse.bass as bass
from concourse import mybir
from concourse.alu_op_type import AluOpType as ALU

F32 = mybir.dt.float32
F32R = mybir.dt.float32r
BF16 = mybir.dt.bfloat16
I32 = mybir.dt.int32
ACT = mybir.ActivationFunctionType
AX_X = mybir.AxisListType.X

P = 128
SEQ = 512
D = 1024
DT = D // P
TT = SEQ // P
EPS = 1e-6
LRU_W = 1536
LT = LRU_W // P
LRU_C = 8.0
CONV1 = 4
HEADS = 16
HD = 64
CONV2 = 3
RH = 4
RQK = 128
RV = 256
D_FF = 4096
LAYERS = 2
ROPE_BASE = 10000.0
CB, CC, CU, CQ, CK, CV, CG, CGA, CGB = (int(v) for v in np.cumsum(
    [0, D, D, D, RH * RQK, RH * RQK, RH * RV, RH * RV, D]))

KT = 2
CW = KT * 512
RING = 4
AHEAD = 3
GROUP = DT // KT
TRI = SEQ * (TT + 1) // 2

V_NG = 0
V_FG = V_NG + 2 * DT
V_CW = V_FG + DT
V_CBIAS = V_CW + CONV1 * LT
V_BA = V_CBIAS + LT
V_BX = V_BA + LT
V_AP = V_BX + LT
V_BF = V_AP + LT
V_NF = V_BF + 1
V_LAYER = V_NF + DT
L_MIX, L_MLP, L_CW, L_RN = 0, DT, 2 * DT, 2 * DT + CONV2 * DT
L_COLS = L_RN + DT
V_COLS = V_LAYER + LAYERS * L_COLS
K_INVF, K_SIGN, K_IDENT, K_ONES, K_MASK, K_DECAY = 0, 1, 2, 2 + P, 2 + 2 * P, 2 + 3 * P
K_COLS = K_DECAY + RH * SEQ

A_TAIL = 11272
A_WORDS = A_TAIL + RH * SEQ + 2 * SEQ

PREP_V = 22
MAGIC = float(1.5 * 2 ** 23)
ATANH = [1 / 13, 1 / 11, 1 / 9, 1 / 7, 1 / 5, 1 / 3]


def two_pi_parts():
    parts, rest = [], 2 * math.pi
    for _ in range(3):
        unit = 2.0 ** (math.floor(math.log2(rest)) - 7)
        parts.append(math.floor(rest / unit) * unit)
        rest -= parts[-1]
    return parts + [float(np.float32(rest))]



class Step:
    def __init__(self, kind, chunks=0, turns=0, incs=None, **args):
        self.kind, self.chunks, self.turns, self.args = kind, chunks, turns, args
        self.incs = incs or {}


class Loop:
    def __init__(self, name, count, body):
        self.name, self.count, self.body = name, count, body


SPLIT = {"a_hi": 4, "a_lo": 4}
INCS = {
    "prep": {},
    "norm": {"a_hi": DT, "a_lo": DT, "act_out": DT, "vec": DT},
    "x": {"act_out": 4, "vec": 12, **SPLIT},
    "gates": {"act_out": 18, "vec": 12},
    "lru_gate": {"act_out": 4, "vec": 4, **SPLIT},
    "residual": {},
    "forget": {"act_out": 1, "vec": 22},
    "fq": {}, "fk": {}, "v": {},
    "attention": {},
    "fox_gate": {"act_out": 4, "vec": 4, **SPLIT},
    "midnorm": {"act_out": DT + 1, "vec": 2 * DT + 1},
    "trig": {"act_out": 2, "vec": 19},
    "qk": {"act_out": 8, "vec": 10},
    "ret_scores": {},
    "ret_out": {"act_out": 1, "vec": TT + 7},
    "ret_turn": SPLIT,
    "g": {"act_out": 4},
    "gb": {"act_out": 4},
    "ret_proj": {},
    "cc": {"vec": 1},
    "cu": {"vec": 4},
    "cb": {"vec": 16, **SPLIT},
    "ga": {"act_out": 4},
    "merge": {"vec": 4, **SPLIT},
    "up": {"vec": 4, **SPLIT},
    "final": {"act_out": DT + 1, "vec": DT + 1},
}
STATS = {"stats": 1, "sumsq_read": 1, "vec": 1 + TT}


def schedule():
    def s(kind, chunks=0, turns=0, stats=False, **args):
        incs = dict(INCS[kind])
        if stats:
            for k, v in STATS.items():
                incs[k] = incs.get(k, 0) + v
        return Step(kind, chunks, turns, incs, stats=stats, **args)

    lru = [s("prep"), s("norm", gain=V_NG),
           s("x", 4, 1, True, b=0), s("x", 4, 1, b=1), s("gates", 1, 2, b=0),
           s("x", 4, 1, b=2), s("gates", 1, 2, b=1), s("lru_gate", 4, 1, b=0),
           s("gates", 1, 2, b=2), s("lru_gate", 4, 1, b=1), s("lru_gate", 4, 1, b=2),
           s("residual", LT // KT, 1, k="lru", j=0), s("residual", LT // KT, 1, k="lru", j=1)]
    fox = [s("norm", gain=V_NG + DT), s("forget", 1, 1, True),
           Loop("half", 2, [s("fq", 4, 1), s("fk", 4, 1), s("v", 4, 1, to="fox"), s("attention"),
                            s("fox_gate", 4, 1)]),
           s("residual", 4, 1, k="y", j=0), s("residual", 4, 1, k="y", j=1),
           s("midnorm"), s("trig")]
    layer = [s("norm", gain="mix"),
             Loop("half", 2, [s("qk", 4, 1, True), s("v", 4, 1, to="ret"),
                              s("ret_scores", 0, 1, hh=0), s("ret_scores", 0, 1, hh=1),
                              s("ret_out", 0, 1, hh=0), s("ret_out", 0, 1, hh=1),
                              s("g", 4, 1), s("ret_turn", 0, 1)]),
             Loop("half", 2, [s("gb", 4, 1), s("ret_proj", 4, 1)]),
             Loop("half", 2, [s("cc", 4, 1), s("cu", 4, 1), s("cb", 4, 1), s("ga", 4, 1)]),
             s("merge", 4, 1, j=0), s("merge", 4, 1, j=1),
             s("residual", 4, 1, k="m", j=0), s("residual", 4, 1, k="m", j=1),
             s("norm", gain="mlp"),
             Loop("quarter", 4, [s("up", 4, 1, True, j=0), s("up", 4, 1, j=1),
                                 s("residual", 4, 1, k="y", j=0), s("residual", 4, 1, k="y", j=1)])]
    return lru + fox + [Loop("layer", LAYERS, layer), s("final")]


COUNTED = ("turn", "chunk", "used", "a_hi", "a_lo", "act_out", "vec", "stats", "sumsq_read", "halves")


def step_delta(step):
    out = {k: step.incs.get(k, 0) for k in COUNTED}
    out["turn"], out["chunk"] = step.turns, step.chunks
    out["used"] = max(step.chunks - 1, 0)
    out["halves"] = step.kind == "attention"
    return out


def delta(item):
    if isinstance(item, Step):
        return step_delta(item)
    total = {k: 0 for k in COUNTED}
    for x in item.body:
        for k, v in delta(x).items():
            total[k] += v
    return {k: v * item.count for k, v in total.items()}


class Tally:

    def __init__(self):
        self.fixed = {k: 0 for k in COUNTED}
        self.loops = []
        self.mark = {}
        self.fresh_stats = False

    def value(self, name, plus=0, times=1):
        out = times * self.fixed[name] + plus
        for _, var, per in self.loops:
            if per[name]:
                out = var * (times * per[name]) + out
        return out

    def var(self, name):
        return next(v for n, v, _ in reversed(self.loops) if n == name)

    def walk(self, eng, items, emit):
        for item in items:
            if isinstance(item, Step):
                before = dict(self.fixed)
                emit(item)
                assert self.fixed == before
                for k, v in step_delta(item).items():
                    self.fixed[k] += v
                continue
            per = delta(Loop("", 1, item.body))
            assert per["chunk"] % RING == 0 and per["turn"] % 2 == 0
            before = dict(self.fixed)
            with eng.Fori(0, item.count) as i:
                self.loops.append((item.name, i, per))
                self.walk(eng, item.body, emit)
                self.loops.pop()
            self.fixed = {k: before[k] + item.count * per[k] for k in COUNTED}


def build(nc, stream, xT, vecs, consts, positions, outT, cum_dram):
    steps = schedule()
    n_chunks = sum(delta(x)["chunk"] for x in steps)
    assert stream.shape[0] == n_chunks + AHEAD
    ctx = ExitStack()
    with ctx:
        def sb(name, shape, dt):
            return ctx.enter_context(nc.sbuf_tensor(name, shape, dt))

        def sem(name):
            return ctx.enter_context(nc.semaphore(name))

        x = sb("x", [P, DT, SEQ], F32)
        h_hi = sb("h_hi", [P, DT, SEQ], F32R)
        h_lo = sb("h_lo", [P, DT, SEQ], F32R)
        y_hi = sb("y_hi", [P, LT, SEQ], F32R)
        y_lo = sb("y_lo", [P, LT, SEQ], F32R)
        w_raw = sb("w_raw", [P, RING, CW], F32)
        w_hi = sb("w_hi", [P, RING, CW], F32R)
        w_lo = sb("w_lo", [P, RING, CW], F32R)
        arena = sb("arena", [P, A_WORDS], F32)
        rms = sb("rms", [P, SEQ], F32)
        rms_col = sb("rms_col", [P, TT], F32)
        sumsq = sb("sumsq", [P, SEQ], F32)
        vec_t = sb("vec_t", [P, V_COLS], F32)
        ident = sb("ident", [P, P], F32)
        ones = sb("ones", [P, P], F32)
        ident_b = sb("ident_b", [P, P], BF16)
        mask_b = sb("mask_b", [P, P], BF16)
        ones_b = sb("ones_b", [P, P], BF16)
        pcol = sb("pcol", [P, 2], F32)
        eps_t = sb("eps_t", [P, 1], F32)
        rate = sb("rate", [P, LT], F32)
        rate_m2 = sb("rate_m2", [P, LT], F32)
        small = sb("small", [P, 80], F32)
        junk = sb("junk", [P, P], F32)
        bank = [ctx.enter_context(nc.psum_tensor(f"bank{i}", [P, SEQ], F32)) for i in range(8)]

        def area(at, *shape):
            n = int(np.prod(shape))
            assert at + n <= A_WORDS
            v = arena[:, at:at + n]
            if len(shape) == 2:
                v = v.rearrange("p (a b) -> p a b", a=shape[0])
            return v

        xc = area(0, LT, SEQ)
        u_pad = area(LT * SEQ, 4, SEQ + CONV1 - 1)
        at = LT * SEQ + 4 * (SEQ + CONV1 - 1)
        g_r, g_i, g_t, g_d = (area(at + 1024 * n, 2, SEQ) for n in range(4))
        gate_t = u_pad
        fq, fk = area(0, 4, SEQ), area(4 * SEQ, 4, SEQ)
        v_tok = area(8 * SEQ, TT, SEQ)
        probs = area(6144, 2, TRI)
        probs_t = area(6144 + 2 * TRI, TRI)
        AUG = 6144 + 3 * TRI
        cum_rows = arena[0:3, AUG:AUG + HEADS * SEQ // 2].bitcast(BF16).rearrange("p (h t) -> p h t", h=HEADS)
        qk = area(0, 4, SEQ)
        rv = area(2048, TT, SEQ)
        sg = area(4096, 4, SEQ)
        st = area(6144, 2, TRI)
        cos_r, sin_r = area(6144 + 2 * TRI, SEQ), area(6144 + 2 * TRI + SEQ, SEQ)
        swap = area(6144 + 2 * TRI + 2 * SEQ, 2, SEQ)
        m_t = area(0, DT, SEQ)
        ga_t = area(4096, DT, SEQ)
        z_pad = area(8192, 4, SEQ + CONV2 - 1)
        tmp2 = area(8192 + 4 * (SEQ + CONV2 - 1), 2, SEQ)
        decay = area(A_TAIL, RH, SEQ)
        cos_t, sin_t = area(A_TAIL + RH * SEQ, SEQ), area(A_TAIL + RH * SEQ + SEQ, SEQ)
        up_t = area(0, 4, SEQ)
        xsq = area(0, 2, SEQ)

        fox_t = area(6144, 4, SEQ)

        def ft(n):
            return area(6144 + SEQ * n, SEQ)[0:HEADS, :]

        def cum_part(r):
            return area(6144 + SEQ * (4 + r), SEQ // 2)[0:HEADS, :].bitcast(BF16)

        def turned_bank(j):
            return bank[4 + j] if j < 3 else bank[6][:, 2 * P:3 * P]

        def xc_slot(b, n):
            return (4 if b == 1 else 8) + n

        def tri(j):
            start = sum(SEQ - P * i for i in range(j))
            return start, SEQ - P * j

        inputs_in = sem("inputs_in")
        x_in = sem("x_in")
        decay_in = sem("decay_in")
        raw_loaded = [sem(f"raw_loaded{i}") for i in range(RING)]
        hi_ready = sem("hi_ready")
        lo_ready = sem("lo_ready")
        chunk_used = sem("chunk_used")
        bank_ready = sem("bank_ready")
        evacuated = sem("evacuated")
        a_hi = sem("a_hi")
        a_lo = sem("a_lo")
        act_out = sem("act_out")
        vec = sem("vec")
        stats_ready = sem("stats_ready")
        sumsq_read = sem("sumsq_read")
        prep_v = sem("prep_v")
        prep_a = sem("prep_a")
        norm_ready = sem("norm_ready")
        cum_out = sem("cum_out")
        cum_in = sem("cum_in")
        scores_ready = sem("scores_ready")
        max_ready = sem("max_ready")
        exp_ready = sem("exp_ready")
        probs_ready = sem("probs_ready")
        turned = sem("turned")
        turned_act = sem("turned_act")
        turned_vec = sem("turned_vec")
        o_ready = sem("o_ready")
        o_copied = sem("o_copied")
        out_ready = sem("out_ready")
        stored = sem("stored")

        block = ctx.enter_context(nc.Block())

        def wait(eng, s, value):
            if not isinstance(value, int) or value > 0:
                eng.wait_ge(s, value)

        @block.sync
        def _(sp):
            sp.dma_start(vec_t[:, :], vecs).then_inc(inputs_in, 16)
            sp.dma_start(pcol[:, :], consts[:, K_INVF:K_INVF + 2]).then_inc(inputs_in, 16)
            sp.dma_start(ident[:, :], consts[:, K_IDENT:K_IDENT + P]).then_inc(inputs_in, 16)
            sp.dma_start(junk[:, :], consts[:, K_MASK:K_MASK + P]).then_inc(inputs_in, 16)
            sp.dma_start(x[:, :, :], xT.rearrange("(k p) t -> p k t", p=P)).then_inc(x_in, 16)
            for c in range(RING):
                sp.dma_start(w_raw[:, c, :], stream[c, :, :]).then_inc(raw_loaded[c], 16)
            rounds = (n_chunks + AHEAD) // RING
            with sp.Fori(1, rounds) as r:
                for slot in range(RING):
                    sp.wait_ge(lo_ready, r * RING + (slot - RING + 1))
                    sp.dma_start(w_raw[:, slot, :], stream[r * RING + slot, :, :])\
                        .then_inc(raw_loaded[slot], 16)
            for c in range(rounds * RING, n_chunks + AHEAD):
                sp.wait_ge(lo_ready, c - RING + 1)
                sp.dma_start(w_raw[:, c % RING, :], stream[c, :, :]).then_inc(raw_loaded[c % RING], 16)
            for k in range(DT):
                sp.wait_ge(out_ready, k + 1)
                sp.dma_start(outT[k * P:(k + 1) * P, :], x[:, k, :]).then_inc(stored, 16)
            sp.wait_ge(stored, 16 * DT)

        @block.gpsimd
        def _(pool):
            T = Tally()
            for item in steps:
                if isinstance(item, Step) and item.kind == "forget":
                    pool.wait_ge(vec, T.value("vec", item.incs["vec"]))
                    for r in range(3):
                        pool.dma_start(cum_dram[r, :, :], cum_part(r)).then_inc(cum_out, 16)
                    pool.wait_ge(cum_out, 48)
                    pool.dma_start(cum_rows, cum_dram).then_inc(cum_in, 16)
                if isinstance(item, Step) and item.kind == "trig":
                    pool.wait_ge(vec, T.value("vec"))
                    pool.dma_start(decay, consts[:, K_DECAY:K_DECAY + RH * SEQ]
                                   .rearrange("p (a b) -> p a b", a=RH)).then_inc(decay_in, 16)
                    pool.dma_start(sin_t.bitcast(I32), positions.partition_broadcast(P)).then_inc(decay_in, 16)
                for k, v in delta(item).items():
                    T.fixed[k] += v

        @block.tensor
        def _(pe):
            T = Tally()

            def begin_turn(plus=0):
                wait(pe, evacuated, T.value("turn", 4 * (plus - 1), 4))
                if T.fresh_stats:
                    pe.wait_ge(sumsq_read, T.value("stats"))
                    T.fresh_stats = False
                return 4 * ((T.fixed["turn"] + plus) % 2)

            def product(step, tile, ready=None, tokens_out=False):
                set_ = begin_turn()
                for c in range(step.chunks):
                    slot = (T.fixed["chunk"] + c) % RING
                    if step.args["stats"] and c == step.chunks - 1:
                        statistics(4 - set_)
                    pe.wait_ge(lo_ready, T.value("chunk", c + 1))
                    for kt in range(KT):
                        k = KT * c + kt
                        if ready:
                            ready(k)
                        a_h, a_l = tile(k)
                        first, last = k == 0, k == KT * step.chunks - 1
                        for n in range(4):
                            out = bank[set_ + n][:, :]
                            if tokens_out:
                                w = slice(kt * 512, kt * 512 + 512)
                                t = slice(n * P, n * P + P)
                                pe.matmul(out, a_h[:, t], w_hi[:, slot, w], start=first, stop=False)
                                pe.matmul(out, a_h[:, t], w_lo[:, slot, w], start=False, stop=False)
                                mm = pe.matmul(out, a_l[:, t], w_hi[:, slot, w], start=False, stop=last)
                            else:
                                w = slice(kt * 512 + n * P, kt * 512 + n * P + P)
                                pe.matmul(out, w_hi[:, slot, w], a_h, start=first, stop=False)
                                pe.matmul(out, w_hi[:, slot, w], a_l, start=False, stop=False)
                                mm = pe.matmul(out, w_lo[:, slot, w], a_h, start=False, stop=last)
                            if last:
                                mm.then_inc(bank_ready, 1)
                    if c < step.chunks - 1:
                        mm.then_inc(chunk_used, 1)

            def statistics(set_):
                pe.wait_ge(vec, T.mark["sumsq"])
                wait(pe, evacuated, T.value("turn", 0, 4))
                pe.matmul(bank[set_ + 3][:, :], ones[:, :], sumsq[:, :], start=True, stop=True)\
                    .then_inc(stats_ready, 1)
                T.fresh_stats = True

            def h_tile(k):
                return h_hi[:, k, :], h_lo[:, k, :]

            def h_ready(k):
                pe.wait_ge(a_lo, T.mark["h"] + (k + 1))

            def norm(step):
                T.mark["h"] = T.value("a_lo")
                T.mark["sumsq"] = T.value("vec", DT)

            def of_h(step):
                product(step, h_tile, h_ready, tokens_out=step.kind == "v")
                if step.kind == "x":
                    T.mark["xc", step.args["b"]] = T.value("a_lo", 4)

            def gates(step):
                b = step.args["b"]
                slot = T.fixed["chunk"] % RING
                pe.wait_ge(a_lo, T.mark["xc", b])
                pe.wait_ge(lo_ready, T.value("chunk", 1))
                for half in range(2):
                    set_ = begin_turn(half)
                    for n in range(4):
                        blk, which = 2 * half + n // 2, n % 2
                        w = slice(which * 512 + blk * P, which * 512 + blk * P + P)
                        y = xc_slot(b, blk)
                        pe.matmul(bank[set_ + n][:, :], w_hi[:, slot, w], y_hi[:, y, :], start=True, stop=False)
                        pe.matmul(bank[set_ + n][:, :], w_hi[:, slot, w], y_lo[:, y, :], start=False, stop=False)
                        pe.matmul(bank[set_ + n][:, :], w_lo[:, slot, w], y_hi[:, y, :], start=False, stop=True)\
                            .then_inc(bank_ready, 1)

            def of_y(step):
                first = step.args.get("j", 0) == 0
                n_k = KT * step.chunks

                def slot(k):
                    return (8 + k if k < 4 else k - 4) if step.args.get("k") == "m" else k

                def ready(k):
                    if first:
                        pe.wait_ge(a_lo, T.value("a_lo", k + 1 - n_k))

                def all_ready(k):
                    if first and k == 0:
                        pe.wait_ge(a_lo, T.value("a_lo"))

                product(step, lambda k: (y_hi[:, slot(k), :], y_lo[:, slot(k), :]),
                        ready if step.kind == "residual" else all_ready)

            def forget(step):
                set_ = begin_turn()
                slot = T.fixed["chunk"] % RING
                pe.wait_ge(lo_ready, T.value("chunk", 1))
                for k in range(DT):
                    h_ready(k)
                    w = slice(k * P, k * P + P)
                    out = bank[set_][:, :]
                    pe.matmul(out, w_hi[:, slot, w], h_hi[:, k, :], start=k == 0, stop=False)
                    pe.matmul(out, w_hi[:, slot, w], h_lo[:, k, :], start=False, stop=False)
                    mm = pe.matmul(out, w_lo[:, slot, w], h_hi[:, k, :], start=False, stop=k == DT - 1)
                mm.then_inc(bank_ready, 4)
                statistics(4 - set_)

            def attention(step):
                pe.wait_ge(evacuated, T.value("turn", 0, 4))
                pe.wait_ge(cum_in, 16)
                half = T.var("half")

                def heads(count, plus=0):
                    return T.value("halves", plus, count * HEADS // 2)

                def scores(hh):
                    rows = slice(HD * (hh % 2), HD * (hh % 2) + HD)
                    for t in range(TT):
                        if hh:
                            pe.wait_ge(exp_ready, heads(4, 4 * (hh - 1) + t + 1))
                        n = P * (t + 1)
                        out = bank[t][:, 0:n]
                        pe.matmul(out, fq[rows, hh // 2, t * P:n], fk[rows, hh // 2, 0:n], start=True, stop=False)
                        pe.matmul(out, ones_b[0:3, :], cum_rows[0:3, half * (HEADS // 2) + hh, 0:n],
                                  start=False, stop=False)
                        pe.matmul(bank[t][:, t * P:n], ident_b[:, :], mask_b[:, :], start=False, stop=True)\
                            .then_inc(scores_ready, 1)

                def turn(hh):
                    pe.wait_ge(probs_ready, heads(5, 5 * hh + 5))
                    if hh:
                        pe.wait_ge(turned_act, heads(2, 2 * hh))
                        pe.wait_ge(turned_vec, heads(1, hh))
                    for j in range(TT):
                        for t in range(j, TT):
                            at = P * t * (t + 1) // 2 + P * j
                            mm = pe.transpose(turned_bank(j)[:, (t - j) * P:(t - j) * P + P],
                                              probs[:, hh % 2, at:at + P], ident[:, :])
                        if j != 2:
                            mm.then_inc(turned, 1)

                def values(hh):
                    rows = slice(HD * (hh % 2), HD * (hh % 2) + HD)
                    pe.wait_ge(turned_act, heads(2, 2 * hh + 2))
                    pe.wait_ge(turned_vec, heads(1, hh + 1))
                    if hh:
                        pe.wait_ge(o_copied, heads(1, hh))
                    for j in range(TT):
                        at, n = tri(j)
                        mm = pe.matmul(bank[7][rows, P * j:SEQ], v_tok[:, j, hh * HD:hh * HD + HD],
                                       probs_t[:, at:at + n], start=j == 0, stop=j == TT - 1)
                    mm.then_inc(o_ready, 1)

                scores(0)
                for hh in range(HEADS // 2):
                    if hh + 1 < HEADS // 2:
                        scores(hh + 1)
                    if hh:
                        values(hh - 1)
                    turn(hh)
                values(HEADS // 2 - 1)
                pe.wait_ge(o_copied, heads(1, HEADS // 2))

            def ret_scores(step):
                hh = step.args["hh"]
                set_ = begin_turn()
                if hh == 0:
                    pe.wait_ge(vec, T.value("vec"))
                for j in range(TT):
                    n = SEQ - P * j
                    pe.matmul(bank[set_ + j][:, 0:n], qk[:, 2 + hh, P * j:P * j + P], qk[:, hh, P * j:SEQ],
                              start=True, stop=True).then_inc(bank_ready, 1)

            def ret_out(step):
                hh = step.args["hh"]
                set_ = begin_turn()
                pe.wait_ge(evacuated, T.value("turn", -4, 4))
                for t in range(TT):
                    for j in range(t + 1):
                        at = tri(j)[0] + (t - j) * P
                        mm = pe.matmul(bank[set_ + t][:, 0:RV], st[:, hh, at:at + P],
                                       rv[:, j, hh * RV:hh * RV + RV], start=j == 0, stop=j == t)
                    mm.then_inc(bank_ready, 1)

            def ret_turn(step):
                set_ = begin_turn()
                pe.wait_ge(evacuated, T.value("turn", -4, 4))
                for n in range(4):
                    hh, f = n // 2, n % 2
                    for t in range(TT):
                        mm = pe.transpose(bank[set_ + n][:, t * P:t * P + P],
                                          st[:, hh, t * RV + f * P:t * RV + f * P + P], ident[:, :])
                    mm.then_inc(bank_ready, 1)

            def whole_norm(step):
                pe.wait_ge(vec, T.value("vec", DT))
                pe.wait_ge(evacuated, T.value("turn", 0, 4))
                pe.matmul(bank[4 * (T.fixed["turn"] % 2)][:, :], ones[:, :], sumsq[:, :], start=True, stop=True)\
                    .then_inc(norm_ready, 1)

            def nothing(step):
                pass

            def prep(step):
                pe.wait_ge(inputs_in, 64)
                pe.wait_ge(prep_v, PREP_V)

            kinds = {"prep": prep, "norm": norm, "x": of_h, "gates": gates, "lru_gate": of_h,
                     "residual": of_y, "forget": forget, "fq": of_h, "fk": of_h, "v": of_h,
                     "attention": attention, "fox_gate": of_h, "midnorm": whole_norm, "trig": nothing,
                     "qk": of_h, "ret_scores": ret_scores, "ret_out": ret_out, "ret_turn": ret_turn,
                     "g": of_h, "gb": of_h, "ret_proj": of_y, "cc": of_h, "cu": of_h, "cb": of_h,
                     "ga": of_h, "merge": of_y, "up": of_h, "final": whole_norm}
            T.walk(pe, steps, lambda step: kinds[step.kind](step))

        def split_slots(T, step):
            for n in range(AHEAD, AHEAD + step.chunks):
                yield n, (T.fixed["chunk"] + n) % RING

        @block.scalar
        def _(act):
            T = Tally()
            A = nc.scalar

            def split_ahead(step):
                for n, slot in split_slots(T, step):
                    if n == RING - 1:
                        wait(act, bank_ready, T.value("turn", 0, 4))
                    else:
                        act.wait_ge(chunk_used, T.value("used", n - RING + 1))
                    loaded = 16 * ((T.fixed["chunk"] + n) // RING + 1)
                    for _, var, per in T.loops:
                        loaded = var * (16 * per["chunk"] // RING) + loaded
                    act.wait_ge(raw_loaded[slot], loaded)
                    A.activation(w_hi[:, slot, :], w_raw[:, slot, :], ACT.Copy).then_inc(hi_ready, 1)

            def join():
                wait(act, evacuated, T.value("turn", 0, 4))
                for s, name in ((vec, "vec"), (a_lo, "a_lo"), (act_out, "act_out"), (a_hi, "a_hi")):
                    wait(act, s, T.value(name))

            def banks(n, plus=0):
                act.wait_ge(bank_ready, T.value("turn", 4 * plus + n + 1, 4))

            def statistics(step):
                act.wait_ge(stats_ready, T.value("stats", 1))
                set_ = 4 - 4 * (T.fixed["turn"] % 2)
                A.activation(rms[:, :], bank[set_ + 3][:, :], ACT.Sqrt, scale=1.0 / D,
                             bias=eps_t[:, 0:1]).then_inc(sumsq_read, 1)

            def hi(n, src, slot):
                A.activation(y_hi[:, slot, :], src, ACT.Copy).then_inc(a_hi, 1)

            def prep(step):
                act.wait_ge(inputs_in, 64)
                act.wait_ge(prep_v, 1)
                A.activation(small[:, 0:LT], small[:, 0:LT], ACT.Exp, scale=-1.0).then_inc(prep_a, 1)
                act.wait_ge(prep_v, PREP_V)
                act.wait_ge(x_in, 16)
                for c in range(AHEAD):
                    act.wait_ge(raw_loaded[c], 16)
                    A.activation(w_hi[:, c, :], w_raw[:, c, :], ACT.Copy).then_inc(hi_ready, 1)

            def gain_column(step, k):
                g = step.args["gain"]
                if isinstance(g, int):
                    return vec_t[:, g + k:g + k + 1]
                base = V_LAYER + {"mix": L_MIX, "mlp": L_MLP}[g] + k
                return vec_t[:, bass.ds(T.var("layer") * L_COLS + base, 1)]

            def norm(step):
                for k in range(DT):
                    A.activation(h_hi[:, k, :], x[:, k, :], ACT.Copy, scale=gain_column(step, k))\
                        .then_inc(a_hi, 1)
                squares()

            def squares():
                for k in range(DT):
                    if k >= 2:
                        act.wait_ge(vec, T.value("vec", k - 1))
                    A.activation(xsq[:, k % 2, :], x[:, k, :], ACT.Square).then_inc(act_out, 1)

            def x_step(step):
                b = step.args["b"]
                vb = 1 + TT if step.args["stats"] else 0
                for n in range(4):
                    col = V_CW + (CONV1 - 1) * LT + 4 * b + n
                    bias = V_CBIAS + 4 * b + n
                    act.wait_ge(evacuated, T.value("turn", n + 1, 4))
                    A.activation(xc[:, 4 * b + n, :], u_pad[:, n, CONV1 - 1:], ACT.Identity,
                                 scale=vec_t[:, col:col + 1], bias=vec_t[:, bias:bias + 1]).then_inc(act_out, 1)
                for n in range(4):
                    act.wait_ge(vec, T.value("vec", vb + 8 + n + 1))
                    hi(n, xc[:, 4 * b + n, :], xc_slot(b, n))

            def gates(step):
                b = step.args["b"]
                for half in range(2):
                    if half:
                        act.wait_ge(vec, T.value("vec", 6))
                    for q in range(2):
                        blk = 4 * b + 2 * half + q
                        for n, (to, bias) in enumerate(((g_r, V_BA), (g_i, V_BX))):
                            banks(2 * q + n, half)
                            set_ = 4 * ((T.fixed["turn"] + half) % 2)
                            A.activation(to[:, q, :], bank[set_ + 2 * q + n][:, :], ACT.Sigmoid,
                                         bias=vec_t[:, bias + blk:bias + blk + 1]).then_inc(act_out, 1)
                    done = 9 * half
                    for q in range(2):
                        blk = 4 * b + 2 * half + q
                        act.wait_ge(act_out, T.value("act_out", done + 4))
                        A.activation(g_t[:, q, :], g_r[:, q, :], ACT.Tanh, scale=rate[:, blk:blk + 1])\
                            .then_inc(act_out, 1)
                    for q in range(2):
                        blk = 4 * b + 2 * half + q
                        A.activation(g_d[:, q, :], g_r[:, q, :], ACT.Exp, scale=rate_m2[:, blk:blk + 1])\
                            .then_inc(act_out, 1)
                    act.wait_ge(vec, T.value("vec", 6 * half + 1))
                    A.activation(g_t, g_t, ACT.Sqrt, scale=-1.0).then_inc(act_out, 1)

            def in_place(tile, func):
                for n in range(4):
                    act.wait_ge(evacuated, T.value("turn", n + 1, 4))
                    A.activation(tile(n), tile(n), func).then_inc(act_out, 1)

            def split_vec(tile, slot, first):
                for n in range(4):
                    act.wait_ge(vec, T.value("vec", first(n)))
                    hi(n, tile(n), slot(n))

            def lru_gate(step):
                b = step.args["b"]
                in_place(lambda n: gate_t[:, n, 0:SEQ], ACT.Silu)
                split_vec(lambda n: gate_t[:, n, 0:SEQ], lambda n: 4 * b + n, lambda n: n + 1)

            def fox_gate(step):
                half = T.var("half")
                in_place(lambda n: fox_t[:, n, :], ACT.Silu)
                split_vec(lambda n: fox_t[:, n, :], lambda n: half * 4 + n, lambda n: n + 1)

            def forget(step):
                act.wait_ge(vec, T.value("vec", 1 + TT + 2))
                A.activation(ft(1), ft(1), ACT.Exp, scale=-1.0).then_inc(act_out, 1)

            def attention(step):
                def heads(count, plus=0):
                    return T.value("halves", plus, count * HEADS // 2)

                def exps(hh):
                    sm = 32 * (hh % 2)
                    if hh >= 2:
                        act.wait_ge(turned, heads(3, 3 * (hh - 1)))
                    for t in range(TT):
                        act.wait_ge(max_ready, heads(8, 8 * hh + 2 * t + 2))
                        at = P * t * (t + 1) // 2
                        A.activation(probs[:, hh % 2, at:at + P * (t + 1)], bank[t][:, 0:P * (t + 1)], ACT.Exp,
                                     bias=small[:, sm + 4 + t:sm + 5 + t],
                                     accum_out=small[:, sm + 8 + t:sm + 9 + t]).then_inc(exp_ready, 1)

                def copies(hh):
                    if hh:
                        act.wait_ge(o_ready, heads(1, hh))
                    for j in range(2):
                        act.wait_ge(turned, heads(3, 3 * hh + j + 1))
                        at, n = tri(j)
                        A.activation(probs_t[:, at:at + n], turned_bank(j)[:, 0:n], ACT.Copy)\
                            .then_inc(turned_act, 1)

                exps(0)
                for hh in range(HEADS // 2):
                    if hh + 1 < HEADS // 2:
                        exps(hh + 1)
                    copies(hh)

            def whole_norm(step):
                squares()
                act.wait_ge(norm_ready, 1 if step.kind == "midnorm" else 2)
                A.activation(rms[:, :], bank[4 * (T.fixed["turn"] % 2)][:, :], ACT.Sqrt, scale=1.0 / D,
                             bias=eps_t[:, 0:1]).then_inc(act_out, 1)

            def trig(step):
                act.wait_ge(vec, T.value("vec", 10))
                A.activation(sin_t, area(1024, SEQ), ACT.Sin, scale=pcol[:, 1:2]).then_inc(act_out, 1)
                act.wait_ge(vec, T.value("vec", 19))
                A.activation(cos_t, area(1536, SEQ), ACT.Sin).then_inc(act_out, 1)

            def qk_step(step):
                vb = 1 + TT
                set_ = 4 * (T.fixed["turn"] % 2)
                for n in range(4):
                    banks(n)
                    if n >= 2:
                        act.wait_ge(vec, T.value("vec", vb + 2 + 2 * (n - 1)))
                    for a, b in ((0, RQK // 2), (RQK // 2, 0)):
                        A.activation(swap[a:a + RQK // 2, n % 2, :], bank[set_ + n][b:b + RQK // 2, :],
                                     ACT.Copy).then_inc(act_out, 1)

            def ret_out(step):
                act.wait_ge(vec, T.value("vec", TT + 6))
                A.activation(small[:, 72:76], small[:, 64:68], ACT.Sqrt, scale=1.0 / RV, bias=eps_t[:, 0:1])\
                    .then_inc(act_out, 1)

            def ret_turn(step):
                half = T.var("half")
                for n in range(4):
                    act.wait_ge(evacuated, T.value("turn", n + 1, 4))
                    hi(n, sg[:, n, :], half * 4 + n)

            def g_step(step):
                in_place(lambda n: sg[:, n, :], ACT.Silu)

            def gb_step(step):
                half = T.var("half")
                in_place(lambda n: m_t[:, half * 4 + n, :], ACT.Sigmoid)

            def ga_step(step):
                half = T.var("half")
                in_place(lambda n: ga_t[:, half * 4 + n, :], ACT.Sigmoid)

            def cb_step(step):
                half = T.var("half")
                split_vec(lambda n: tmp2[:, n % 2, :], lambda n: half * 4 + n,
                          lambda n: 8 * (n // 2) + 6 + n % 2 + 1)

            def merge(step):
                j = step.args["j"]
                split_vec(lambda n: ga_t[:, 4 * j + n, :], lambda n: 8 + n if j == 0 else n, lambda n: n + 1)

            def up(step):
                vb = 1 + TT if step.args["stats"] else 0
                split_vec(lambda n: up_t[:, n, :], lambda n: 4 * step.args["j"] + n, lambda n: vb + n + 1)

            kinds = {"prep": prep, "norm": norm, "x": x_step, "gates": gates, "lru_gate": lru_gate,
                     "forget": forget, "attention": attention, "fox_gate": fox_gate,
                     "midnorm": whole_norm, "trig": trig, "qk": qk_step, "ret_out": ret_out,
                     "ret_turn": ret_turn, "g": g_step, "gb": gb_step, "ga": ga_step, "cb": cb_step,
                     "merge": merge, "up": up, "final": whole_norm}

            def emit(step):
                split_ahead(step)
                if step.kind in kinds:
                    join()
                    if step.args["stats"]:
                        statistics(step)
                    kinds[step.kind](step)

            T.walk(act, steps, emit)

        @block.vector
        def _(dve):
            T = Tally()
            V = nc.vector

            def split_ahead(step):
                for n, slot in split_slots(T, step):
                    dve.wait_ge(hi_ready, T.value("chunk", n + 1))
                    V.tensor_tensor(w_lo[:, slot, :], w_raw[:, slot, :], w_hi[:, slot, :].bitcast(F32),
                                    ALU.subtract).then_inc(lo_ready, 1)

            def join():
                wait(dve, evacuated, T.value("turn", 0, 4))
                for s, name in ((vec, "vec"), (a_lo, "a_lo"), (act_out, "act_out"), (a_hi, "a_hi")):
                    wait(dve, s, T.value(name))

            def banks(n, plus=0):
                dve.wait_ge(bank_ready, T.value("turn", 4 * plus + n + 1, 4))

            def got(n):
                dve.wait_ge(vec, T.value("vec", n))

            def read(n):
                dve.wait_ge(evacuated, T.value("turn", n + 1, 4))

            def acted(n):
                dve.wait_ge(act_out, T.value("act_out", n))

            def the_bank(n):
                return bank[4 * (T.fixed["turn"] % 2) + n]

            def evacuate(tile):
                for n in range(4):
                    banks(n)
                    V.tensor_tensor(tile(n), the_bank(n)[:, :], rms[:, :], ALU.mult).then_inc(evacuated, 1)

            def split_lo(tile, slot):
                for n in range(4):
                    dve.wait_ge(a_hi, T.value("a_hi", n + 1))
                    V.tensor_tensor(y_lo[:, slot(n), :], tile(n), y_hi[:, slot(n), :].bitcast(F32),
                                    ALU.subtract).then_inc(a_lo, 1)

            def statistics():
                dve.wait_ge(sumsq_read, T.value("stats", 1))
                V.reciprocal(rms[:, :], rms[:, :]).then_inc(vec, 1)
                for t in range(TT):
                    got(1 + t)
                    V.tensor_tensor_reduce(junk[:, :], rms[:, t * P:t * P + P], ident[:, :], 1.0, 0.0,
                                           ALU.mult, ALU.add, rms_col[:, t:t + 1]).then_inc(vec, 1)
                got(1 + TT)

            def prep(step):
                count = [0]

                def link(ins):
                    count[0] += 1
                    ins.then_inc(prep_v, 1)
                    dve.wait_ge(prep_v, count[0])

                a = vec_t[:, V_AP:V_AP + LT]
                c0, c1, c2, c3 = (small[:, LT * n:LT * n + LT] for n in range(4))
                dve.wait_ge(inputs_in, 64)
                link(V.scalar_tensor_tensor(out=c0, in0=a, scalar=-1.0, in1=a, op0=ALU.mult, op1=ALU.max))
                dve.wait_ge(prep_a, 1)
                link(V.tensor_scalar(c1, c0, 2.0, None, ALU.add))
                link(V.reciprocal(c1, c1))
                link(V.tensor_tensor(c0, c0, c1, ALU.mult))
                link(V.tensor_tensor(c1, c0, c0, ALU.mult))
                link(V.tensor_scalar(c2, c1, ATANH[0], None, ALU.mult))
                for c in ATANH[1:] + [1.0]:
                    link(V.scalar_tensor_tensor(out=c2, in0=c2, scalar=c, in1=c1 if c < 1 else c0,
                                                op0=ALU.add, op1=ALU.mult))
                link(V.tensor_scalar(c3, a, -1.0, 0.0, ALU.mult, ALU.max))
                link(V.scalar_tensor_tensor(out=c3, in0=c2, scalar=2.0, in1=c3, op0=ALU.mult, op1=ALU.add))
                link(V.tensor_scalar(rate[:, :], c3, LRU_C / 2, None, ALU.mult))
                link(V.tensor_scalar(rate_m2[:, :], c3, -LRU_C, None, ALU.mult))
                link(V.tensor_copy(mask_b[:, :], junk[:, :]))
                link(V.tensor_copy(ident_b[:, :], ident[:, :]))
                link(V.memset(ones_b[:, :], 1.0))
                link(V.memset(ones[:, :], 1.0))
                link(V.memset(eps_t[:, :], EPS))
                link(V.memset(u_pad[:, :, 0:CONV1 - 1], 0.0))
                assert count[0] == PREP_V
                dve.wait_ge(x_in, 16)
                for c in range(AHEAD):
                    dve.wait_ge(hi_ready, c + 1)
                    V.tensor_tensor(w_lo[:, c, :], w_raw[:, c, :], w_hi[:, c, :].bitcast(F32),
                                    ALU.subtract).then_inc(lo_ready, 1)

            def gain_column(step, k):
                g = step.args["gain"]
                if isinstance(g, int):
                    return vec_t[:, g + k:g + k + 1]
                base = V_LAYER + {"mix": L_MIX, "mlp": L_MLP}[g] + k
                return vec_t[:, bass.ds(T.var("layer") * L_COLS + base, 1)]

            def sum_squares():
                for k in range(DT):
                    acted(k + 1)
                    if k == 0:
                        V.tensor_copy(sumsq[:, :], xsq[:, 0, :]).then_inc(vec, 1)
                    else:
                        got(k)
                        V.tensor_tensor(sumsq[:, :], sumsq[:, :], xsq[:, k % 2, :], ALU.add).then_inc(vec, 1)

            def norm(step):
                for k in range(DT):
                    dve.wait_ge(a_hi, T.value("a_hi", k + 1))
                    V.scalar_tensor_tensor(out=h_lo[:, k, :], in0=x[:, k, :], scalar=gain_column(step, k),
                                           in1=h_hi[:, k, :].bitcast(F32), op0=ALU.mult,
                                           op1=ALU.subtract).then_inc(a_lo, 1)
                sum_squares()

            def x_step(step):
                b = step.args["b"]
                vb = 1 + TT if step.args["stats"] else 0
                evacuate(lambda n: u_pad[:, n, CONV1 - 1:])
                for tap in range(1, CONV1):
                    for n in range(4):
                        if tap == 1:
                            acted(n + 1)
                            read(n)
                        else:
                            got(vb + 4 * (tap - 2) + n + 1)
                        col = V_CW + (CONV1 - 1 - tap) * LT + 4 * b + n
                        at = CONV1 - 1 - tap
                        V.scalar_tensor_tensor(out=xc[:, 4 * b + n, :], in0=u_pad[:, n, at:at + SEQ],
                                               scalar=vec_t[:, col:col + 1], in1=xc[:, 4 * b + n, :],
                                               op0=ALU.mult, op1=ALU.add).then_inc(vec, 1)
                split_lo(lambda n: xc[:, 4 * b + n, :], lambda n: xc_slot(b, n))

            def gates(step):
                b = step.args["b"]
                for half in range(2):
                    blk = 4 * b + 2 * half
                    va, aa = 6 * half, 9 * half
                    acted(aa + 8)
                    V.scalar_tensor_tensor(out=g_d, in0=g_d, scalar=1.0, in1=g_t, op0=ALU.add,
                                           op1=ALU.mult).then_inc(evacuated, 4)
                    dve.wait_ge(evacuated, T.value("turn", 4 * half + 4, 4))
                    V.scalar_tensor_tensor(out=g_t, in0=g_d, scalar=2.0, in1=g_d, op0=ALU.subtract,
                                           op1=ALU.mult).then_inc(vec, 1)
                    V.tensor_tensor(g_i, g_i, xc[:, blk:blk + 2, :], ALU.mult).then_inc(vec, 1)
                    got(va + 1)
                    V.tensor_scalar(g_d, g_d, -1.0, 1.0, ALU.mult, ALU.add).then_inc(vec, 1)
                    got(va + 2)
                    acted(aa + 9)
                    V.tensor_tensor(g_i, g_i, g_t, ALU.mult).then_inc(vec, 1)
                    got(va + 4)
                    for q in range(2):
                        V.tensor_tensor_scan(xc[:, blk + q, :], g_d[:, q, :], g_i[:, q, :], 0.0,
                                             ALU.mult, ALU.add).then_inc(vec, 1)

            def gate_times(tile, other, slot):
                for n in range(4):
                    acted(n + 1)
                    V.tensor_tensor(tile(n), tile(n), other(n), ALU.mult).then_inc(vec, 1)
                split_lo(tile, slot)

            def lru_gate(step):
                b = step.args["b"]
                evacuate(lambda n: gate_t[:, n, 0:SEQ])
                gate_times(lambda n: gate_t[:, n, 0:SEQ], lambda n: xc[:, 4 * b + n, :], lambda n: 4 * b + n)

            def residual(step):
                j = step.args["j"]
                for n in range(4):
                    banks(n)
                    V.tensor_tensor(x[:, 4 * j + n, :], the_bank(n)[:, :], x[:, 4 * j + n, :], ALU.add)\
                        .then_inc(evacuated, 1)

            def forget(step):
                count = [1 + TT]

                def link(ins):
                    count[0] += 1
                    ins.then_inc(vec, 1)
                    got(count[0])

                banks(3)
                V.tensor_tensor(ft(0), the_bank(0)[0:HEADS, :], rms[0:HEADS, :], ALU.mult).then_inc(evacuated, 4)
                read(3)
                link(V.tensor_scalar(ft(0), ft(0), vec_t[0:HEADS, V_BF:V_BF + 1], None, ALU.add))
                link(V.scalar_tensor_tensor(out=ft(1), in0=ft(0), scalar=-1.0, in1=ft(0), op0=ALU.mult,
                                            op1=ALU.max))
                acted(1)
                link(V.tensor_scalar(ft(2), ft(1), 2.0, None, ALU.add))
                link(V.reciprocal(ft(2), ft(2)))
                link(V.tensor_tensor(ft(1), ft(1), ft(2), ALU.mult))
                link(V.tensor_tensor(ft(2), ft(1), ft(1), ALU.mult))
                link(V.tensor_scalar(ft(3), ft(2), ATANH[0], None, ALU.mult))
                for c in ATANH[1:] + [1.0]:
                    link(V.scalar_tensor_tensor(out=ft(3), in0=ft(3), scalar=c, in1=ft(2) if c < 1 else ft(1),
                                                op0=ALU.add, op1=ALU.mult))
                link(V.tensor_scalar(ft(0), ft(0), 0.0, None, ALU.min))
                link(V.scalar_tensor_tensor(out=ft(1), in0=ft(3), scalar=2.0, in1=ft(0), op0=ALU.mult,
                                            op1=ALU.subtract))
                link(V.memset(ft(2), 1.0))
                link(V.tensor_tensor_scan(ft(0), ft(2), ft(1), 0.0, ALU.mult, ALU.add))
                link(V.tensor_copy(cum_part(0), ft(0)))
                link(V.tensor_tensor(ft(0), ft(0), cum_part(0), ALU.subtract))
                link(V.tensor_copy(cum_part(1), ft(0)))
                link(V.tensor_tensor(ft(0), ft(0), cum_part(1), ALU.subtract))
                link(V.tensor_copy(cum_part(2), ft(0)))
                assert count[0] == step.incs["vec"], count

            def fq_step(step):
                for n in range(4):
                    banks(n)
                    V.scalar_tensor_tensor(out=fq[:, n, :], in0=the_bank(n)[:, :], scalar=HD ** -0.5,
                                           in1=rms[:, :], op0=ALU.mult, op1=ALU.mult).then_inc(evacuated, 1)

            def v_step(step):
                to = v_tok if step.args["to"] == "fox" else rv
                for t in range(TT):
                    banks(t)
                    V.tensor_scalar(to[:, t, :], the_bank(t)[:, :], rms_col[:, t:t + 1], None, ALU.mult)\
                        .then_inc(evacuated, 1)

            def attention(step):
                def heads(count, plus=0):
                    return T.value("halves", plus, count * HEADS // 2)

                def maxima(hh):
                    sm = 32 * (hh % 2)
                    for t in range(TT):
                        dve.wait_ge(scores_ready, heads(4, 4 * hh + t + 1))
                        V.tensor_reduce(small[:, sm + t:sm + t + 1], bank[t][:, 0:P * (t + 1)], AX_X, ALU.max)\
                            .then_inc(max_ready, 1)
                        dve.wait_ge(max_ready, heads(8, 8 * hh + 2 * t + 1))
                        if hh >= 2 and t == 0:
                            dve.wait_ge(exp_ready, heads(4, 4 * (hh - 1)))
                        V.tensor_scalar(small[:, sm + 4 + t:sm + 5 + t], small[:, sm + t:sm + t + 1], -1.0, None,
                                        ALU.mult).then_inc(max_ready, 1)

                def normalise(hh):
                    sm = 32 * (hh % 2)
                    dve.wait_ge(exp_ready, heads(4, 4 * hh + 4))
                    V.reciprocal(small[:, sm + 12:sm + 16], small[:, sm + 8:sm + 12]).then_inc(probs_ready, 1)
                    dve.wait_ge(probs_ready, heads(5, 5 * hh + 1))
                    for t in range(TT):
                        at = P * t * (t + 1) // 2
                        p_t = probs[:, hh % 2, at:at + P * (t + 1)]
                        V.tensor_scalar(p_t, p_t, small[:, sm + 12 + t:sm + 13 + t], None, ALU.mult)\
                            .then_inc(probs_ready, 1)

                def copies(hh):
                    if hh:
                        dve.wait_ge(o_ready, heads(1, hh))
                    dve.wait_ge(turned, heads(3, 3 * hh + 3))
                    at, n = tri(2)[0], 3 * P
                    V.tensor_copy(probs_t[:, at:at + n], bank[6][:, 0:n]).then_inc(turned_vec, 1)

                def output(hh):
                    rows = slice(HD * (hh % 2), HD * (hh % 2) + HD)
                    dve.wait_ge(o_ready, heads(1, hh + 1))
                    V.tensor_copy(fq[rows, hh // 2, :], bank[7][rows, :]).then_inc(o_copied, 1)

                maxima(0)
                normalise(0)
                for hh in range(HEADS // 2):
                    if hh + 1 < HEADS // 2:
                        maxima(hh + 1)
                    if hh:
                        output(hh - 1)
                    copies(hh)
                    if hh + 1 < HEADS // 2:
                        normalise(hh + 1)
                output(HEADS // 2 - 1)
                dve.wait_ge(o_copied, heads(1, HEADS // 2))

            def fox_gate(step):
                half = T.var("half")
                evacuate(lambda n: fox_t[:, n, :])
                gate_times(lambda n: fox_t[:, n, :], lambda n: fq[:, n, :], lambda n: half * 4 + n)

            def whole_norm(step):
                sum_squares()
                acted(DT + 1)
                V.reciprocal(rms[:, :], rms[:, :]).then_inc(vec, 1)
                got(DT + 1)
                last = step.kind == "final"
                g = V_NF if last else V_FG
                for k in range(DT):
                    V.scalar_tensor_tensor(out=x[:, k, :], in0=x[:, k, :], scalar=vec_t[:, g + k:g + k + 1],
                                           in1=rms[:, :], op0=ALU.mult, op1=ALU.mult)\
                        .then_inc(out_ready if last else vec, 1)

            def trig(step):
                count = [0]

                def link(ins):
                    count[0] += 1
                    ins.then_inc(vec, 1)
                    got(count[0])

                angle, k_t, r_s, r_c = (area(SEQ * n, SEQ) for n in range(4))
                dve.wait_ge(decay_in, 32)
                link(V.tensor_copy(cos_t, sin_t.bitcast(I32)))
                link(V.tensor_scalar(angle, cos_t, pcol[:, 0:1], None, ALU.mult))

                def reduce(out, quarter):
                    link(V.tensor_scalar(k_t, angle, 1 / (2 * math.pi), quarter, ALU.mult, ALU.add))
                    link(V.tensor_scalar(k_t, k_t, MAGIC, None, ALU.add))
                    link(V.tensor_scalar(k_t, k_t, MAGIC, None, ALU.subtract))
                    for n, part in enumerate(two_pi_parts()):
                        link(V.scalar_tensor_tensor(out=out, in0=k_t, scalar=-part, in1=out if n else angle,
                                                    op0=ALU.mult, op1=ALU.add))
                top = 3.1415925
                reduce(r_s, 0.0)
                link(V.tensor_scalar(r_s, r_s, top, -top, ALU.min, ALU.max))
                reduce(r_c, 0.25)
                link(V.tensor_scalar(r_c, r_c, math.pi / 2, top, ALU.add, ALU.min))
                link(V.tensor_scalar(r_c, r_c, -top, None, ALU.max))
                assert count[0] == 19, count

            def qk_step(step):
                vb = 1 + TT
                V.tensor_tensor(cos_r, cos_t, rms[:, :], ALU.mult).then_inc(vec, 1)
                V.tensor_tensor(sin_r, sin_t, rms[:, :], ALU.mult).then_inc(vec, 1)
                got(vb + 2)
                for n in range(4):
                    acted(2 * n + 2)
                    V.tensor_tensor(swap[:, n % 2, :], swap[:, n % 2, :], sin_r, ALU.mult).then_inc(vec, 1)
                    V.tensor_tensor(qk[:, n, :], the_bank(n)[:, :], cos_r, ALU.mult).then_inc(evacuated, 1)
                    got(vb + 2 + 2 * n + 1)
                    read(n)
                    V.tensor_tensor(qk[:, n, :], qk[:, n, :], swap[:, n % 2, :], ALU.add).then_inc(vec, 1)

            def ret_scores(step):
                hh = step.args["hh"]
                half = T.var("half")
                for j in range(TT):
                    at, n = tri(j)
                    banks(j)
                    V.scalar_tensor_tensor(out=st[:, hh, at:at + n], in0=the_bank(j)[:, 0:n],
                                           scalar=RQK ** -0.5, in1=decay[:, half * 2 + hh, 0:n],
                                           op0=ALU.mult, op1=ALU.mult).then_inc(evacuated, 1)

            def ret_out(step):
                hh = step.args["hh"]
                for t in range(TT):
                    banks(t)
                    V.bn_stats(small[:, 32 + 6 * t:38 + 6 * t], the_bank(t)[:, 0:RV]).then_inc(vec, 1)
                parts = small[:, 32:32 + 6 * TT].rearrange("p (t s) -> p t s", s=6)
                diff, mean, var = small[:, 56:60], small[:, 60:64], small[:, 64:68]
                got(TT)
                V.tensor_tensor(diff, parts[:, :, 1], parts[:, :, 4], ALU.subtract).then_inc(vec, 1)
                V.tensor_tensor(mean, parts[:, :, 1], parts[:, :, 4], ALU.add).then_inc(vec, 1)
                V.tensor_tensor(var, parts[:, :, 2], parts[:, :, 5], ALU.add).then_inc(vec, 1)
                got(TT + 1)
                V.scalar_tensor_tensor(out=diff, in0=diff, scalar=RV / 4, in1=diff, op0=ALU.mult,
                                       op1=ALU.mult).then_inc(vec, 1)
                got(TT + 2)
                V.tensor_scalar(mean, mean, 0.5, None, ALU.mult).then_inc(vec, 1)
                got(TT + 4)
                V.tensor_tensor(var, var, diff, ALU.add).then_inc(vec, 1)
                acted(1)
                V.reciprocal(small[:, 76:80], small[:, 72:76]).then_inc(vec, 1)
                got(TT + 7)
                for t in range(TT):
                    V.tensor_scalar(st[:, hh, t * RV:t * RV + RV], the_bank(t)[:, 0:RV],
                                    small[:, 60 + t:61 + t], small[:, 76 + t:77 + t],
                                    ALU.subtract, ALU.mult).then_inc(evacuated, 1)

            def layer_column(at):
                return vec_t[:, bass.ds(T.var("layer") * L_COLS + at, 1)]

            def ret_turn(step):
                half = T.var("half")
                for n in range(4):
                    banks(n)
                    col = vec_t[:, bass.ds(T.var("layer") * L_COLS + (half * 4 + (V_LAYER + L_RN + n)), 1)]
                    V.scalar_tensor_tensor(out=sg[:, n, :], in0=the_bank(n)[:, :], scalar=col, in1=sg[:, n, :],
                                           op0=ALU.mult, op1=ALU.mult).then_inc(evacuated, 1)
                split_lo(lambda n: sg[:, n, :], lambda n: half * 4 + n)

            def g_step(step):
                evacuate(lambda n: sg[:, n, :])

            def gb_step(step):
                half = T.var("half")
                evacuate(lambda n: m_t[:, half * 4 + n, :])

            def ga_step(step):
                half = T.var("half")
                evacuate(lambda n: ga_t[:, half * 4 + n, :])

            def ret_proj(step):
                half = T.var("half")
                for n in range(4):
                    banks(n)
                    m = m_t[:, half * 4 + n, :]
                    V.tensor_tensor(m, the_bank(n)[:, :], m, ALU.mult).then_inc(evacuated, 1)

            def cc_step(step):
                V.memset(z_pad[:, :, 0:CONV2 - 1], 0.0).then_inc(vec, 1)
                evacuate(lambda n: z_pad[:, n, CONV2 - 1:])

            def cu_step(step):
                for n in range(4):
                    banks(n)
                    if n >= 2:
                        got(n - 1)
                    V.tensor_tensor(tmp2[:, n % 2, :], the_bank(n)[:, :], rms[:, :], ALU.mult).then_inc(evacuated, 1)
                    read(n)
                    z = z_pad[:, n, CONV2 - 1:]
                    V.tensor_tensor(z, z, tmp2[:, n % 2, :], ALU.mult).then_inc(vec, 1)

            def cb_step(step):
                half = T.var("half")
                for pair in range(2):
                    vb = 8 * pair
                    if pair:
                        dve.wait_ge(a_lo, T.value("a_lo", 2))
                    for tap in range(CONV2):
                        for q in range(2):
                            n = 2 * pair + q
                            col = vec_t[:, bass.ds(T.var("layer") * L_COLS + (
                                half * 4 + (V_LAYER + L_CW + (CONV2 - 1 - tap) * DT + n)), 1)]
                            z = z_pad[:, n, CONV2 - 1 - tap:CONV2 - 1 - tap + SEQ]
                            if tap == 0:
                                V.tensor_scalar(tmp2[:, q, :], z, col, None, ALU.mult).then_inc(vec, 1)
                            else:
                                got(vb + 2 * tap - 2 + q + 1)
                                V.scalar_tensor_tensor(out=tmp2[:, q, :], in0=z, scalar=col, in1=tmp2[:, q, :],
                                                       op0=ALU.mult, op1=ALU.add).then_inc(vec, 1)
                    for q in range(2):
                        n = 2 * pair + q
                        banks(n)
                        got(vb + 4 + q + 1)
                        V.tensor_tensor(tmp2[:, q, :], the_bank(n)[:, :], tmp2[:, q, :], ALU.mult)\
                            .then_inc(evacuated, 1)
                    for q in range(2):
                        read(2 * pair + q)
                        V.tensor_tensor(tmp2[:, q, :], tmp2[:, q, :], rms[:, :], ALU.mult).then_inc(vec, 1)
                    for q in range(2):
                        n = 2 * pair + q
                        dve.wait_ge(a_hi, T.value("a_hi", n + 1))
                        V.tensor_tensor(y_lo[:, half * 4 + n, :], tmp2[:, q, :],
                                        y_hi[:, half * 4 + n, :].bitcast(F32), ALU.subtract).then_inc(a_lo, 1)

            def merge(step):
                j = step.args["j"]
                for n in range(4):
                    banks(n)
                    g = ga_t[:, 4 * j + n, :]
                    V.tensor_tensor(g, the_bank(n)[:, :], g, ALU.mult).then_inc(evacuated, 1)
                for n in range(4):
                    read(n)
                    g = ga_t[:, 4 * j + n, :]
                    V.tensor_tensor(g, g, m_t[:, 4 * j + n, :], ALU.add).then_inc(vec, 1)
                split_lo(lambda n: ga_t[:, 4 * j + n, :], lambda n: 8 + n if j == 0 else n)

            def up(step):
                evacuate(lambda n: up_t[:, n, :])
                for n in range(4):
                    read(n)
                    V.scalar_tensor_tensor(out=up_t[:, n, :], in0=up_t[:, n, :], scalar=0.0, in1=up_t[:, n, :],
                                           op0=ALU.max, op1=ALU.mult).then_inc(vec, 1)
                split_lo(lambda n: up_t[:, n, :], lambda n: 4 * step.args["j"] + n)

            kinds = {"prep": prep, "norm": norm, "x": x_step, "gates": gates, "lru_gate": lru_gate,
                     "residual": residual, "forget": forget, "fq": fq_step,
                     "fk": lambda step: evacuate(lambda n: fk[:, n, :]), "v": v_step,
                     "attention": attention, "fox_gate": fox_gate, "midnorm": whole_norm, "trig": trig,
                     "qk": qk_step, "ret_scores": ret_scores, "ret_out": ret_out, "ret_turn": ret_turn,
                     "g": g_step, "gb": gb_step, "ret_proj": ret_proj, "cc": cc_step, "cu": cu_step,
                     "cb": cb_step, "ga": ga_step, "merge": merge, "up": up, "final": whole_norm}

            def emit(step):
                split_ahead(step)
                join()
                if step.args["stats"]:
                    statistics()
                kinds[step.kind](step)

            T.walk(dve, steps, emit)



def order_of_weights(lru_w_in, lru_wa, lru_wx, lru_w_out, fox_w_in, fox_w_out, w_in, w_conv_out,
                     w_ret_out, w_o, w_up, w_down):
    def group(w, columns, rows=None):
        w = w[rows] if rows is not None else w
        cols = np.concatenate([w[:, a:a + n] for a, n in columns], axis=1)
        return cols.reshape(-1, KT, P, 512).transpose(0, 2, 1, 3).reshape(-1, P, CW)

    out = []
    for kind, args in flat_order():
        b = args.get("b", 0)
        half = args.get("half", 0)
        layer = args.get("layer", 0)
        j = args.get("j", 0)
        if kind == "x":
            out.append(group(lru_w_in, [(512 * b, 512)]))
        elif kind == "gates":
            blocks = slice(4 * b, 4 * b + 4)
            both = np.stack([lru_wa[blocks], lru_wx[blocks]])
            out.append(both.transpose(2, 0, 1, 3).reshape(1, P, CW))
        elif kind == "lru_gate":
            out.append(group(lru_w_in, [(LRU_W + 512 * b, 512)]))
        elif kind == "residual" and args["k"] == "lru":
            out.append(group(lru_w_out, [(512 * j, 512)]))
        elif kind == "residual" and "layer" not in args:
            out.append(group(fox_w_out, [(512 * j, 512)]))
        elif kind == "residual" and args["k"] == "m":
            out.append(group(w_o[layer], [(512 * j, 512)]))
        elif kind == "residual":
            q = args["quarter"]
            out.append(group(w_down[layer], [(512 * j, 512)], slice(1024 * q, 1024 * q + 1024)))
        elif kind == "forget":
            w = np.zeros((D, P), fox_w_in.dtype)
            w[:, 0:HEADS] = fox_w_in[:, 4 * D:]
            out.append(w.reshape(DT, P, P).transpose(1, 0, 2).reshape(1, P, CW))
        elif kind in ("fq", "fk", "fox_gate") or (kind == "v" and "layer" not in args):
            at = {"fq": 0, "fk": D, "v": 2 * D, "fox_gate": 3 * D}[kind]
            out.append(group(fox_w_in, [(at + 512 * half, 512)]))
        elif kind == "qk":
            out.append(group(w_in[layer], [(CQ + 256 * half, 256), (CK + 256 * half, 256)]))
        elif kind in ("v", "g", "gb", "cc", "cu", "cb", "ga"):
            at = {"v": CV, "g": CG, "gb": CGB, "cc": CC, "cu": CU, "cb": CB, "ga": CGA}[kind]
            out.append(group(w_in[layer], [(at + 512 * half, 512)]))
        elif kind == "ret_proj":
            out.append(group(w_ret_out[layer], [(512 * half, 512)]))
        elif kind == "merge":
            out.append(group(w_conv_out[layer], [(512 * j, 512)]))
        elif kind == "up":
            out.append(group(w_up[layer], [(1024 * args["quarter"] + 512 * j, 512)]))
    out.append(np.zeros((AHEAD, P, CW), np.float32))
    return np.concatenate(out)


def flat_order():
    def walk(items, env):
        for item in items:
            if isinstance(item, Loop):
                for i in range(item.count):
                    yield from walk(item.body, {**env, item.name: i})
            else:
                yield item.kind, {**env, **item.args}
    return walk(schedule(), {})


def shape_constants():
    out = np.zeros((P, K_COLS), np.float32)
    half = RQK // 2
    inv = np.float32(ROPE_BASE) ** (-np.arange(half, dtype=np.float32) / np.float32(half))
    out[:, K_INVF] = np.tile(inv, 2)
    out[:, K_SIGN] = np.repeat([-1.0, 1.0], half)
    out[:, K_IDENT:K_IDENT + P] = np.eye(P)
    row, col = np.arange(P)[:, None], np.arange(P)[None, :]
    out[:, K_MASK:K_MASK + P] = np.where(col > row, -1e30, 0.0)
    rel = (np.arange(SEQ)[None, :] - np.arange(P)[:, None]).astype(np.float64)
    for h in range(RH):
        log_gamma = np.log1p(-(2.0 ** (-5.0 - h)))
        out[:, K_DECAY + h * SEQ:K_DECAY + (h + 1) * SEQ] = np.where(
            rel >= 0, np.exp(log_gamma * np.maximum(rel, 0)), 0.0)
    return out


def kernel(**inputs):
    from concourse import bacc
    from concourse.bass_utils import run_bass_kernel_spmd

    a = {k: np.asarray(v) for k, v in inputs.items()}

    def columns(*vectors):
        return np.concatenate([v.reshape(-1, P).T for v in vectors], axis=1)

    b_f = np.zeros((P, 1), np.float32)
    b_f[0:HEADS, 0] = a["fox_b_f"][0]
    vecs = [columns(a["norm_g"][0], a["norm_g"][1], a["final_g"], *a["lru_conv_w"][0], a["lru_conv_b"][0],
                    a["lru_ba"][0], a["lru_bx"][0], a["lru_a_param"][0]), b_f, columns(a["norm_final_2"])]
    for i in range(LAYERS):
        vecs.append(columns(a["norm_mix_2"][i], a["norm_mlp_2"][i], *a["conv_w_2"][i], a["ret_norm_2"][i]))
    arrays = {
        "stream": order_of_weights(a["lru_w_in"][0], a["lru_wa"][0], a["lru_wx"][0], a["lru_w_out"][0],
                                   a["fox_w_in"][0], a["fox_w_out"][0], a["w_in_2"], a["w_conv_out_2"],
                                   a["w_ret_out_2"], a["w_o_2"], a["w_up_2"], a["w_down_2"]),
        "x_t": np.ascontiguousarray(a["x"][0].T),
        "vecs": np.ascontiguousarray(np.concatenate(vecs, axis=1)),
        "consts": shape_constants(),
        "positions": a["positions_2"][0],
    }
    assert arrays["vecs"].shape[1] == V_COLS
    nc = bacc.Bacc("TRN2", target_bir_lowering=False, num_devices=1)
    args = [nc.dram_tensor(f"in_{k}", v.shape, mybir.dt.from_np(v.dtype), kind="ExternalInput").ap()
            for k, v in arrays.items()]
    out = nc.dram_tensor("out_t", (D, SEQ), F32, kind="ExternalOutput").ap()
    scratch = nc.dram_tensor("cum_parts", (3, HEADS, SEQ), BF16).ap()
    build(nc, *args, out, scratch)
    r = run_bass_kernel_spmd(nc, [{f"in_{k}": v for k, v in arrays.items()}], core_ids=[0])
    return np.ascontiguousarray(r.results[0]["out_t"].T)[None]
```

```python
import math
from contextlib import ExitStack

import numpy as np

import concourse.bass as bass
from concourse import mybir
from concourse.alu_op_type import AluOpType as ALU

F32 = mybir.dt.float32
F32R = mybir.dt.float32r
BF16 = mybir.dt.bfloat16
I32 = mybir.dt.int32
ACT = mybir.ActivationFunctionType
AX_X = mybir.AxisListType.X

P = 128
SEQ = 512
D = 1024
DT = D // P
TT = SEQ // P
EPS = 1e-6
LRU_W = 1536
LT = LRU_W // P
LRU_C = 8.0
CONV1 = 4
HEADS = 16
HD = 64
CONV2 = 3
RH = 4
RQK = 128
RV = 256
D_FF = 4096
LAYERS = 2
ROPE_BASE = 10000.0
CB, CC, CU, CQ, CK, CV, CG, CGA, CGB = (int(v) for v in np.cumsum(
    [0, D, D, D, RH * RQK, RH * RQK, RH * RV, RH * RV, D]))

KT = 2
CW = KT * 512
RING = 4
AHEAD = 3
GROUP = DT // KT
TRI = SEQ * (TT + 1) // 2

V_NG = 0
V_FG = V_NG + 2 * DT
V_CW = V_FG + DT
V_CBIAS = V_CW + CONV1 * LT
V_BA = V_CBIAS + LT
V_BX = V_BA + LT
V_AP = V_BX + LT
V_BF = V_AP + LT
V_LAYER = V_BF + 1
L_MIX, L_MLP, L_CW, L_RN = 0, DT, 2 * DT, 2 * DT + CONV2 * DT
L_COLS = L_RN + DT
V_NF = V_LAYER + LAYERS * L_COLS
V_COLS = V_NF + DT
K_INVF, K_SIGN, K_IDENT, K_ONES, K_MASK, K_DECAY = 0, 1, 2, 2 + P, 2 + 2 * P, 2 + 3 * P
K_COLS = K_DECAY + RH * SEQ

A_TAIL = 11276
A_WORDS = A_TAIL + RH * SEQ + 2 * SEQ

RATES_V = 16
CONSTS = 6
MAGIC = float(1.5 * 2 ** 23)
ATANH = [1 / 13, 1 / 11, 1 / 9, 1 / 7, 1 / 5, 1 / 3]


def two_pi_parts():
    parts, rest = [], 2 * math.pi
    for _ in range(3):
        unit = 2.0 ** (math.floor(math.log2(rest)) - 7)
        parts.append(math.floor(rest / unit) * unit)
        rest -= parts[-1]
    return parts + [float(np.float32(rest))]



class Step:
    def __init__(self, kind, chunks=0, turns=0, incs=None, **args):
        self.kind, self.chunks, self.turns, self.args = kind, chunks, turns, args
        self.incs = incs or {}


class Loop:
    def __init__(self, name, count, body):
        self.name, self.count, self.body = name, count, body


SPLIT = {"a_hi": 4, "a_lo": 4}
INCS = {
    "prep": {}, "rates": {}, "enter": {},
    "norm": {"a_hi": DT // 2, "a_lo": DT // 2, "act_out": DT // 2, "vec": DT // 2},
    "x": {"act_out": 4, "vec": 12, **SPLIT},
    "gates": {"act_out": 9, "vec": 7},
    "lru_gate": {"act_out": 4},
    "gate_mul": {"vec": 4, **SPLIT},
    "residual": {},
    "forget": {"act_out": 1, "vec": 22},
    "fq": {}, "fk": {}, "v": {},
    "attention": {},
    "fox_gate": {"act_out": 4, "vec": 4, **SPLIT},
    "renorm": {"act_out": 2 * DT + 1, "vec": 3 * DT + 1, "a_hi": DT, "a_lo": DT},
    "trig": {"act_out": 2, "vec": 19},
    "qk": {"act_out": 8, "vec": 10},
    "ret_scores": {},
    "ret_out": {"act_out": 1, "vec": TT + 7},
    "ret_turn": SPLIT,
    "g": {"act_out": 4},
    "gb": {"act_out": 4},
    "ret_proj": {},
    "cc": {"vec": 1},
    "cu": {"vec": 4},
    "cb": {"vec": 16, **SPLIT},
    "ga": {"act_out": 4},
    "merge": {"vec": 4, **SPLIT},
    "up": {"vec": 4, **SPLIT},
    "final": {"act_out": 1, "vec": 1},
}
STATS = {"stats": 1, "sumsq_read": 1, "vec": 1 + TT}


def schedule():
    def s(kind, chunks=0, turns=0, stats=False, **args):
        incs = dict(INCS[kind])
        if stats:
            for k, v in STATS.items():
                incs[k] = incs.get(k, 0) + v
        return Step(kind, chunks, turns, incs, stats=stats, **args)

    def norm(gain):
        return [s("norm", gain=gain, part=0), s("norm", gain=gain, part=1)]

    def last_product(chunks, k, gain):
        first, second = norm(gain)
        return [s("residual", chunks, 1, k=k, j=0), first, s("residual", chunks, 1, k=k, j=1), second]

    lru = [s("prep"), *norm(V_NG),
           s("x", 4, 1, True, b=0), s("rates"), s("x", 4, 1, b=1), s("gates", 1, 1, b=0, half=0),
           s("x", 4, 1, b=2), s("gates", 1, 1, b=0, half=1),
           s("lru_gate", 4, 1, b=0), s("gate_mul", b=0), s("gates", 1, 1, b=1, half=0),
           s("lru_gate", 4, 1, b=1), s("gates", 1, 1, b=1, half=1), s("gate_mul", b=1),
           s("lru_gate", 4, 1, b=2), s("gates", 1, 1, b=2, half=0), s("gates", 1, 1, b=2, half=1),
           s("gate_mul", b=2), *last_product(LT // KT, "lru", V_NG + DT)]
    fox = [s("forget", 1, 1, True),
           Loop("half", 2, [s("fq", 4, 1), s("fk", 4, 1), s("v", 4, 1, to="fox"), s("attention"),
                            s("fox_gate", 4, 1)]),
           s("residual", 4, 1, k="y", j=0), s("trig"), s("residual", 4, 1, k="y", j=1), s("renorm")]
    layer = [s("enter"),
             Loop("half", 2, [s("qk", 4, 1, True), s("v", 4, 1, to="ret"),
                              s("ret_scores", 0, 1, hh=0), s("ret_scores", 0, 1, hh=1),
                              s("ret_out", 0, 1, hh=0), s("ret_out", 0, 1, hh=1),
                              s("g", 4, 1), s("ret_turn", 0, 1)]),
             Loop("half", 2, [s("gb", 4, 1), s("ret_proj", 4, 1)]),
             Loop("half", 2, [s("cc", 4, 1), s("cu", 4, 1), s("cb", 4, 1), s("ga", 4, 1)]),
             s("merge", 4, 1, j=0), s("merge", 4, 1, j=1), *last_product(4, "m", "mlp"),
             Loop("quarter", 4, [s("up", 4, 1, True, j=0), s("up", 4, 1, j=1),
                                 s("residual", 4, 1, k="y", j=0), s("residual", 4, 1, k="y", j=1)]),
             *norm("next")]
    return lru + fox + [Loop("layer", LAYERS, layer), s("final")]


COUNTED = ("turn", "chunk", "used", "a_hi", "a_lo", "act_out", "vec", "stats", "sumsq_read", "halves")


def step_delta(step):
    out = {k: step.incs.get(k, 0) for k in COUNTED}
    out["turn"], out["chunk"] = step.turns, step.chunks
    out["used"] = max(step.chunks - 1, 0)
    out["halves"] = step.kind == "attention"
    return out


def delta(item):
    if isinstance(item, Step):
        return step_delta(item)
    total = {k: 0 for k in COUNTED}
    for x in item.body:
        for k, v in delta(x).items():
            total[k] += v
    return {k: v * item.count for k, v in total.items()}


class Tally:

    def __init__(self):
        self.fixed = {k: 0 for k in COUNTED}
        self.loops = []
        self.mark = {}
        self.fresh_stats = False

    def value(self, name, plus=0, times=1):
        out = times * self.fixed[name] + plus
        for _, var, per in self.loops:
            if per[name]:
                out = var * (times * per[name]) + out
        return out

    def var(self, name):
        return next(v for n, v, _ in reversed(self.loops) if n == name)

    def walk(self, eng, items, emit):
        for item in items:
            if isinstance(item, Step):
                before = dict(self.fixed)
                emit(item)
                assert self.fixed == before
                for k, v in step_delta(item).items():
                    self.fixed[k] += v
                continue
            per = delta(Loop("", 1, item.body))
            assert per["chunk"] % RING == 0 and per["turn"] % 2 == 0
            before = dict(self.fixed)
            with eng.Fori(0, item.count) as i:
                self.loops.append((item.name, i, per))
                self.walk(eng, item.body, emit)
                self.loops.pop()
            self.fixed = {k: before[k] + item.count * per[k] for k in COUNTED}


def build(nc, stream, xT, vecs, consts, positions, outT, cum_dram):
    steps = schedule()
    n_chunks = sum(delta(x)["chunk"] for x in steps)
    assert stream.shape[0] == n_chunks + AHEAD
    ctx = ExitStack()
    with ctx:
        def sb(name, shape, dt):
            return ctx.enter_context(nc.sbuf_tensor(name, shape, dt))

        def sem(name):
            return ctx.enter_context(nc.semaphore(name))

        x = sb("x", [P, DT, SEQ], F32)
        h_hi = sb("h_hi", [P, DT, SEQ], F32R)
        h_lo = sb("h_lo", [P, DT, SEQ], F32R)
        y_hi = sb("y_hi", [P, LT, SEQ], F32R)
        y_lo = sb("y_lo", [P, LT, SEQ], F32R)
        w_raw = sb("w_raw", [P, RING, CW], F32)
        w_hi = sb("w_hi", [P, RING, CW], F32R)
        w_lo = sb("w_lo", [P, RING, CW], F32R)
        arena = sb("arena", [P, A_WORDS], F32)
        rms = sb("rms", [P, SEQ], F32)
        rms_col = sb("rms_col", [P, TT], F32)
        sumsq = sb("sumsq", [P, SEQ], F32)
        vec_t = sb("vec_t", [P, V_COLS], F32)
        ident = sb("ident", [P, P], F32)
        ones = sb("ones", [P, P], F32)
        ident_b = sb("ident_b", [P, P], BF16)
        mask_b = sb("mask_b", [P, P], BF16)
        ones_b = sb("ones_b", [P, P], BF16)
        pcol = sb("pcol", [P, 2], F32)
        eps_t = sb("eps_t", [P, 1], F32)
        rate = sb("rate", [P, LT], F32)
        rate_m2 = sb("rate_m2", [P, LT], F32)
        small = sb("small", [P, 80], F32)
        junk = sb("junk", [P, P], F32)
        bank = [ctx.enter_context(nc.psum_tensor(f"bank{i}", [P, SEQ], F32)) for i in range(8)]

        def area(at, *shape):
            n = int(np.prod(shape))
            assert at + n <= A_WORDS
            v = arena[:, at:at + n]
            if len(shape) == 2:
                v = v.rearrange("p (a b) -> p a b", a=shape[0])
            return v

        xc = area(0, LT, SEQ)
        u_pad = area(LT * SEQ, 4, SEQ + CONV1 - 1)
        at = LT * SEQ + 4 * (SEQ + CONV1 - 1)
        g_r, g_i, g_t, g_d = (area(at + 1024 * n, 2, SEQ) for n in range(4))
        gate_own = area(at + 4096, 4, SEQ)

        def gate_t(b, n):
            return gate_own[:, n, :] if b == 1 else u_pad[:, n, 0:SEQ]
        fq, fk = area(0, 4, SEQ), area(4 * SEQ, 4, SEQ)
        v_tok = area(8 * SEQ, TT, SEQ)
        probs = area(6144, 2, TRI)
        probs_t = area(6144 + 2 * TRI, TRI)
        AUG = 6144 + 3 * TRI
        cum_rows = arena[0:3, AUG:AUG + HEADS * SEQ // 2].bitcast(BF16).rearrange("p (h t) -> p h t", h=HEADS)
        qk = area(0, 4, SEQ)
        rv = area(2048, TT, SEQ)
        sg = area(4096, 4, SEQ)
        st = area(6144, 2, TRI)
        cos_r, sin_r = area(6144 + 2 * TRI, SEQ), area(6144 + 2 * TRI + SEQ, SEQ)
        swap = area(6144 + 2 * TRI + 2 * SEQ, 2, SEQ)
        m_t = area(0, DT, SEQ)
        ga_t = area(4096, DT, SEQ)
        z_pad = area(8192, 4, SEQ + CONV2 - 1)
        tmp2 = area(8192 + 4 * (SEQ + CONV2 - 1), 2, SEQ)
        decay = area(A_TAIL, RH, SEQ)
        cos_t, sin_t = area(A_TAIL + RH * SEQ, SEQ), area(A_TAIL + RH * SEQ + SEQ, SEQ)
        up_t = area(0, 4, SEQ)
        xsq = area(0, 2, SEQ)

        fox_t = area(6144, 4, SEQ)

        def ft(n):
            return area(6144 + SEQ * n, SEQ)[0:HEADS, :]

        def cum_part(r):
            return area(6144 + SEQ * (4 + r), SEQ // 2)[0:HEADS, :].bitcast(BF16)

        def turned_bank(j):
            return bank[4 + j] if j < 3 else bank[6][:, 2 * P:3 * P]

        def xc_slot(b, n):
            return 4 * b + n

        def tri(j):
            start = sum(SEQ - P * i for i in range(j))
            return start, SEQ - P * j

        inputs_in = sem("inputs_in")
        x_in = [sem(f"x_in{k}") for k in range(DT)]
        decay_in = sem("decay_in")
        raw_loaded = [sem(f"raw_loaded{i}") for i in range(RING)]
        hi_ready = sem("hi_ready")
        lo_ready = sem("lo_ready")
        chunk_used = sem("chunk_used")
        bank_ready = sem("bank_ready")
        evacuated = sem("evacuated")
        a_hi = sem("a_hi")
        a_lo = sem("a_lo")
        act_out = sem("act_out")
        vec = sem("vec")
        stats_ready = sem("stats_ready")
        sumsq_read = sem("sumsq_read")
        consts_ready = sem("consts_ready")
        rates_v = sem("rates_v")
        rates_a = sem("rates_a")
        norm_ready = sem("norm_ready")
        cum_out = sem("cum_out")
        cum_in = sem("cum_in")
        scores_ready = sem("scores_ready")
        max_ready = sem("max_ready")
        exp_ready = sem("exp_ready")
        probs_ready = sem("probs_ready")
        turned = sem("turned")
        turned_act = sem("turned_act")
        turned_vec = sem("turned_vec")
        o_ready = sem("o_ready")
        o_copied = sem("o_copied")
        out_ready = sem("out_ready")
        stored = sem("stored")

        block = ctx.enter_context(nc.Block())

        def wait(eng, s, value):
            if not isinstance(value, int) or value > 0:
                eng.wait_ge(s, value)

        @block.sync
        def _(sp):
            sp.dma_start(vec_t[:, :], vecs).then_inc(inputs_in, 16)
            for c in range(RING):
                sp.dma_start(w_raw[:, c, :], stream[c, :, :]).then_inc(raw_loaded[c], 16)
                if c == 0:
                    sp.dma_start(pcol[:, :], consts[:, K_INVF:K_INVF + 2]).then_inc(inputs_in, 16)
                    sp.dma_start(ident[:, :], consts[:, K_IDENT:K_IDENT + P]).then_inc(inputs_in, 16)
                    sp.dma_start(junk[:, :], consts[:, K_MASK:K_MASK + P]).then_inc(inputs_in, 16)
            rounds = (n_chunks + AHEAD) // RING
            with sp.Fori(1, rounds) as r:
                for slot in range(RING):
                    sp.wait_ge(lo_ready, r * RING + (slot - RING + 1))
                    sp.dma_start(w_raw[:, slot, :], stream[r * RING + slot, :, :])\
                        .then_inc(raw_loaded[slot], 16)
            for c in range(rounds * RING, n_chunks + AHEAD):
                sp.wait_ge(lo_ready, c - RING + 1)
                sp.dma_start(w_raw[:, c % RING, :], stream[c, :, :]).then_inc(raw_loaded[c % RING], 16)
            for k in range(DT):
                sp.wait_ge(out_ready, k + 1)
                sp.dma_start(outT[k * P:(k + 1) * P, :], x[:, k, :]).then_inc(stored, 16)
            sp.wait_ge(stored, 16 * DT)

        @block.gpsimd
        def _(pool):
            T = Tally()
            for item in steps:
                if isinstance(item, Step) and item.kind == "forget":
                    pool.wait_ge(vec, T.value("vec", item.incs["vec"]))
                    for r in range(3):
                        pool.dma_start(cum_dram[r, :, :], cum_part(r)).then_inc(cum_out, 16)
                    pool.wait_ge(cum_out, 48)
                    pool.dma_start(cum_rows, cum_dram).then_inc(cum_in, 16)
                if isinstance(item, Step) and item.kind == "trig":
                    pool.wait_ge(o_copied, HEADS)
                    pool.dma_start(decay, consts[:, K_DECAY:K_DECAY + RH * SEQ]
                                   .rearrange("p (a b) -> p a b", a=RH)).then_inc(decay_in, 16)
                    pool.dma_start(sin_t.bitcast(I32), positions.partition_broadcast(P)).then_inc(decay_in, 16)
                for k, v in delta(item).items():
                    T.fixed[k] += v

        @block.tensor
        def _(pe):
            T = Tally()

            def begin_turn(plus=0):
                wait(pe, evacuated, T.value("turn", 4 * (plus - 1), 4))
                if T.fresh_stats:
                    pe.wait_ge(sumsq_read, T.value("stats"))
                    T.fresh_stats = False
                return 4 * ((T.fixed["turn"] + plus) % 2)

            def product(step, tile, ready=None, tokens_out=False):
                set_ = begin_turn()
                for c in range(step.chunks):
                    slot = (T.fixed["chunk"] + c) % RING
                    if step.args["stats"] and c == step.chunks - 1:
                        statistics(4 - set_)
                        T.fresh_stats = True
                    pe.wait_ge(lo_ready, T.value("chunk", c + 1))
                    for kt in range(KT):
                        k = KT * c + kt
                        if ready:
                            ready(k)
                        a_h, a_l = tile(k)
                        first, last = k == 0, k == KT * step.chunks - 1
                        for n in range(4):
                            out = bank[set_ + n][:, :]
                            if tokens_out:
                                w = slice(kt * 512, kt * 512 + 512)
                                t = slice(n * P, n * P + P)
                                pe.matmul(out, a_h[:, t], w_hi[:, slot, w], start=first, stop=False)
                                pe.matmul(out, a_h[:, t], w_lo[:, slot, w], start=False, stop=False)
                                mm = pe.matmul(out, a_l[:, t], w_hi[:, slot, w], start=False, stop=last)
                            else:
                                w = slice(kt * 512 + n * P, kt * 512 + n * P + P)
                                pe.matmul(out, w_hi[:, slot, w], a_h, start=first, stop=False)
                                pe.matmul(out, w_hi[:, slot, w], a_l, start=False, stop=False)
                                mm = pe.matmul(out, w_lo[:, slot, w], a_h, start=False, stop=last)
                            if last:
                                mm.then_inc(bank_ready, 1)
                    if c < step.chunks - 1:
                        mm.then_inc(chunk_used, 1)

            def statistics(set_):
                pe.wait_ge(vec, T.mark["sumsq"])
                wait(pe, evacuated, T.value("turn", 0, 4))
                pe.matmul(bank[set_ + 3][:, :], ones[:, :], sumsq[:, :], start=True, stop=True)\
                    .then_inc(stats_ready, 1)

            def h_tile(k):
                return h_hi[:, k, :], h_lo[:, k, :]

            def h_ready(k):
                pe.wait_ge(a_lo, T.mark["h0" if k < DT // 2 else "h1"] + (k % (DT // 2) + 1))

            def norm(step):
                if step.args["part"] == 0:
                    T.mark["h0"] = T.value("a_lo")
                else:
                    T.mark["h1"] = T.value("a_lo")
                    T.mark["sumsq"] = T.value("vec", DT // 2)

            def enter(step):
                T.mark["h0"] = T.value("a_lo", -DT)
                T.mark["h1"] = T.value("a_lo", -DT // 2)
                T.mark["sumsq"] = T.value("vec")

            def of_h(step):
                product(step, h_tile, h_ready, tokens_out=step.kind == "v")
                if step.kind == "x":
                    T.mark["xc", step.args["b"]] = T.value("a_lo", 4)

            def gates(step):
                b, half = step.args["b"], step.args["half"]
                slot = T.fixed["chunk"] % RING
                set_ = begin_turn()
                pe.wait_ge(a_lo, T.mark["xc", b])
                pe.wait_ge(lo_ready, T.value("chunk", 1))
                for n in range(4):
                    blk, which = n // 2, n % 2
                    w = slice((2 * which + blk) * P, (2 * which + blk) * P + P)
                    y = xc_slot(b, 2 * half + blk)
                    pe.matmul(bank[set_ + n][:, :], w_hi[:, slot, w], y_hi[:, y, :], start=True, stop=False)
                    pe.matmul(bank[set_ + n][:, :], w_hi[:, slot, w], y_lo[:, y, :], start=False, stop=False)
                    pe.matmul(bank[set_ + n][:, :], w_lo[:, slot, w], y_hi[:, y, :], start=False, stop=True)\
                        .then_inc(bank_ready, 1)

            def of_y(step):
                first = step.args.get("j", 0) == 0
                n_k = KT * step.chunks

                def slot(k):
                    return (8 + k if k < 4 else k - 4) if step.args.get("k") == "m" else k

                def ready(k):
                    if first:
                        pe.wait_ge(a_lo, T.value("a_lo", k + 1 - n_k))

                def all_ready(k):
                    if first and k == 0:
                        pe.wait_ge(a_lo, T.value("a_lo"))

                product(step, lambda k: (y_hi[:, slot(k), :], y_lo[:, slot(k), :]),
                        ready if step.kind == "residual" else all_ready)

            def forget(step):
                set_ = begin_turn()
                slot = T.fixed["chunk"] % RING
                pe.wait_ge(lo_ready, T.value("chunk", 1))
                for k in range(DT):
                    h_ready(k)
                    w = slice(k * P, k * P + P)
                    out = bank[set_][:, :]
                    pe.matmul(out, w_hi[:, slot, w], h_hi[:, k, :], start=k == 0, stop=False)
                    pe.matmul(out, w_hi[:, slot, w], h_lo[:, k, :], start=False, stop=False)
                    mm = pe.matmul(out, w_lo[:, slot, w], h_hi[:, k, :], start=False, stop=k == DT - 1)
                mm.then_inc(bank_ready, 4)
                statistics(set_)

            def attention(step):
                pe.wait_ge(evacuated, T.value("turn", 0, 4))
                pe.wait_ge(cum_in, 16)
                half = T.var("half")

                def heads(count, plus=0):
                    return T.value("halves", plus, count * HEADS // 2)

                def scores(hh):
                    rows = slice(HD * (hh % 2), HD * (hh % 2) + HD)
                    for t in range(TT):
                        if hh:
                            pe.wait_ge(exp_ready, heads(4, 4 * (hh - 1) + t + 1))
                        n = P * (t + 1)
                        out = bank[t][:, 0:n]
                        pe.matmul(out, fq[rows, hh // 2, t * P:n], fk[rows, hh // 2, 0:n], start=True, stop=False)
                        pe.matmul(out, ones_b[0:3, :], cum_rows[0:3, half * (HEADS // 2) + hh, 0:n],
                                  start=False, stop=False)
                        pe.matmul(bank[t][:, t * P:n], ident_b[:, :], mask_b[:, :], start=False, stop=True)\
                            .then_inc(scores_ready, 1)

                def turn(hh):
                    pe.wait_ge(probs_ready, heads(5, 5 * hh + 5))
                    if hh:
                        pe.wait_ge(turned_act, heads(2, 2 * hh))
                        pe.wait_ge(turned_vec, heads(1, hh))
                    for j in range(TT):
                        for t in range(j, TT):
                            at = P * t * (t + 1) // 2 + P * j
                            mm = pe.transpose(turned_bank(j)[:, (t - j) * P:(t - j) * P + P],
                                              probs[:, hh % 2, at:at + P], ident[:, :])
                        if j != 2:
                            mm.then_inc(turned, 1)

                def values(hh):
                    rows = slice(HD * (hh % 2), HD * (hh % 2) + HD)
                    pe.wait_ge(turned_act, heads(2, 2 * hh + 2))
                    pe.wait_ge(turned_vec, heads(1, hh + 1))
                    if hh:
                        pe.wait_ge(o_copied, heads(1, hh))
                    for j in range(TT):
                        at, n = tri(j)
                        mm = pe.matmul(bank[7][rows, P * j:SEQ], v_tok[:, j, hh * HD:hh * HD + HD],
                                       probs_t[:, at:at + n], start=j == 0, stop=j == TT - 1)
                    mm.then_inc(o_ready, 1)

                scores(0)
                for hh in range(HEADS // 2):
                    if hh + 1 < HEADS // 2:
                        scores(hh + 1)
                    if hh:
                        values(hh - 1)
                    turn(hh)
                values(HEADS // 2 - 1)
                pe.wait_ge(o_copied, heads(1, HEADS // 2))

            def ret_scores(step):
                hh = step.args["hh"]
                set_ = begin_turn()
                if hh == 0:
                    pe.wait_ge(vec, T.value("vec"))
                for j in range(TT):
                    n = SEQ - P * j
                    pe.matmul(bank[set_ + j][:, 0:n], qk[:, 2 + hh, P * j:P * j + P], qk[:, hh, P * j:SEQ],
                              start=True, stop=True).then_inc(bank_ready, 1)

            def ret_out(step):
                hh = step.args["hh"]
                set_ = begin_turn()
                pe.wait_ge(evacuated, T.value("turn", -4, 4))
                for t in range(TT):
                    for j in range(t + 1):
                        at = tri(j)[0] + (t - j) * P
                        mm = pe.matmul(bank[set_ + t][:, 0:RV], st[:, hh, at:at + P],
                                       rv[:, j, hh * RV:hh * RV + RV], start=j == 0, stop=j == t)
                    mm.then_inc(bank_ready, 1)

            def ret_turn(step):
                set_ = begin_turn()
                pe.wait_ge(evacuated, T.value("turn", -4, 4))
                for n in range(4):
                    hh, f = n // 2, n % 2
                    for t in range(TT):
                        mm = pe.transpose(bank[set_ + n][:, t * P:t * P + P],
                                          st[:, hh, t * RV + f * P:t * RV + f * P + P], ident[:, :])
                    mm.then_inc(bank_ready, 1)

            def whole_norm(step):
                pe.wait_ge(vec, T.value("vec", DT if step.kind == "renorm" else 0))
                pe.wait_ge(evacuated, T.value("turn", 0, 4))
                pe.matmul(bank[4 * (T.fixed["turn"] % 2)][:, :], ones[:, :], sumsq[:, :], start=True, stop=True)\
                    .then_inc(norm_ready, 1)

            def nothing(step):
                pass

            def prep(step):
                pe.wait_ge(inputs_in, 64)
                pe.wait_ge(consts_ready, CONSTS)

            kinds = {"prep": prep, "norm": norm, "x": of_h, "gates": gates, "lru_gate": of_h,
                     "residual": of_y, "forget": forget, "fq": of_h, "fk": of_h, "v": of_h,
                     "attention": attention, "fox_gate": of_h, "renorm": whole_norm, "trig": nothing,
                     "rates": nothing, "enter": enter, "gate_mul": nothing,
                     "qk": of_h, "ret_scores": ret_scores, "ret_out": ret_out, "ret_turn": ret_turn,
                     "g": of_h, "gb": of_h, "ret_proj": of_y, "cc": of_h, "cu": of_h, "cb": of_h,
                     "ga": of_h, "merge": of_y, "up": of_h, "final": whole_norm}
            T.walk(pe, steps, lambda step: kinds[step.kind](step))

        def split_slots(T, step):
            for n in range(AHEAD, AHEAD + step.chunks):
                yield n, (T.fixed["chunk"] + n) % RING

        @block.scalar
        def _(act):
            T = Tally()
            A = nc.scalar

            def split_ahead(step):
                for n, slot in split_slots(T, step):
                    if n == RING - 1:
                        wait(act, bank_ready, T.value("turn", 0, 4))
                    else:
                        act.wait_ge(chunk_used, T.value("used", n - RING + 1))
                    loaded = 16 * ((T.fixed["chunk"] + n) // RING + 1)
                    for _, var, per in T.loops:
                        loaded = var * (16 * per["chunk"] // RING) + loaded
                    act.wait_ge(raw_loaded[slot], loaded)
                    A.activation(w_hi[:, slot, :], w_raw[:, slot, :], ACT.Copy).then_inc(hi_ready, 1)

            def join():
                wait(act, evacuated, T.value("turn", 0, 4))
                for s, name in ((vec, "vec"), (a_lo, "a_lo"), (act_out, "act_out"), (a_hi, "a_hi")):
                    wait(act, s, T.value(name))

            def banks(n, plus=0):
                act.wait_ge(bank_ready, T.value("turn", 4 * plus + n + 1, 4))

            def statistics(step):
                act.wait_ge(stats_ready, T.value("stats", 1))
                set_ = 4 * (T.fixed["turn"] % 2)
                if step.kind != "forget":
                    set_ = 4 - set_
                A.activation(rms[:, :], bank[set_ + 3][:, :], ACT.Sqrt, scale=1.0 / D,
                             bias=eps_t[:, 0:1]).then_inc(sumsq_read, 1)

            def hi(n, src, slot):
                A.activation(y_hi[:, slot, :], src, ACT.Copy).then_inc(a_hi, 1)

            def prep(step):
                for k in range(DT):
                    act.dma_start(x[:, k, :], xT[k * P:(k + 1) * P, :]).then_inc(x_in[k], 16)
                act.wait_ge(inputs_in, 64)
                act.wait_ge(consts_ready, CONSTS)
                act.wait_ge(raw_loaded[0], 16)
                A.activation(w_hi[:, 0, :], w_raw[:, 0, :], ACT.Copy).then_inc(hi_ready, 1)

            def rates(step):
                act.wait_ge(rates_v, 1)
                A.activation(small[:, 0:LT], small[:, 0:LT], ACT.Exp, scale=-1.0).then_inc(rates_a, 1)

            def gain_column(step, k):
                g = step.args["gain"]
                if isinstance(g, int):
                    return vec_t[:, g + k:g + k + 1]
                base = V_LAYER + {"next": L_COLS + L_MIX, "mlp": L_MLP}[g] + k
                return vec_t[:, bass.ds(T.var("layer") * L_COLS + base, 1)]

            def norm(step):
                first = T.fixed["turn"] == 0
                for i in range(DT // 2):
                    k = step.args["part"] * DT // 2 + i
                    if first:
                        act.wait_ge(x_in[k], 16)
                    A.activation(h_hi[:, k, :], x[:, k, :], ACT.Copy, scale=gain_column(step, k))\
                        .then_inc(a_hi, 1)
                    square(k, i)
                    if first and k < AHEAD - 1:
                        act.wait_ge(raw_loaded[k + 1], 16)
                        A.activation(w_hi[:, k + 1, :], w_raw[:, k + 1, :], ACT.Copy).then_inc(hi_ready, 1)

            def square(k, i, before=0):
                if i >= 2:
                    act.wait_ge(vec, T.value("vec", before + i - 1))
                A.activation(xsq[:, i % 2, :], x[:, k, :], ACT.Square).then_inc(act_out, 1)

            def x_step(step):
                b = step.args["b"]
                vb = 1 + TT if step.args["stats"] else 0
                for n in range(4):
                    col = V_CW + (CONV1 - 1) * LT + 4 * b + n
                    bias = V_CBIAS + 4 * b + n
                    act.wait_ge(evacuated, T.value("turn", n + 1, 4))
                    A.activation(xc[:, 4 * b + n, :], u_pad[:, n, CONV1 - 1:], ACT.Identity,
                                 scale=vec_t[:, col:col + 1], bias=vec_t[:, bias:bias + 1]).then_inc(act_out, 1)
                for n in range(4):
                    act.wait_ge(vec, T.value("vec", vb + 8 + n + 1))
                    hi(n, xc[:, 4 * b + n, :], xc_slot(b, n))

            def gates(step):
                first = 4 * step.args["b"] + 2 * step.args["half"]
                set_ = 4 * (T.fixed["turn"] % 2)
                if first == 0:
                    act.wait_ge(rates_v, RATES_V)
                for q in range(2):
                    for n, (to, bias) in enumerate(((g_r, V_BA), (g_i, V_BX))):
                        banks(2 * q + n)
                        A.activation(to[:, q, :], bank[set_ + 2 * q + n][:, :], ACT.Sigmoid,
                                     bias=vec_t[:, bias + first + q:bias + first + q + 1]).then_inc(act_out, 1)
                act.wait_ge(act_out, T.value("act_out", 4))
                for to, scale, func in ((g_t, rate, ACT.Tanh), (g_d, rate_m2, ACT.Exp)):
                    for q in range(2):
                        A.activation(to[:, q, :], g_r[:, q, :], func, scale=scale[:, first + q:first + q + 1])\
                            .then_inc(act_out, 1)
                act.wait_ge(vec, T.value("vec", 2))
                A.activation(g_t, g_t, ACT.Sqrt, scale=-1.0).then_inc(act_out, 1)

            def in_place(tile, func):
                for n in range(4):
                    act.wait_ge(evacuated, T.value("turn", n + 1, 4))
                    A.activation(tile(n), tile(n), func).then_inc(act_out, 1)

            def split_vec(tile, slot, first):
                for n in range(4):
                    act.wait_ge(vec, T.value("vec", first(n)))
                    hi(n, tile(n), slot(n))

            def lru_gate(step):
                b = step.args["b"]
                in_place(lambda n: gate_t(b, n), ACT.Silu)

            def gate_mul(step):
                b = step.args["b"]
                split_vec(lambda n: gate_t(b, n), lambda n: 4 * b + n, lambda n: n + 1)

            def fox_gate(step):
                half = T.var("half")
                in_place(lambda n: fox_t[:, n, :], ACT.Silu)
                split_vec(lambda n: fox_t[:, n, :], lambda n: half * 4 + n, lambda n: n + 1)

            def forget(step):
                act.wait_ge(vec, T.value("vec", 1 + TT + 2))
                A.activation(ft(1), ft(1), ACT.Exp, scale=-1.0).then_inc(act_out, 1)

            def attention(step):
                def heads(count, plus=0):
                    return T.value("halves", plus, count * HEADS // 2)

                def exps(hh):
                    sm = 32 * (hh % 2)
                    if hh >= 2:
                        act.wait_ge(turned, heads(3, 3 * (hh - 1)))
                    for t in range(TT):
                        act.wait_ge(max_ready, heads(8, 8 * hh + 2 * t + 2))
                        at = P * t * (t + 1) // 2
                        A.activation(probs[:, hh % 2, at:at + P * (t + 1)], bank[t][:, 0:P * (t + 1)], ACT.Exp,
                                     bias=small[:, sm + 4 + t:sm + 5 + t],
                                     accum_out=small[:, sm + 8 + t:sm + 9 + t]).then_inc(exp_ready, 1)

                def copies(hh):
                    if hh:
                        act.wait_ge(o_ready, heads(1, hh))
                    for j in range(2):
                        act.wait_ge(turned, heads(3, 3 * hh + j + 1))
                        at, n = tri(j)
                        A.activation(probs_t[:, at:at + n], turned_bank(j)[:, 0:n], ACT.Copy)\
                            .then_inc(turned_act, 1)

                exps(0)
                for hh in range(HEADS // 2):
                    if hh + 1 < HEADS // 2:
                        exps(hh + 1)
                    copies(hh)

            def take_root():
                A.activation(rms[:, :], bank[4 * (T.fixed["turn"] % 2)][:, :], ACT.Sqrt, scale=1.0 / D,
                             bias=eps_t[:, 0:1]).then_inc(act_out, 1)

            def renorm(step):
                for k in range(DT):
                    square(k, k)
                act.wait_ge(norm_ready, 1)
                take_root()
                for k in range(DT):
                    act.wait_ge(vec, T.value("vec", DT + 1 + 2 * k + 1 if k == 0 else DT + 1 + 2 * k))
                    A.activation(h_hi[:, k, :], x[:, k, :], ACT.Copy,
                                 scale=vec_t[:, V_LAYER + L_MIX + k:V_LAYER + L_MIX + k + 1]).then_inc(a_hi, 1)
                    A.activation(xsq[:, k % 2, :], x[:, k, :], ACT.Square).then_inc(act_out, 1)

            def final(step):
                act.wait_ge(norm_ready, 2)
                take_root()

            def trig(step):
                act.wait_ge(vec, T.value("vec", 10))
                A.activation(sin_t, area(1024, SEQ), ACT.Sin, scale=pcol[:, 1:2]).then_inc(act_out, 1)
                act.wait_ge(vec, T.value("vec", 19))
                A.activation(cos_t, area(1536, SEQ), ACT.Sin).then_inc(act_out, 1)

            def qk_step(step):
                vb = 1 + TT
                set_ = 4 * (T.fixed["turn"] % 2)
                for n in range(4):
                    banks(n)
                    if n >= 2:
                        act.wait_ge(vec, T.value("vec", vb + 2 + 2 * (n - 1)))
                    for a, b in ((0, RQK // 2), (RQK // 2, 0)):
                        A.activation(swap[a:a + RQK // 2, n % 2, :], bank[set_ + n][b:b + RQK // 2, :],
                                     ACT.Copy).then_inc(act_out, 1)

            def ret_out(step):
                act.wait_ge(vec, T.value("vec", TT + 6))
                A.activation(small[:, 72:76], small[:, 64:68], ACT.Sqrt, scale=1.0 / RV, bias=eps_t[:, 0:1])\
                    .then_inc(act_out, 1)

            def ret_turn(step):
                half = T.var("half")
                for n in range(4):
                    act.wait_ge(evacuated, T.value("turn", n + 1, 4))
                    hi(n, sg[:, n, :], half * 4 + n)

            def g_step(step):
                in_place(lambda n: sg[:, n, :], ACT.Silu)

            def gb_step(step):
                half = T.var("half")
                in_place(lambda n: m_t[:, half * 4 + n, :], ACT.Sigmoid)

            def ga_step(step):
                half = T.var("half")
                in_place(lambda n: ga_t[:, half * 4 + n, :], ACT.Sigmoid)

            def cb_step(step):
                half = T.var("half")
                split_vec(lambda n: tmp2[:, n % 2, :], lambda n: half * 4 + n,
                          lambda n: 8 * (n // 2) + 6 + n % 2 + 1)

            def merge(step):
                j = step.args["j"]
                split_vec(lambda n: ga_t[:, 4 * j + n, :], lambda n: 8 + n if j == 0 else n, lambda n: n + 1)

            def up(step):
                vb = 1 + TT if step.args["stats"] else 0
                split_vec(lambda n: up_t[:, n, :], lambda n: 4 * step.args["j"] + n, lambda n: vb + n + 1)

            kinds = {"prep": prep, "norm": norm, "x": x_step, "gates": gates, "lru_gate": lru_gate,
                     "forget": forget, "attention": attention, "fox_gate": fox_gate,
                     "renorm": renorm, "trig": trig, "qk": qk_step, "ret_out": ret_out,
                     "rates": rates, "gate_mul": gate_mul,
                     "ret_turn": ret_turn, "g": g_step, "gb": gb_step, "ga": ga_step, "cb": cb_step,
                     "merge": merge, "up": up, "final": final}

            def emit(step):
                split_ahead(step)
                if step.kind in kinds:
                    join()
                    if step.args["stats"]:
                        statistics(step)
                    kinds[step.kind](step)

            T.walk(act, steps, emit)

        @block.vector
        def _(dve):
            T = Tally()
            V = nc.vector

            def split_ahead(step):
                for n, slot in split_slots(T, step):
                    dve.wait_ge(hi_ready, T.value("chunk", n + 1))
                    V.tensor_tensor(w_lo[:, slot, :], w_raw[:, slot, :], w_hi[:, slot, :].bitcast(F32),
                                    ALU.subtract).then_inc(lo_ready, 1)

            def join():
                wait(dve, evacuated, T.value("turn", 0, 4))
                for s, name in ((vec, "vec"), (a_lo, "a_lo"), (act_out, "act_out"), (a_hi, "a_hi")):
                    wait(dve, s, T.value(name))

            def banks(n, plus=0):
                dve.wait_ge(bank_ready, T.value("turn", 4 * plus + n + 1, 4))

            def got(n):
                dve.wait_ge(vec, T.value("vec", n))

            def read(n):
                dve.wait_ge(evacuated, T.value("turn", n + 1, 4))

            def acted(n):
                dve.wait_ge(act_out, T.value("act_out", n))

            def the_bank(n):
                return bank[4 * (T.fixed["turn"] % 2) + n]

            def evacuate(tile):
                for n in range(4):
                    banks(n)
                    V.tensor_tensor(tile(n), the_bank(n)[:, :], rms[:, :], ALU.mult).then_inc(evacuated, 1)

            def split_lo(tile, slot):
                for n in range(4):
                    dve.wait_ge(a_hi, T.value("a_hi", n + 1))
                    V.tensor_tensor(y_lo[:, slot(n), :], tile(n), y_hi[:, slot(n), :].bitcast(F32),
                                    ALU.subtract).then_inc(a_lo, 1)

            def statistics():
                dve.wait_ge(sumsq_read, T.value("stats", 1))
                V.reciprocal(rms[:, :], rms[:, :]).then_inc(vec, 1)
                for t in range(TT):
                    got(1 + t)
                    V.tensor_tensor_reduce(junk[:, :], rms[:, t * P:t * P + P], ident[:, :], 1.0, 0.0,
                                           ALU.mult, ALU.add, rms_col[:, t:t + 1]).then_inc(vec, 1)
                got(1 + TT)

            def prep(step):
                V.memset(ones_b[:, :], 1.0).then_inc(consts_ready, 1)
                V.memset(ones[:, :], 1.0).then_inc(consts_ready, 1)
                V.memset(eps_t[:, :], EPS).then_inc(consts_ready, 1)
                V.memset(u_pad[:, :, 0:CONV1 - 1], 0.0).then_inc(consts_ready, 1)
                dve.wait_ge(inputs_in, 64)
                V.tensor_copy(mask_b[:, :], junk[:, :]).then_inc(consts_ready, 1)
                V.tensor_copy(ident_b[:, :], ident[:, :]).then_inc(consts_ready, 1)
                dve.wait_ge(consts_ready, CONSTS)
                first_lo(0)

            def first_lo(c):
                dve.wait_ge(hi_ready, c + 1)
                V.tensor_tensor(w_lo[:, c, :], w_raw[:, c, :], w_hi[:, c, :].bitcast(F32),
                                ALU.subtract).then_inc(lo_ready, 1)

            def rates(step):
                count = [0]

                def link(ins):
                    count[0] += 1
                    ins.then_inc(rates_v, 1)
                    dve.wait_ge(rates_v, count[0])

                a = vec_t[:, V_AP:V_AP + LT]
                c0, c1, c2, c3 = (small[:, LT * n:LT * n + LT] for n in range(4))
                link(V.scalar_tensor_tensor(out=c0, in0=a, scalar=-1.0, in1=a, op0=ALU.mult, op1=ALU.max))
                dve.wait_ge(rates_a, 1)
                link(V.tensor_scalar(c1, c0, 2.0, None, ALU.add))
                link(V.reciprocal(c1, c1))
                link(V.tensor_tensor(c0, c0, c1, ALU.mult))
                link(V.tensor_tensor(c1, c0, c0, ALU.mult))
                link(V.tensor_scalar(c2, c1, ATANH[0], None, ALU.mult))
                for c in ATANH[1:] + [1.0]:
                    link(V.scalar_tensor_tensor(out=c2, in0=c2, scalar=c, in1=c1 if c < 1 else c0,
                                                op0=ALU.add, op1=ALU.mult))
                link(V.tensor_scalar(c3, a, -1.0, 0.0, ALU.mult, ALU.max))
                link(V.scalar_tensor_tensor(out=c3, in0=c2, scalar=2.0, in1=c3, op0=ALU.mult, op1=ALU.add))
                link(V.tensor_scalar(rate[:, :], c3, LRU_C / 2, None, ALU.mult))
                link(V.tensor_scalar(rate_m2[:, :], c3, -LRU_C, None, ALU.mult))
                assert count[0] == RATES_V, count

            def gain_column(step, k):
                g = step.args["gain"]
                if isinstance(g, int):
                    return vec_t[:, g + k:g + k + 1]
                base = V_LAYER + {"next": L_COLS + L_MIX, "mlp": L_MLP}[g] + k
                return vec_t[:, bass.ds(T.var("layer") * L_COLS + base, 1)]

            def lo_of_h(k, i, gain):
                dve.wait_ge(a_hi, T.value("a_hi", i + 1))
                V.scalar_tensor_tensor(out=h_lo[:, k, :], in0=x[:, k, :], scalar=gain,
                                       in1=h_hi[:, k, :].bitcast(F32), op0=ALU.mult,
                                       op1=ALU.subtract).then_inc(a_lo, 1)

            def add_square(k, square, last):
                acted(square)
                if k == 0:
                    V.tensor_copy(sumsq[:, :], xsq[:, 0, :]).then_inc(vec, 1)
                else:
                    got(last)
                    V.tensor_tensor(sumsq[:, :], sumsq[:, :], xsq[:, k % 2, :], ALU.add)\
                        .then_inc(vec, 1)

            def norm(step):
                first = T.fixed["turn"] == 0
                for i in range(DT // 2):
                    k = step.args["part"] * DT // 2 + i
                    lo_of_h(k, i, gain_column(step, k))
                    add_square(k, i + 1, i)
                    if first and k < AHEAD - 1:
                        first_lo(k + 1)

            def x_step(step):
                b = step.args["b"]
                vb = 1 + TT if step.args["stats"] else 0
                evacuate(lambda n: u_pad[:, n, CONV1 - 1:])
                for tap in range(1, CONV1):
                    for n in range(4):
                        if tap == 1:
                            acted(n + 1)
                            read(n)
                        else:
                            got(vb + 4 * (tap - 2) + n + 1)
                        col = V_CW + (CONV1 - 1 - tap) * LT + 4 * b + n
                        at = CONV1 - 1 - tap
                        V.scalar_tensor_tensor(out=xc[:, 4 * b + n, :], in0=u_pad[:, n, at:at + SEQ],
                                               scalar=vec_t[:, col:col + 1], in1=xc[:, 4 * b + n, :],
                                               op0=ALU.mult, op1=ALU.add).then_inc(vec, 1)
                split_lo(lambda n: xc[:, 4 * b + n, :], lambda n: xc_slot(b, n))

            def gates(step):
                blk = 4 * step.args["b"] + 2 * step.args["half"]
                acted(4)
                dve.sem_inc(evacuated, 4)
                acted(8)
                V.scalar_tensor_tensor(out=g_d, in0=g_d, scalar=1.0, in1=g_t, op0=ALU.add,
                                       op1=ALU.mult).then_inc(vec, 1)
                got(1)
                V.scalar_tensor_tensor(out=g_t, in0=g_d, scalar=2.0, in1=g_d, op0=ALU.subtract,
                                       op1=ALU.mult).then_inc(vec, 1)
                V.tensor_tensor(g_i, g_i, xc[:, blk:blk + 2, :], ALU.mult).then_inc(vec, 1)
                got(2)
                V.tensor_scalar(g_d, g_d, -1.0, 1.0, ALU.mult, ALU.add).then_inc(vec, 1)
                got(3)
                acted(9)
                V.tensor_tensor(g_i, g_i, g_t, ALU.mult).then_inc(vec, 1)
                got(5)
                for q in range(2):
                    V.tensor_tensor_scan(xc[:, blk + q, :], g_d[:, q, :], g_i[:, q, :], 0.0,
                                         ALU.mult, ALU.add).then_inc(vec, 1)

            def times_and_split(tile, other, slot):
                for n in range(4):
                    V.tensor_tensor(tile(n), tile(n), other(n), ALU.mult).then_inc(vec, 1)
                split_lo(tile, slot)

            def lru_gate(step):
                evacuate(lambda n: gate_t(step.args["b"], n))

            def gate_mul(step):
                b = step.args["b"]
                times_and_split(lambda n: gate_t(b, n), lambda n: xc[:, 4 * b + n, :], lambda n: 4 * b + n)

            def residual(step):
                j = step.args["j"]
                for n in range(4):
                    banks(n)
                    V.tensor_tensor(x[:, 4 * j + n, :], the_bank(n)[:, :], x[:, 4 * j + n, :], ALU.add)\
                        .then_inc(evacuated, 1)

            def forget(step):
                count = [1 + TT]

                def link(ins):
                    count[0] += 1
                    ins.then_inc(vec, 1)
                    got(count[0])

                banks(3)
                V.tensor_tensor(ft(0), the_bank(0)[0:HEADS, :], rms[0:HEADS, :], ALU.mult).then_inc(evacuated, 4)
                read(3)
                link(V.tensor_scalar(ft(0), ft(0), vec_t[0:HEADS, V_BF:V_BF + 1], None, ALU.add))
                link(V.scalar_tensor_tensor(out=ft(1), in0=ft(0), scalar=-1.0, in1=ft(0), op0=ALU.mult,
                                            op1=ALU.max))
                acted(1)
                link(V.tensor_scalar(ft(2), ft(1), 2.0, None, ALU.add))
                link(V.reciprocal(ft(2), ft(2)))
                link(V.tensor_tensor(ft(1), ft(1), ft(2), ALU.mult))
                link(V.tensor_tensor(ft(2), ft(1), ft(1), ALU.mult))
                link(V.tensor_scalar(ft(3), ft(2), ATANH[0], None, ALU.mult))
                for c in ATANH[1:] + [1.0]:
                    link(V.scalar_tensor_tensor(out=ft(3), in0=ft(3), scalar=c, in1=ft(2) if c < 1 else ft(1),
                                                op0=ALU.add, op1=ALU.mult))
                link(V.tensor_scalar(ft(0), ft(0), 0.0, None, ALU.min))
                link(V.scalar_tensor_tensor(out=ft(1), in0=ft(3), scalar=2.0, in1=ft(0), op0=ALU.mult,
                                            op1=ALU.subtract))
                link(V.memset(ft(2), 1.0))
                link(V.tensor_tensor_scan(ft(0), ft(2), ft(1), 0.0, ALU.mult, ALU.add))
                link(V.tensor_copy(cum_part(0), ft(0)))
                link(V.tensor_tensor(ft(0), ft(0), cum_part(0), ALU.subtract))
                link(V.tensor_copy(cum_part(1), ft(0)))
                link(V.tensor_tensor(ft(0), ft(0), cum_part(1), ALU.subtract))
                link(V.tensor_copy(cum_part(2), ft(0)))
                assert count[0] == step.incs["vec"], count

            def fq_step(step):
                for n in range(4):
                    banks(n)
                    V.scalar_tensor_tensor(out=fq[:, n, :], in0=the_bank(n)[:, :], scalar=HD ** -0.5,
                                           in1=rms[:, :], op0=ALU.mult, op1=ALU.mult).then_inc(evacuated, 1)

            def v_step(step):
                to = v_tok if step.args["to"] == "fox" else rv
                for t in range(TT):
                    banks(t)
                    V.tensor_scalar(to[:, t, :], the_bank(t)[:, :], rms_col[:, t:t + 1], None, ALU.mult)\
                        .then_inc(evacuated, 1)

            def attention(step):
                def heads(count, plus=0):
                    return T.value("halves", plus, count * HEADS // 2)

                def maxima(hh):
                    sm = 32 * (hh % 2)
                    for t in range(TT):
                        dve.wait_ge(scores_ready, heads(4, 4 * hh + t + 1))
                        V.tensor_reduce(small[:, sm + t:sm + t + 1], bank[t][:, 0:P * (t + 1)], AX_X, ALU.max)\
                            .then_inc(max_ready, 1)
                        dve.wait_ge(max_ready, heads(8, 8 * hh + 2 * t + 1))
                        if hh >= 2 and t == 0:
                            dve.wait_ge(exp_ready, heads(4, 4 * (hh - 1)))
                        V.tensor_scalar(small[:, sm + 4 + t:sm + 5 + t], small[:, sm + t:sm + t + 1], -1.0, None,
                                        ALU.mult).then_inc(max_ready, 1)

                def normalise(hh):
                    sm = 32 * (hh % 2)
                    dve.wait_ge(exp_ready, heads(4, 4 * hh + 4))
                    V.reciprocal(small[:, sm + 12:sm + 16], small[:, sm + 8:sm + 12]).then_inc(probs_ready, 1)
                    dve.wait_ge(probs_ready, heads(5, 5 * hh + 1))
                    for t in range(TT):
                        at = P * t * (t + 1) // 2
                        p_t = probs[:, hh % 2, at:at + P * (t + 1)]
                        V.tensor_scalar(p_t, p_t, small[:, sm + 12 + t:sm + 13 + t], None, ALU.mult)\
                            .then_inc(probs_ready, 1)

                def copies(hh):
                    if hh:
                        dve.wait_ge(o_ready, heads(1, hh))
                    dve.wait_ge(turned, heads(3, 3 * hh + 3))
                    at, n = tri(2)[0], 3 * P
                    V.tensor_copy(probs_t[:, at:at + n], bank[6][:, 0:n]).then_inc(turned_vec, 1)

                def output(hh):
                    rows = slice(HD * (hh % 2), HD * (hh % 2) + HD)
                    dve.wait_ge(o_ready, heads(1, hh + 1))
                    V.tensor_copy(fq[rows, hh // 2, :], bank[7][rows, :]).then_inc(o_copied, 1)

                maxima(0)
                normalise(0)
                for hh in range(HEADS // 2):
                    if hh + 1 < HEADS // 2:
                        maxima(hh + 1)
                    if hh:
                        output(hh - 1)
                    copies(hh)
                    if hh + 1 < HEADS // 2:
                        normalise(hh + 1)
                output(HEADS // 2 - 1)
                dve.wait_ge(o_copied, heads(1, HEADS // 2))

            def fox_gate(step):
                half = T.var("half")
                evacuate(lambda n: fox_t[:, n, :])
                acted(4)
                times_and_split(lambda n: fox_t[:, n, :], lambda n: fq[:, n, :], lambda n: half * 4 + n)

            def renorm(step):
                for k in range(DT):
                    add_square(k, k + 1, k)
                acted(DT + 1)
                V.reciprocal(rms[:, :], rms[:, :]).then_inc(vec, 1)
                got(DT + 1)

                def scaled(k):
                    V.scalar_tensor_tensor(out=x[:, k, :], in0=x[:, k, :], scalar=vec_t[:, V_FG + k:V_FG + k + 1],
                                           in1=rms[:, :], op0=ALU.mult, op1=ALU.mult).then_inc(vec, 1)

                scaled(0)
                for k in range(DT):
                    if k + 1 < DT:
                        scaled(k + 1)
                    lo_of_h(k, k, vec_t[:, V_LAYER + L_MIX + k:V_LAYER + L_MIX + k + 1])
                    add_square(k, DT + 1 + k + 1, DT + 1 + 2 * k + 1)

            def final(step):
                acted(1)
                V.reciprocal(rms[:, :], rms[:, :]).then_inc(vec, 1)
                got(1)
                for k in range(DT):
                    V.scalar_tensor_tensor(out=x[:, k, :], in0=x[:, k, :], scalar=vec_t[:, V_NF + k:V_NF + k + 1],
                                           in1=rms[:, :], op0=ALU.mult, op1=ALU.mult).then_inc(out_ready, 1)

            def trig(step):
                count = [0]

                def link(ins):
                    count[0] += 1
                    ins.then_inc(vec, 1)
                    got(count[0])

                angle, k_t, r_s, r_c = (area(SEQ * n, SEQ) for n in range(4))
                dve.wait_ge(decay_in, 32)
                link(V.tensor_copy(cos_t, sin_t.bitcast(I32)))
                link(V.tensor_scalar(angle, cos_t, pcol[:, 0:1], None, ALU.mult))

                def reduce(out, quarter):
                    link(V.tensor_scalar(k_t, angle, 1 / (2 * math.pi), quarter, ALU.mult, ALU.add))
                    link(V.tensor_scalar(k_t, k_t, MAGIC, None, ALU.add))
                    link(V.tensor_scalar(k_t, k_t, MAGIC, None, ALU.subtract))
                    for n, part in enumerate(two_pi_parts()):
                        link(V.scalar_tensor_tensor(out=out, in0=k_t, scalar=-part, in1=out if n else angle,
                                                    op0=ALU.mult, op1=ALU.add))
                top = 3.1415925
                reduce(r_s, 0.0)
                link(V.tensor_scalar(r_s, r_s, top, -top, ALU.min, ALU.max))
                reduce(r_c, 0.25)
                link(V.tensor_scalar(r_c, r_c, math.pi / 2, top, ALU.add, ALU.min))
                link(V.tensor_scalar(r_c, r_c, -top, None, ALU.max))
                assert count[0] == 19, count

            def qk_step(step):
                vb = 1 + TT
                V.tensor_tensor(cos_r, cos_t, rms[:, :], ALU.mult).then_inc(vec, 1)
                V.tensor_tensor(sin_r, sin_t, rms[:, :], ALU.mult).then_inc(vec, 1)
                got(vb + 2)
                for n in range(4):
                    acted(2 * n + 2)
                    V.tensor_tensor(swap[:, n % 2, :], swap[:, n % 2, :], sin_r, ALU.mult).then_inc(vec, 1)
                    V.tensor_tensor(qk[:, n, :], the_bank(n)[:, :], cos_r, ALU.mult).then_inc(evacuated, 1)
                    got(vb + 2 + 2 * n + 1)
                    read(n)
                    V.tensor_tensor(qk[:, n, :], qk[:, n, :], swap[:, n % 2, :], ALU.add).then_inc(vec, 1)

            def ret_scores(step):
                hh = step.args["hh"]
                half = T.var("half")
                for j in range(TT):
                    at, n = tri(j)
                    banks(j)
                    V.scalar_tensor_tensor(out=st[:, hh, at:at + n], in0=the_bank(j)[:, 0:n],
                                           scalar=RQK ** -0.5, in1=decay[:, half * 2 + hh, 0:n],
                                           op0=ALU.mult, op1=ALU.mult).then_inc(evacuated, 1)

            def ret_out(step):
                hh = step.args["hh"]
                for t in range(TT):
                    banks(t)
                    V.bn_stats(small[:, 32 + 6 * t:38 + 6 * t], the_bank(t)[:, 0:RV]).then_inc(vec, 1)
                parts = small[:, 32:32 + 6 * TT].rearrange("p (t s) -> p t s", s=6)
                diff, mean, var = small[:, 56:60], small[:, 60:64], small[:, 64:68]
                got(TT)
                V.tensor_tensor(diff, parts[:, :, 1], parts[:, :, 4], ALU.subtract).then_inc(vec, 1)
                V.tensor_tensor(mean, parts[:, :, 1], parts[:, :, 4], ALU.add).then_inc(vec, 1)
                V.tensor_tensor(var, parts[:, :, 2], parts[:, :, 5], ALU.add).then_inc(vec, 1)
                got(TT + 1)
                V.scalar_tensor_tensor(out=diff, in0=diff, scalar=RV / 4, in1=diff, op0=ALU.mult,
                                       op1=ALU.mult).then_inc(vec, 1)
                got(TT + 2)
                V.tensor_scalar(mean, mean, 0.5, None, ALU.mult).then_inc(vec, 1)
                got(TT + 4)
                V.tensor_tensor(var, var, diff, ALU.add).then_inc(vec, 1)
                acted(1)
                V.reciprocal(small[:, 76:80], small[:, 72:76]).then_inc(vec, 1)
                got(TT + 7)
                for t in range(TT):
                    V.tensor_scalar(st[:, hh, t * RV:t * RV + RV], the_bank(t)[:, 0:RV],
                                    small[:, 60 + t:61 + t], small[:, 76 + t:77 + t],
                                    ALU.subtract, ALU.mult).then_inc(evacuated, 1)

            def layer_column(at):
                return vec_t[:, bass.ds(T.var("layer") * L_COLS + at, 1)]

            def ret_turn(step):
                half = T.var("half")
                for n in range(4):
                    banks(n)
                    col = vec_t[:, bass.ds(T.var("layer") * L_COLS + (half * 4 + (V_LAYER + L_RN + n)), 1)]
                    V.scalar_tensor_tensor(out=sg[:, n, :], in0=the_bank(n)[:, :], scalar=col, in1=sg[:, n, :],
                                           op0=ALU.mult, op1=ALU.mult).then_inc(evacuated, 1)
                split_lo(lambda n: sg[:, n, :], lambda n: half * 4 + n)

            def g_step(step):
                evacuate(lambda n: sg[:, n, :])

            def gb_step(step):
                half = T.var("half")
                evacuate(lambda n: m_t[:, half * 4 + n, :])

            def ga_step(step):
                half = T.var("half")
                evacuate(lambda n: ga_t[:, half * 4 + n, :])

            def ret_proj(step):
                half = T.var("half")
                for n in range(4):
                    banks(n)
                    m = m_t[:, half * 4 + n, :]
                    V.tensor_tensor(m, the_bank(n)[:, :], m, ALU.mult).then_inc(evacuated, 1)

            def cc_step(step):
                V.memset(z_pad[:, :, 0:CONV2 - 1], 0.0).then_inc(vec, 1)
                evacuate(lambda n: z_pad[:, n, CONV2 - 1:])

            def cu_step(step):
                for n in range(4):
                    banks(n)
                    if n >= 2:
                        got(n - 1)
                    V.tensor_tensor(tmp2[:, n % 2, :], the_bank(n)[:, :], rms[:, :], ALU.mult).then_inc(evacuated, 1)
                    read(n)
                    z = z_pad[:, n, CONV2 - 1:]
                    V.tensor_tensor(z, z, tmp2[:, n % 2, :], ALU.mult).then_inc(vec, 1)

            def cb_step(step):
                half = T.var("half")
                for pair in range(2):
                    vb = 8 * pair
                    if pair:
                        dve.wait_ge(a_lo, T.value("a_lo", 2))
                    for tap in range(CONV2):
                        for q in range(2):
                            n = 2 * pair + q
                            col = vec_t[:, bass.ds(T.var("layer") * L_COLS + (
                                half * 4 + (V_LAYER + L_CW + (CONV2 - 1 - tap) * DT + n)), 1)]
                            z = z_pad[:, n, CONV2 - 1 - tap:CONV2 - 1 - tap + SEQ]
                            if tap == 0:
                                V.tensor_scalar(tmp2[:, q, :], z, col, None, ALU.mult).then_inc(vec, 1)
                            else:
                                got(vb + 2 * tap - 2 + q + 1)
                                V.scalar_tensor_tensor(out=tmp2[:, q, :], in0=z, scalar=col, in1=tmp2[:, q, :],
                                                       op0=ALU.mult, op1=ALU.add).then_inc(vec, 1)
                    for q in range(2):
                        n = 2 * pair + q
                        banks(n)
                        got(vb + 4 + q + 1)
                        V.tensor_tensor(tmp2[:, q, :], the_bank(n)[:, :], tmp2[:, q, :], ALU.mult)\
                            .then_inc(evacuated, 1)
                    for q in range(2):
                        read(2 * pair + q)
                        V.tensor_tensor(tmp2[:, q, :], tmp2[:, q, :], rms[:, :], ALU.mult).then_inc(vec, 1)
                    for q in range(2):
                        n = 2 * pair + q
                        dve.wait_ge(a_hi, T.value("a_hi", n + 1))
                        V.tensor_tensor(y_lo[:, half * 4 + n, :], tmp2[:, q, :],
                                        y_hi[:, half * 4 + n, :].bitcast(F32), ALU.subtract).then_inc(a_lo, 1)

            def merge(step):
                j = step.args["j"]
                for n in range(4):
                    banks(n)
                    g = ga_t[:, 4 * j + n, :]
                    V.tensor_tensor(g, the_bank(n)[:, :], g, ALU.mult).then_inc(evacuated, 1)
                for n in range(4):
                    read(n)
                    g = ga_t[:, 4 * j + n, :]
                    V.tensor_tensor(g, g, m_t[:, 4 * j + n, :], ALU.add).then_inc(vec, 1)
                split_lo(lambda n: ga_t[:, 4 * j + n, :], lambda n: 8 + n if j == 0 else n)

            def up(step):
                evacuate(lambda n: up_t[:, n, :])
                for n in range(4):
                    read(n)
                    V.scalar_tensor_tensor(out=up_t[:, n, :], in0=up_t[:, n, :], scalar=0.0, in1=up_t[:, n, :],
                                           op0=ALU.max, op1=ALU.mult).then_inc(vec, 1)
                split_lo(lambda n: up_t[:, n, :], lambda n: 4 * step.args["j"] + n)

            kinds = {"prep": prep, "norm": norm, "x": x_step, "gates": gates, "lru_gate": lru_gate,
                     "residual": residual, "forget": forget, "fq": fq_step,
                     "fk": lambda step: evacuate(lambda n: fk[:, n, :]), "v": v_step,
                     "attention": attention, "fox_gate": fox_gate, "renorm": renorm, "trig": trig,
                     "rates": rates, "gate_mul": gate_mul,
                     "qk": qk_step, "ret_scores": ret_scores, "ret_out": ret_out, "ret_turn": ret_turn,
                     "g": g_step, "gb": gb_step, "ret_proj": ret_proj, "cc": cc_step, "cu": cu_step,
                     "cb": cb_step, "ga": ga_step, "merge": merge, "up": up, "final": final}

            def emit(step):
                if step.kind not in kinds:
                    return
                split_ahead(step)
                join()
                if step.args["stats"]:
                    statistics()
                kinds[step.kind](step)

            T.walk(dve, steps, emit)



def order_of_weights(lru_w_in, lru_wa, lru_wx, lru_w_out, fox_w_in, fox_w_out, w_in, w_conv_out,
                     w_ret_out, w_o, w_up, w_down):
    def group(w, columns, rows=None):
        w = w[rows] if rows is not None else w
        cols = np.concatenate([w[:, a:a + n] for a, n in columns], axis=1)
        return cols.reshape(-1, KT, P, 512).transpose(0, 2, 1, 3).reshape(-1, P, CW)

    out = []
    for kind, args in flat_order():
        b = args.get("b", 0)
        half = args.get("half", 0)
        layer = args.get("layer", 0)
        j = args.get("j", 0)
        if kind == "x":
            out.append(group(lru_w_in, [(512 * b, 512)]))
        elif kind == "gates":
            blocks = slice(4 * b + 2 * half, 4 * b + 2 * half + 2)
            both = np.concatenate([lru_wa[blocks], lru_wx[blocks]])
            out.append(np.zeros((1, P, CW), np.float32))
            out[-1][0, :, 0:4 * P] = both.transpose(1, 0, 2).reshape(P, 4 * P)
        elif kind == "lru_gate":
            out.append(group(lru_w_in, [(LRU_W + 512 * b, 512)]))
        elif kind == "residual" and args["k"] == "lru":
            out.append(group(lru_w_out, [(512 * j, 512)]))
        elif kind == "residual" and "layer" not in args:
            out.append(group(fox_w_out, [(512 * j, 512)]))
        elif kind == "residual" and args["k"] == "m":
            out.append(group(w_o[layer], [(512 * j, 512)]))
        elif kind == "residual":
            q = args["quarter"]
            out.append(group(w_down[layer], [(512 * j, 512)], slice(1024 * q, 1024 * q + 1024)))
        elif kind == "forget":
            w = np.zeros((D, P), fox_w_in.dtype)
            w[:, 0:HEADS] = fox_w_in[:, 4 * D:]
            out.append(w.reshape(DT, P, P).transpose(1, 0, 2).reshape(1, P, CW))
        elif kind in ("fq", "fk", "fox_gate") or (kind == "v" and "layer" not in args):
            at = {"fq": 0, "fk": D, "v": 2 * D, "fox_gate": 3 * D}[kind]
            out.append(group(fox_w_in, [(at + 512 * half, 512)]))
        elif kind == "qk":
            out.append(group(w_in[layer], [(CQ + 256 * half, 256), (CK + 256 * half, 256)]))
        elif kind in ("v", "g", "gb", "cc", "cu", "cb", "ga"):
            at = {"v": CV, "g": CG, "gb": CGB, "cc": CC, "cu": CU, "cb": CB, "ga": CGA}[kind]
            out.append(group(w_in[layer], [(at + 512 * half, 512)]))
        elif kind == "ret_proj":
            out.append(group(w_ret_out[layer], [(512 * half, 512)]))
        elif kind == "merge":
            out.append(group(w_conv_out[layer], [(512 * j, 512)]))
        elif kind == "up":
            out.append(group(w_up[layer], [(1024 * args["quarter"] + 512 * j, 512)]))
    out.append(np.zeros((AHEAD, P, CW), np.float32))
    return np.concatenate(out)


def flat_order():
    def walk(items, env):
        for item in items:
            if isinstance(item, Loop):
                for i in range(item.count):
                    yield from walk(item.body, {**env, item.name: i})
            else:
                yield item.kind, {**env, **item.args}
    return walk(schedule(), {})


def shape_constants():
    out = np.zeros((P, K_COLS), np.float32)
    half = RQK // 2
    inv = np.float32(ROPE_BASE) ** (-np.arange(half, dtype=np.float32) / np.float32(half))
    out[:, K_INVF] = np.tile(inv, 2)
    out[:, K_SIGN] = np.repeat([-1.0, 1.0], half)
    out[:, K_IDENT:K_IDENT + P] = np.eye(P)
    row, col = np.arange(P)[:, None], np.arange(P)[None, :]
    out[:, K_MASK:K_MASK + P] = np.where(col > row, -1e30, 0.0)
    rel = (np.arange(SEQ)[None, :] - np.arange(P)[:, None]).astype(np.float64)
    for h in range(RH):
        log_gamma = np.log1p(-(2.0 ** (-5.0 - h)))
        out[:, K_DECAY + h * SEQ:K_DECAY + (h + 1) * SEQ] = np.where(
            rel >= 0, np.exp(log_gamma * np.maximum(rel, 0)), 0.0)
    return out


def kernel(**inputs):
    from concourse import bacc
    from concourse.bass_utils import run_bass_kernel_spmd

    a = {k: np.asarray(v) for k, v in inputs.items()}

    def columns(*vectors):
        return np.concatenate([v.reshape(-1, P).T for v in vectors], axis=1)

    b_f = np.zeros((P, 1), np.float32)
    b_f[0:HEADS, 0] = a["fox_b_f"][0]
    vecs = [columns(a["norm_g"][0], a["norm_g"][1], a["final_g"], *a["lru_conv_w"][0], a["lru_conv_b"][0],
                    a["lru_ba"][0], a["lru_bx"][0], a["lru_a_param"][0]), b_f]
    for i in range(LAYERS):
        vecs.append(columns(a["norm_mix_2"][i], a["norm_mlp_2"][i], *a["conv_w_2"][i], a["ret_norm_2"][i]))
    vecs.append(columns(a["norm_final_2"]))
    arrays = {
        "stream": order_of_weights(a["lru_w_in"][0], a["lru_wa"][0], a["lru_wx"][0], a["lru_w_out"][0],
                                   a["fox_w_in"][0], a["fox_w_out"][0], a["w_in_2"], a["w_conv_out_2"],
                                   a["w_ret_out_2"], a["w_o_2"], a["w_up_2"], a["w_down_2"]),
        "x_t": np.ascontiguousarray(a["x"][0].T),
        "vecs": np.ascontiguousarray(np.concatenate(vecs, axis=1)),
        "consts": shape_constants(),
        "positions": a["positions_2"][0],
    }
    assert arrays["vecs"].shape[1] == V_COLS
    nc = bacc.Bacc("TRN2", target_bir_lowering=False, num_devices=1)
    args = [nc.dram_tensor(f"in_{k}", v.shape, mybir.dt.from_np(v.dtype), kind="ExternalInput").ap()
            for k, v in arrays.items()]
    out = nc.dram_tensor("out_t", (D, SEQ), F32, kind="ExternalOutput").ap()
    scratch = nc.dram_tensor("cum_parts", (3, HEADS, SEQ), BF16).ap()
    build(nc, *args, out, scratch)
    r = run_bass_kernel_spmd(nc, [{f"in_{k}": v for k, v in arrays.items()}], core_ids=[0])
    return np.ascontiguousarray(r.results[0]["out_t"].T)[None]
```

```python
import math
from contextlib import ExitStack

import numpy as np

import concourse.bass as bass
from concourse import mybir
from concourse.alu_op_type import AluOpType as ALU

F32 = mybir.dt.float32
F32R = mybir.dt.float32r
BF16 = mybir.dt.bfloat16
I32 = mybir.dt.int32
ACT = mybir.ActivationFunctionType
AX_X = mybir.AxisListType.X

P = 128
SEQ = 512
D = 1024
DT = D // P
TT = SEQ // P
EPS = 1e-6
LRU_W = 1536
LT = LRU_W // P
LRU_C = 8.0
CONV1 = 4
HEADS = 16
HD = 64
CONV2 = 3
RH = 4
RQK = 128
RV = 256
D_FF = 4096
LAYERS = 2
ROPE_BASE = 10000.0
CB, CC, CU, CQ, CK, CV, CG, CGA, CGB = (int(v) for v in np.cumsum(
    [0, D, D, D, RH * RQK, RH * RQK, RH * RV, RH * RV, D]))

KT = 2
CW = KT * 512
RING = 4
AHEAD = 3
GROUP = DT // KT
TRI = SEQ * (TT + 1) // 2

V_NG = 0
V_FG = V_NG + 2 * DT
V_CW = V_FG + DT
V_CBIAS = V_CW + CONV1 * LT
V_BA = V_CBIAS + LT
V_BX = V_BA + LT
V_AP = V_BX + LT
V_BF = V_AP + LT
V_LAYER = V_BF + 1
L_MIX, L_MLP, L_CW, L_RN = 0, DT, 2 * DT, 2 * DT + CONV2 * DT
L_COLS = L_RN + DT
V_NF = V_LAYER + LAYERS * L_COLS
V_COLS = V_NF + DT
K_INVF, K_SIGN, K_IDENT, K_ONES, K_MASK, K_DECAY = 0, 1, 2, 2 + P, 2 + 2 * P, 2 + 3 * P
K_COLS = K_DECAY + RH * SEQ

A_TAIL = 11276
A_WORDS = A_TAIL + RH * SEQ + 2 * SEQ

RATES_V = 16
CONSTS = 6
MAGIC = float(1.5 * 2 ** 23)
ATANH = [1 / 13, 1 / 11, 1 / 9, 1 / 7, 1 / 5, 1 / 3]


def two_pi_parts():
    parts, rest = [], 2 * math.pi
    for _ in range(3):
        unit = 2.0 ** (math.floor(math.log2(rest)) - 7)
        parts.append(math.floor(rest / unit) * unit)
        rest -= parts[-1]
    return parts + [float(np.float32(rest))]



class Step:
    def __init__(self, kind, chunks=0, turns=0, incs=None, **args):
        self.kind, self.chunks, self.turns, self.args = kind, chunks, turns, args
        self.incs = incs or {}


class Loop:
    def __init__(self, name, count, body):
        self.name, self.count, self.body = name, count, body


SPLIT = {"a_hi": 4, "a_lo": 4}
INCS = {
    "prep": {}, "rates": {}, "enter": {},
    "norm": {"a_hi": DT // 2, "a_lo": DT // 2, "act_out": DT // 2, "vec": DT // 2},
    "x": {},
    "taps": {"act_out": 4},
    "conv": {"vec": 12, **SPLIT},
    "gates": {},
    "input_gate": {"act_out": 5, "vec": 4},
    "scan": {"vec": 3},
    "lru_gate": {"act_out": 4},
    "gate_mul": {"vec": 4, **SPLIT},
    "residual": {},
    "forget": {"act_out": 1, "vec": 22 + TT},
    "fq": {"act_out": 4, "vec": 4}, "fk": {"act_out": 4, "vec": 4}, "v": {},
    "first_head": {}, "attention": {}, "last_head": {},
    "fox_gate": {"act_out": 4, "vec": 4, **SPLIT},
    "squares": {"act_out": DT // 2, "vec": DT // 2},
    "renorm": {"act_out": DT + DT // 2 + 1, "vec": 2 * DT + DT // 2 + 1, "a_hi": DT, "a_lo": DT},
    "trig": {"act_out": 2, "vec": 19},
    "qk": {"act_out": 8, "vec": 10},
    "ret_scores": {},
    "ret_out": {"act_out": 1, "vec": TT + 7},
    "ret_turn": SPLIT,
    "g": {"act_out": 4},
    "gb": {"act_out": 4},
    "ret_proj": {},
    "cc": {"vec": 1},
    "cu": {"vec": 4},
    "cb": {"vec": 16, **SPLIT},
    "ga": {"act_out": 4},
    "merge": {"vec": 4, **SPLIT},
    "up": {"vec": 4, **SPLIT},
    "final": {"act_out": 1, "vec": 1},
}
STATS = {"stats": 1, "sumsq_read": 1, "vec": 1 + TT}


def schedule():
    def s(kind, chunks=0, turns=0, stats=False, **args):
        incs = dict(INCS[kind])
        if stats:
            for k, v in STATS.items():
                incs[k] = incs.get(k, 0) + v
        return Step(kind, chunks, turns, incs, stats=stats, **args)

    def norm(gain):
        return [s("norm", gain=gain, part=0), s("norm", gain=gain, part=1)]

    def open_and_close(kind, *between, chunks=4, stats=False, **args):
        n = chunks // 2
        opening = s(kind, n, 0, part="open", **args)
        opening.incs = {}
        return [opening, *between, s(kind, n, 1, stats, part="close", **args)]

    def last_product(chunks, k, gain, **args):
        first, second = norm(gain)
        return [s("residual", chunks, 1, k=k, j=0, **args), first,
                s("residual", chunks, 1, k=k, j=1, **args), second]

    def gates(n):
        at = {"b": n // 2, "half": n % 2}
        return s("gates", 1, 1, **at), s("input_gate", **at), s("scan", **at)

    g = [gates(n) for n in range(6)]
    lru = [s("prep"), *norm(V_NG),
           *open_and_close("x", s("rates"), stats=True, b=0), s("taps", b=0), s("conv", b=0),
           *open_and_close("x", b=1), s("taps", b=1), g[0][0], s("conv", b=1, beside=True),
           *open_and_close("x", g[0][1], b=2), g[0][2], s("taps", b=2), g[1][0], s("conv", b=2, beside=True),
           *open_and_close("lru_gate", g[1][1], b=0), g[1][2], g[2][0], s("gate_mul", b=0, beside=True),
           *open_and_close("lru_gate", g[2][1], b=1), g[2][2], g[3][0],
           *open_and_close("lru_gate", g[3][1], b=2), g[3][2], g[4][0], s("gate_mul", b=1, beside=True),
           *open_and_close("residual", g[4][1], k="lru", b=0, j=0), g[4][2], g[5][0],
           *open_and_close("residual", g[5][1], k="lru", b=0, j=1), g[5][2],
           s("gate_mul", b=2), *last_product(2, "lru", V_NG + DT, b=2)]
    fox = [s("forget", 1, 1, True),
           Loop("half", 2, [s("fq", 4, 1), s("fk", 4, 1),
                            *open_and_close("v", s("first_head"), to="fox"), s("attention"),
                            *open_and_close("fox_gate", s("last_head"))]),
           s("residual", 4, 1, k="y", j=0), s("squares"), s("trig"),
           s("residual", 4, 1, k="y", j=1), s("renorm")]
    layer = [s("enter"),
             Loop("half", 2, [s("qk", 4, 1, True), s("v", 4, 1, to="ret"),
                              s("ret_scores", 0, 1, hh=0), s("ret_scores", 0, 1, hh=1),
                              s("ret_out", 0, 1, hh=0), s("ret_out", 0, 1, hh=1),
                              s("g", 4, 1), s("ret_turn", 0, 1)]),
             Loop("half", 2, [s("gb", 4, 1), s("ret_proj", 4, 1)]),
             Loop("half", 2, [s("cc", 4, 1), s("cu", 4, 1), s("cb", 4, 1), s("ga", 4, 1)]),
             s("merge", 4, 1, j=0), s("merge", 4, 1, j=1), *last_product(4, "m", "mlp"),
             Loop("quarter", 4, [s("up", 4, 1, True, j=0), s("up", 4, 1, j=1),
                                 s("residual", 4, 1, k="y", j=0), s("residual", 4, 1, k="y", j=1)]),
             *norm("next")]
    return lru + fox + [Loop("layer", LAYERS, layer), s("final")]


COUNTED = ("turn", "chunk", "used", "a_hi", "a_lo", "act_out", "vec", "stats", "sumsq_read", "halves")


def step_delta(step):
    out = {k: step.incs.get(k, 0) for k in COUNTED}
    out["turn"], out["chunk"] = step.turns, step.chunks
    out["used"] = step.chunks if step.args.get("part") == "open" else max(step.chunks - 1, 0)
    out["halves"] = step.kind == "last_head"
    return out


def delta(item):
    if isinstance(item, Step):
        return step_delta(item)
    total = {k: 0 for k in COUNTED}
    for x in item.body:
        for k, v in delta(x).items():
            total[k] += v
    return {k: v * item.count for k, v in total.items()}


class Tally:

    def __init__(self):
        self.fixed = {k: 0 for k in COUNTED}
        self.loops = []
        self.mark = {}
        self.fresh_stats = False

    def value(self, name, plus=0, times=1):
        out = times * self.fixed[name] + plus
        for _, var, per in self.loops:
            if per[name]:
                out = var * (times * per[name]) + out
        return out

    def var(self, name):
        return next(v for n, v, _ in reversed(self.loops) if n == name)

    def walk(self, eng, items, emit):
        for item in items:
            if isinstance(item, Step):
                before = dict(self.fixed)
                emit(item)
                assert self.fixed == before
                for k, v in step_delta(item).items():
                    self.fixed[k] += v
                continue
            per = delta(Loop("", 1, item.body))
            assert per["chunk"] % RING == 0 and per["turn"] % 2 == 0
            before = dict(self.fixed)
            with eng.Fori(0, item.count) as i:
                self.loops.append((item.name, i, per))
                self.walk(eng, item.body, emit)
                self.loops.pop()
            self.fixed = {k: before[k] + item.count * per[k] for k in COUNTED}


def build(nc, stream, xT, vecs, consts, positions, outT, cum_dram):
    steps = schedule()
    n_chunks = sum(delta(x)["chunk"] for x in steps)
    assert stream.shape[0] == n_chunks + AHEAD
    ctx = ExitStack()
    with ctx:
        def sb(name, shape, dt):
            return ctx.enter_context(nc.sbuf_tensor(name, shape, dt))

        def sem(name):
            return ctx.enter_context(nc.semaphore(name))

        x = sb("x", [P, DT, SEQ], F32)
        h_hi = sb("h_hi", [P, DT, SEQ], F32R)
        h_lo = sb("h_lo", [P, DT, SEQ], F32R)
        y_hi = sb("y_hi", [P, LT, SEQ], F32R)
        y_lo = sb("y_lo", [P, LT, SEQ], F32R)
        w_raw = sb("w_raw", [P, RING, CW], F32)
        w_hi = sb("w_hi", [P, RING, CW], F32R)
        w_lo = sb("w_lo", [P, RING, CW], F32R)
        arena = sb("arena", [P, A_WORDS], F32)
        rms = sb("rms", [P, SEQ], F32)
        rms_col = sb("rms_col", [P, TT], F32)
        sumsq = sb("sumsq", [P, SEQ], F32)
        vec_t = sb("vec_t", [P, V_COLS], F32)
        ident = sb("ident", [P, P], F32)
        ones = sb("ones", [P, P], F32)
        ident_b = sb("ident_b", [P, P], BF16)
        mask_b = sb("mask_b", [P, P], BF16)
        ones_b = sb("ones_b", [P, P], BF16)
        pcol = sb("pcol", [P, 2], F32)
        eps_t = sb("eps_t", [P, 1], F32)
        rate = sb("rate", [P, LT], F32)
        rate_m2 = sb("rate_m2", [P, LT], F32)
        small = sb("small", [P, 80], F32)
        junk = sb("junk", [P, P], F32)
        bank = [ctx.enter_context(nc.psum_tensor(f"bank{i}", [P, SEQ], F32)) for i in range(8)]

        def area(at, *shape):
            n = int(np.prod(shape))
            assert at + n <= A_WORDS
            v = arena[:, at:at + n]
            if len(shape) == 2:
                v = v.rearrange("p (a b) -> p a b", a=shape[0])
            return v

        xc = area(0, LT, SEQ)
        u_pad = area(LT * SEQ, 4, SEQ + CONV1 - 1)
        at = LT * SEQ + 4 * (SEQ + CONV1 - 1)
        g_r, g_i, g_t, g_d = (area(at + 1024 * n, 2, SEQ) for n in range(4))
        gate_own = area(at + 4096, 4, SEQ)

        def gate_t(b, n):
            return gate_own[:, n, :] if b == 1 else u_pad[:, n, 0:SEQ]
        fq, fk = area(0, 4, SEQ), area(4 * SEQ, 4, SEQ)
        v_tok = area(8 * SEQ, TT, SEQ)
        q_hi, q_lo = y_hi[:, 4:8, :], y_lo[:, 4:8, :]
        k_hi, k_lo = y_hi[:, 8:12, :], y_lo[:, 8:12, :]
        probs = area(6144, 2, TRI)
        probs_t = area(6144 + 2 * TRI, TRI)
        AUG = 6144 + 3 * TRI
        cum_rows = arena[0:3, AUG:AUG + HEADS * SEQ // 2].bitcast(BF16).rearrange("p (h t) -> p h t", h=HEADS)
        qk = area(0, 4, SEQ)
        rv = area(2048, TT, SEQ)
        sg = area(4096, 4, SEQ)
        st = area(6144, 2, TRI)
        cos_r, sin_r = area(6144 + 2 * TRI, SEQ), area(6144 + 2 * TRI + SEQ, SEQ)
        swap = area(6144 + 2 * TRI + 2 * SEQ, 2, SEQ)
        m_t = area(0, DT, SEQ)
        ga_t = area(4096, DT, SEQ)
        z_pad = area(8192, 4, SEQ + CONV2 - 1)
        tmp2 = area(8192 + 4 * (SEQ + CONV2 - 1), 2, SEQ)
        decay = area(A_TAIL, RH, SEQ)
        cos_t, sin_t = area(A_TAIL + RH * SEQ, SEQ), area(A_TAIL + RH * SEQ + SEQ, SEQ)
        up_t = area(0, 4, SEQ)
        xsq = area(0, 2, SEQ)

        fox_t = area(6144, 4, SEQ)

        def ft(n):
            return area(6144 + SEQ * n, SEQ)[0:HEADS, :]

        def quarter(n):
            return area(6144 + 3 * SEQ + P * n, P)

        def cum_part(r):
            return area(6144 + SEQ * (4 + r), SEQ // 2)[0:HEADS, :].bitcast(BF16)

        def turned_bank(j):
            return bank[4 + j] if j < 3 else bank[6][:, 2 * P:3 * P]

        def xc_slot(b, n):
            return 4 * b + n

        def tri(j):
            start = sum(SEQ - P * i for i in range(j))
            return start, SEQ - P * j

        inputs_in = sem("inputs_in")
        x_in = [sem(f"x_in{k}") for k in range(DT)]
        decay_in = sem("decay_in")
        raw_loaded = [sem(f"raw_loaded{i}") for i in range(RING)]
        hi_ready = sem("hi_ready")
        lo_ready = sem("lo_ready")
        chunk_used = sem("chunk_used")
        bank_ready = sem("bank_ready")
        evacuated = sem("evacuated")
        a_hi = sem("a_hi")
        a_lo = sem("a_lo")
        act_out = sem("act_out")
        vec = sem("vec")
        stats_ready = sem("stats_ready")
        sumsq_read = sem("sumsq_read")
        consts_ready = sem("consts_ready")
        rates_v = sem("rates_v")
        rates_a = sem("rates_a")
        norm_ready = sem("norm_ready")
        cum_out = sem("cum_out")
        cum_in = sem("cum_in")
        scores_ready = sem("scores_ready")
        max_ready = sem("max_ready")
        exp_ready = sem("exp_ready")
        probs_ready = sem("probs_ready")
        turned = sem("turned")
        turned_act = sem("turned_act")
        turned_vec = sem("turned_vec")
        o_ready = sem("o_ready")
        o_copied = sem("o_copied")
        out_ready = sem("out_ready")
        stored = sem("stored")

        block = ctx.enter_context(nc.Block())

        def wait(eng, s, value):
            if not isinstance(value, int) or value > 0:
                eng.wait_ge(s, value)

        @block.sync
        def _(sp):
            sp.dma_start(vec_t[:, :], vecs).then_inc(inputs_in, 16)
            for c in range(RING):
                sp.dma_start(w_raw[:, c, :], stream[c, :, :]).then_inc(raw_loaded[c], 16)
                if c == 0:
                    sp.dma_start(pcol[:, :], consts[:, K_INVF:K_INVF + 2]).then_inc(inputs_in, 16)
                    sp.dma_start(ident[:, :], consts[:, K_IDENT:K_IDENT + P]).then_inc(inputs_in, 16)
                    sp.dma_start(junk[:, :], consts[:, K_MASK:K_MASK + P]).then_inc(inputs_in, 16)
            rounds = (n_chunks + AHEAD) // RING
            with sp.Fori(1, rounds) as r:
                for slot in range(RING):
                    sp.wait_ge(lo_ready, r * RING + (slot - RING + 1))
                    sp.dma_start(w_raw[:, slot, :], stream[r * RING + slot, :, :])\
                        .then_inc(raw_loaded[slot], 16)
            for c in range(rounds * RING, n_chunks + AHEAD):
                sp.wait_ge(lo_ready, c - RING + 1)
                sp.dma_start(w_raw[:, c % RING, :], stream[c, :, :]).then_inc(raw_loaded[c % RING], 16)
            for k in range(DT):
                sp.wait_ge(out_ready, k + 1)
                sp.dma_start(outT[k * P:(k + 1) * P, :], x[:, k, :]).then_inc(stored, 16)
            sp.wait_ge(stored, 16 * DT)

        @block.gpsimd
        def _(pool):
            T = Tally()
            for item in steps:
                if isinstance(item, Step) and item.kind == "forget":
                    pool.wait_ge(vec, T.value("vec", item.incs["vec"]))
                    for r in range(3):
                        pool.dma_start(cum_dram[r, :, :], cum_part(r)).then_inc(cum_out, 16)
                    pool.wait_ge(cum_out, 48)
                    pool.dma_start(cum_rows, cum_dram).then_inc(cum_in, 16)
                if isinstance(item, Step) and item.kind == "trig":
                    pool.wait_ge(o_copied, HEADS)
                    pool.dma_start(decay, consts[:, K_DECAY:K_DECAY + RH * SEQ]
                                   .rearrange("p (a b) -> p a b", a=RH)).then_inc(decay_in, 16)
                    pool.dma_start(sin_t.bitcast(I32), positions.partition_broadcast(P)).then_inc(decay_in, 16)
                for k, v in delta(item).items():
                    T.fixed[k] += v

        @block.tensor
        def _(pe):
            T = Tally()

            def begin_turn(plus=0):
                wait(pe, evacuated, T.value("turn", 4 * (plus - 1), 4))
                if T.fresh_stats:
                    pe.wait_ge(sumsq_read, T.value("stats"))
                    T.fresh_stats = False
                return 4 * ((T.fixed["turn"] + plus) % 2)

            def product(step, tile, ready=None, tokens_out=False):
                part = step.args.get("part")
                set_ = 4 * (T.fixed["turn"] % 2) if part == "close" else begin_turn()
                k_at = KT * step.chunks if part == "close" else 0
                for c in range(step.chunks):
                    slot = (T.fixed["chunk"] + c) % RING
                    if step.args["stats"] and c == step.chunks - 1:
                        statistics(4 - set_)
                        T.fresh_stats = True
                    pe.wait_ge(lo_ready, T.value("chunk", c + 1))
                    for kt in range(KT):
                        k = k_at + KT * c + kt
                        if ready:
                            ready(k)
                        a_h, a_l = tile(k)
                        first = k == 0
                        last = part != "open" and c == step.chunks - 1 and kt == KT - 1
                        for n in range(4):
                            out = bank[set_ + n][:, :]
                            if tokens_out:
                                w = slice(kt * 512, kt * 512 + 512)
                                t = slice(n * P, n * P + P)
                                pe.matmul(out, a_h[:, t], w_hi[:, slot, w], start=first, stop=False)
                                pe.matmul(out, a_h[:, t], w_lo[:, slot, w], start=False, stop=False)
                                mm = pe.matmul(out, a_l[:, t], w_hi[:, slot, w], start=False, stop=last)
                            else:
                                w = slice(kt * 512 + n * P, kt * 512 + n * P + P)
                                pe.matmul(out, w_hi[:, slot, w], a_h, start=first, stop=False)
                                pe.matmul(out, w_hi[:, slot, w], a_l, start=False, stop=False)
                                mm = pe.matmul(out, w_lo[:, slot, w], a_h, start=False, stop=last)
                            if last:
                                mm.then_inc(bank_ready, 1)
                    if c < step.chunks - 1 or part == "open":
                        mm.then_inc(chunk_used, 1)

            def statistics(set_):
                pe.wait_ge(vec, T.mark["sumsq"])
                wait(pe, evacuated, T.value("turn", 0, 4))
                pe.matmul(bank[set_ + 3][:, :], ones[:, :], sumsq[:, :], start=True, stop=True)\
                    .then_inc(stats_ready, 1)

            def h_tile(k):
                return h_hi[:, k, :], h_lo[:, k, :]

            def h_ready(k):
                pe.wait_ge(a_lo, T.mark["h0" if k < DT // 2 else "h1"] + (k % (DT // 2) + 1))

            def norm(step):
                if step.args["part"] == 0:
                    T.mark["h0"] = T.value("a_lo")
                else:
                    T.mark["h1"] = T.value("a_lo")
                    T.mark["sumsq"] = T.value("vec", DT // 2)

            def enter(step):
                T.mark["h0"] = T.value("a_lo", -DT)
                T.mark["h1"] = T.value("a_lo", -DT // 2)
                T.mark["sumsq"] = T.value("vec")

            def of_h(step):
                product(step, h_tile, h_ready, tokens_out=step.kind == "v")

            def fox_gate(step):
                of_h(step)
                if step.args["part"] == "close":
                    pe.wait_ge(o_copied, T.value("halves", 0, HEADS // 2))

            def conv(step):
                T.mark["xc", step.args["b"]] = T.value("a_lo", 4)

            def gate_mul(step):
                T.mark["y", step.args["b"]] = T.value("a_lo")

            def gates(step):
                b, half = step.args["b"], step.args["half"]
                slot = T.fixed["chunk"] % RING
                set_ = begin_turn()
                pe.wait_ge(a_lo, T.mark["xc", b])
                pe.wait_ge(lo_ready, T.value("chunk", 1))
                for n in range(4):
                    blk, which = n // 2, n % 2
                    w = slice((2 * which + blk) * P, (2 * which + blk) * P + P)
                    y = xc_slot(b, 2 * half + blk)
                    pe.matmul(bank[set_ + n][:, :], w_hi[:, slot, w], y_hi[:, y, :], start=True, stop=False)
                    pe.matmul(bank[set_ + n][:, :], w_hi[:, slot, w], y_lo[:, y, :], start=False, stop=False)
                    pe.matmul(bank[set_ + n][:, :], w_lo[:, slot, w], y_hi[:, y, :], start=False, stop=True)\
                        .then_inc(bank_ready, 1)

            def of_y(step):
                first = step.args.get("j", 0) == 0
                n_k = KT * step.chunks

                lru = step.args.get("k") == "lru"

                def slot(k):
                    if lru:
                        return 4 * step.args["b"] + k
                    return (8 + k if k < 4 else k - 4) if step.args.get("k") == "m" else k

                def ready(k):
                    if lru:
                        pe.wait_ge(a_lo, T.mark["y", step.args["b"] + k // 4] + (k % 4 + 1))
                    elif first:
                        pe.wait_ge(a_lo, T.value("a_lo", k + 1 - n_k))

                def all_ready(k):
                    if first and k == 0:
                        pe.wait_ge(a_lo, T.value("a_lo"))

                product(step, lambda k: (y_hi[:, slot(k), :], y_lo[:, slot(k), :]),
                        ready if step.kind == "residual" else all_ready)

            def forget(step):
                set_ = begin_turn()
                slot = T.fixed["chunk"] % RING
                pe.wait_ge(lo_ready, T.value("chunk", 1))
                for k in range(DT):
                    h_ready(k)
                    w = slice(k * P, k * P + P)
                    out = bank[set_][:, :]
                    pe.matmul(out, w_hi[:, slot, w], h_hi[:, k, :], start=k == 0, stop=False)
                    pe.matmul(out, w_hi[:, slot, w], h_lo[:, k, :], start=False, stop=False)
                    mm = pe.matmul(out, w_lo[:, slot, w], h_hi[:, k, :], start=False, stop=k == DT - 1)
                mm.then_inc(bank_ready, 4)
                statistics(set_)

            def attention(step):
                half = T.var("half")

                def heads(count, plus=0):
                    return T.value("halves", plus, count * HEADS // 2)

                def scores(hh):
                    rows = slice(HD * (hh % 2), HD * (hh % 2) + HD)
                    for t in range(TT):
                        if hh:
                            pe.wait_ge(exp_ready, heads(4, 4 * (hh - 1) + t + 1))
                        n = P * (t + 1)
                        out = bank[t][:, 0:n]
                        q_cols, pair = slice(t * P, n), hh // 2
                        pe.matmul(out, q_hi[rows, pair, q_cols], k_hi[rows, pair, 0:n], start=True, stop=False)
                        pe.matmul(out, q_hi[rows, pair, q_cols], k_lo[rows, pair, 0:n], start=False, stop=False)
                        pe.matmul(out, q_lo[rows, pair, q_cols], k_hi[rows, pair, 0:n], start=False, stop=False)
                        pe.matmul(out, ones_b[0:3, :], cum_rows[0:3, half * (HEADS // 2) + hh, 0:n],
                                  start=False, stop=False)
                        pe.matmul(bank[t][:, t * P:n], ident_b[:, :], mask_b[:, :], start=False, stop=True)\
                            .then_inc(scores_ready, 1)

                def turn(hh):
                    pe.wait_ge(probs_ready, heads(5, 5 * hh + 5))
                    if hh:
                        pe.wait_ge(turned_act, heads(2, 2 * hh))
                        pe.wait_ge(turned_vec, heads(1, hh))
                    for j in range(TT):
                        for t in range(j, TT):
                            at = P * t * (t + 1) // 2 + P * j
                            mm = pe.transpose(turned_bank(j)[:, (t - j) * P:(t - j) * P + P],
                                              probs[:, hh % 2, at:at + P], ident[:, :])
                        if j != 2:
                            mm.then_inc(turned, 1)

                def values(hh):
                    rows = slice(HD * (hh % 2), HD * (hh % 2) + HD)
                    pe.wait_ge(turned_act, heads(2, 2 * hh + 2))
                    pe.wait_ge(turned_vec, heads(1, hh + 1))
                    if hh:
                        pe.wait_ge(o_copied, heads(1, hh))
                    for j in range(TT):
                        at, n = tri(j)
                        mm = pe.matmul(bank[7][rows, P * j:SEQ], v_tok[:, j, hh * HD:hh * HD + HD],
                                       probs_t[:, at:at + n], start=j == 0, stop=j == TT - 1)
                    mm.then_inc(o_ready, 1)

                pe.wait_ge(evacuated, T.value("turn", 0, 4))
                if step.kind == "first_head":
                    pe.wait_ge(vec, T.value("vec"))
                    pe.wait_ge(cum_in, 16)
                    scores(0)
                if step.kind == "attention":
                    for hh in range(HEADS // 2):
                        if hh + 1 < HEADS // 2:
                            scores(hh + 1)
                        if hh:
                            values(hh - 1)
                        turn(hh)
                if step.kind == "last_head":
                    values(HEADS // 2 - 1)

            def ret_scores(step):
                hh = step.args["hh"]
                set_ = begin_turn()
                if hh == 0:
                    pe.wait_ge(vec, T.value("vec"))
                for j in range(TT):
                    n = SEQ - P * j
                    pe.matmul(bank[set_ + j][:, 0:n], qk[:, 2 + hh, P * j:P * j + P], qk[:, hh, P * j:SEQ],
                              start=True, stop=True).then_inc(bank_ready, 1)

            def ret_out(step):
                hh = step.args["hh"]
                set_ = begin_turn()
                pe.wait_ge(evacuated, T.value("turn", -4, 4))
                for t in range(TT):
                    for j in range(t + 1):
                        at = tri(j)[0] + (t - j) * P
                        mm = pe.matmul(bank[set_ + t][:, 0:RV], st[:, hh, at:at + P],
                                       rv[:, j, hh * RV:hh * RV + RV], start=j == 0, stop=j == t)
                    mm.then_inc(bank_ready, 1)

            def ret_turn(step):
                set_ = begin_turn()
                pe.wait_ge(evacuated, T.value("turn", -4, 4))
                for n in range(4):
                    hh, f = n // 2, n % 2
                    for t in range(TT):
                        mm = pe.transpose(bank[set_ + n][:, t * P:t * P + P],
                                          st[:, hh, t * RV + f * P:t * RV + f * P + P], ident[:, :])
                    mm.then_inc(bank_ready, 1)

            def whole_norm(step):
                pe.wait_ge(vec, T.value("vec", DT // 2 if step.kind == "renorm" else 0))
                pe.wait_ge(evacuated, T.value("turn", 0, 4))
                pe.matmul(bank[4 * (T.fixed["turn"] % 2)][:, :], ones[:, :], sumsq[:, :], start=True, stop=True)\
                    .then_inc(norm_ready, 1)

            def nothing(step):
                pass

            def prep(step):
                pe.wait_ge(inputs_in, 64)
                pe.wait_ge(consts_ready, CONSTS)

            kinds = {"prep": prep, "norm": norm, "x": of_h, "gates": gates, "lru_gate": of_h,
                     "residual": of_y, "forget": forget, "fq": of_h, "fk": of_h, "v": of_h,
                     "first_head": attention, "attention": attention, "last_head": attention,
                     "fox_gate": fox_gate, "renorm": whole_norm, "trig": nothing,
                     "rates": nothing, "enter": enter, "gate_mul": gate_mul, "conv": conv,
                     "taps": nothing, "input_gate": nothing, "scan": nothing, "squares": nothing,
                     "qk": of_h, "ret_scores": ret_scores, "ret_out": ret_out, "ret_turn": ret_turn,
                     "g": of_h, "gb": of_h, "ret_proj": of_y, "cc": of_h, "cu": of_h, "cb": of_h,
                     "ga": of_h, "merge": of_y, "up": of_h, "final": whole_norm}
            T.walk(pe, steps, lambda step: kinds[step.kind](step))

        def split_slots(T, step):
            for n in range(AHEAD, AHEAD + step.chunks):
                yield n, (T.fixed["chunk"] + n) % RING

        @block.scalar
        def _(act):
            T = Tally()
            A = nc.scalar

            part_before = [None]

            def split_ahead(step):
                opened = part_before[0] == "open"
                if step.chunks:
                    part_before[0] = step.args.get("part")
                for n, slot in split_slots(T, step):
                    if n == RING - 1 and not opened:
                        wait(act, bank_ready, T.value("turn", 0, 4))
                    else:
                        act.wait_ge(chunk_used, T.value("used", n - RING + 1))
                    loaded = 16 * ((T.fixed["chunk"] + n) // RING + 1)
                    for _, var, per in T.loops:
                        loaded = var * (16 * per["chunk"] // RING) + loaded
                    act.wait_ge(raw_loaded[slot], loaded)
                    A.activation(w_hi[:, slot, :], w_raw[:, slot, :], ACT.Copy).then_inc(hi_ready, 1)

            def join(step):
                wait(act, evacuated, T.value("turn", -4 if step.args.get("beside") else 0, 4))
                for s, name in ((vec, "vec"), (a_lo, "a_lo"), (act_out, "act_out"), (a_hi, "a_hi")):
                    wait(act, s, T.value(name))

            def banks(n, plus=0):
                act.wait_ge(bank_ready, T.value("turn", 4 * plus + n + 1, 4))

            def statistics(step):
                act.wait_ge(stats_ready, T.value("stats", 1))
                set_ = 4 * (T.fixed["turn"] % 2)
                if step.kind != "forget":
                    set_ = 4 - set_
                A.activation(rms[:, :], bank[set_ + 3][:, :], ACT.Sqrt, scale=1.0 / D,
                             bias=eps_t[:, 0:1]).then_inc(sumsq_read, 1)

            def hi(n, src, slot):
                A.activation(y_hi[:, slot, :], src, ACT.Copy).then_inc(a_hi, 1)

            def prep(step):
                for k in range(DT):
                    act.dma_start(x[:, k, :], xT[k * P:(k + 1) * P, :]).then_inc(x_in[k], 16)
                act.wait_ge(inputs_in, 64)
                act.wait_ge(consts_ready, CONSTS)
                act.wait_ge(raw_loaded[0], 16)
                A.activation(w_hi[:, 0, :], w_raw[:, 0, :], ACT.Copy).then_inc(hi_ready, 1)

            def rates(step):
                act.wait_ge(rates_v, 1)
                A.activation(small[:, 0:LT], small[:, 0:LT], ACT.Exp, scale=-1.0).then_inc(rates_a, 1)

            def gain_column(step, k):
                g = step.args["gain"]
                if isinstance(g, int):
                    return vec_t[:, g + k:g + k + 1]
                base = V_LAYER + {"next": L_COLS + L_MIX, "mlp": L_MLP}[g] + k
                return vec_t[:, bass.ds(T.var("layer") * L_COLS + base, 1)]

            def norm(step):
                first = T.fixed["turn"] == 0
                if step.args["part"] == 1 and not isinstance(step.args["gain"], int):
                    for i in range(DT // 2):
                        square(DT // 2 + i, i)
                    for i in range(DT // 2):
                        k = DT // 2 + i
                        A.activation(h_hi[:, k, :], x[:, k, :], ACT.Copy, scale=gain_column(step, k))\
                            .then_inc(a_hi, 1)
                    return
                for i in range(DT // 2):
                    k = step.args["part"] * DT // 2 + i
                    if first:
                        act.wait_ge(x_in[k], 16)
                    A.activation(h_hi[:, k, :], x[:, k, :], ACT.Copy, scale=gain_column(step, k))\
                        .then_inc(a_hi, 1)
                    square(k, i)
                    if first and k < AHEAD - 1:
                        act.wait_ge(raw_loaded[k + 1], 16)
                        A.activation(w_hi[:, k + 1, :], w_raw[:, k + 1, :], ACT.Copy).then_inc(hi_ready, 1)

            def square(k, i, before=0):
                if i >= 2:
                    act.wait_ge(vec, T.value("vec", before + i - 1))
                A.activation(xsq[:, i % 2, :], x[:, k, :], ACT.Square).then_inc(act_out, 1)

            def taps(step):
                b = step.args["b"]
                for n in range(4):
                    col = V_CW + (CONV1 - 1) * LT + 4 * b + n
                    bias = V_CBIAS + 4 * b + n
                    A.activation(xc[:, 4 * b + n, :], u_pad[:, n, CONV1 - 1:], ACT.Identity,
                                 scale=vec_t[:, col:col + 1], bias=vec_t[:, bias:bias + 1]).then_inc(act_out, 1)

            def conv(step):
                b = step.args["b"]
                for n in range(4):
                    act.wait_ge(vec, T.value("vec", 8 + n + 1))
                    hi(n, xc[:, 4 * b + n, :], xc_slot(b, n))

            def gates(step):
                first = 4 * step.args["b"] + 2 * step.args["half"]
                set_ = 4 * (T.fixed["turn"] % 2)
                for q in range(2):
                    for n, (to, bias) in enumerate(((g_r, V_BA), (g_i, V_BX))):
                        banks(2 * q + n)
                        A.activation(to[:, q, :], bank[set_ + 2 * q + n][:, :], ACT.Sigmoid,
                                     bias=vec_t[:, bias + first + q:bias + first + q + 1]).then_inc(evacuated, 1)

            def input_gate(step):
                first = 4 * step.args["b"] + 2 * step.args["half"]
                if first == 0:
                    act.wait_ge(rates_v, RATES_V)
                for to, scale, func in ((g_t, rate, ACT.Tanh), (g_d, rate_m2, ACT.Exp)):
                    for q in range(2):
                        A.activation(to[:, q, :], g_r[:, q, :], func, scale=scale[:, first + q:first + q + 1])\
                            .then_inc(act_out, 1)
                act.wait_ge(vec, T.value("vec", 2))
                A.activation(g_t, g_t, ACT.Sqrt, scale=-1.0).then_inc(act_out, 1)

            def in_place(tile, func):
                for n in range(4):
                    act.wait_ge(evacuated, T.value("turn", n + 1, 4))
                    A.activation(tile(n), tile(n), func).then_inc(act_out, 1)

            def split_vec(tile, slot, first):
                for n in range(4):
                    act.wait_ge(vec, T.value("vec", first(n)))
                    hi(n, tile(n), slot(n))

            def lru_gate(step):
                b = step.args["b"]
                in_place(lambda n: gate_t(b, n), ACT.Silu)

            def gate_mul(step):
                b = step.args["b"]
                split_vec(lambda n: gate_t(b, n), lambda n: 4 * b + n, lambda n: n + 1)

            def hi_parts(raw, part):
                for n in range(4):
                    act.wait_ge(evacuated, T.value("turn", n + 1, 4))
                    A.activation(part[:, n, :], raw[:, n, :], ACT.Copy).then_inc(act_out, 1)

            def fox_gate(step):
                half = T.var("half")
                in_place(lambda n: fox_t[:, n, :], ACT.Silu)
                split_vec(lambda n: fox_t[:, n, :], lambda n: half * 4 + n, lambda n: n + 1)

            def forget(step):
                act.wait_ge(vec, T.value("vec", 1 + TT + 2))
                A.activation(quarter(1), quarter(1), ACT.Exp, scale=-1.0).then_inc(act_out, 1)

            def attention(step):
                def heads(count, plus=0):
                    return T.value("halves", plus, count * HEADS // 2)

                def exps(hh):
                    sm = 32 * (hh % 2)
                    if hh >= 2:
                        act.wait_ge(turned, heads(3, 3 * (hh - 1)))
                    for t in range(TT):
                        act.wait_ge(max_ready, heads(4, 4 * hh + t + 1))
                        at = P * t * (t + 1) // 2
                        A.activation(probs[:, hh % 2, at:at + P * (t + 1)], bank[t][:, 0:P * (t + 1)], ACT.Exp,
                                     scale=-1.0, bias=small[:, sm + 4 + t:sm + 5 + t],
                                     accum_out=small[:, sm + 8 + t:sm + 9 + t]).then_inc(exp_ready, 1)

                def copies(hh):
                    if hh:
                        act.wait_ge(o_ready, heads(1, hh))
                    for j in range(2):
                        act.wait_ge(turned, heads(3, 3 * hh + j + 1))
                        at, n = tri(j)
                        A.activation(probs_t[:, at:at + n], turned_bank(j)[:, 0:n], ACT.Copy)\
                            .then_inc(turned_act, 1)

                if step.kind == "first_head":
                    exps(0)
                    return
                for hh in range(HEADS // 2):
                    if hh + 1 < HEADS // 2:
                        exps(hh + 1)
                    copies(hh)

            def take_root():
                A.activation(rms[:, :], bank[4 * (T.fixed["turn"] % 2)][:, :], ACT.Sqrt, scale=1.0 / D,
                             bias=eps_t[:, 0:1]).then_inc(act_out, 1)

            def squares(step):
                for k in range(DT // 2):
                    square(k, k)

            def renorm(step):
                for k in range(DT // 2, DT):
                    square(k, k - DT // 2)
                act.wait_ge(norm_ready, 1)
                take_root()
                at = DT // 2 + 1
                for k in range(DT):
                    act.wait_ge(vec, T.value("vec", at + 1 if k == 0 else at + 2 * k))
                    A.activation(h_hi[:, k, :], x[:, k, :], ACT.Copy,
                                 scale=vec_t[:, V_LAYER + L_MIX + k:V_LAYER + L_MIX + k + 1]).then_inc(a_hi, 1)
                    A.activation(xsq[:, k % 2, :], x[:, k, :], ACT.Square).then_inc(act_out, 1)

            def final(step):
                act.wait_ge(norm_ready, 2)
                take_root()

            def trig(step):
                act.wait_ge(vec, T.value("vec", 10))
                A.activation(sin_t, area(1024, SEQ), ACT.Sin, scale=pcol[:, 1:2]).then_inc(act_out, 1)
                act.wait_ge(vec, T.value("vec", 19))
                A.activation(cos_t, area(1536, SEQ), ACT.Sin).then_inc(act_out, 1)

            def qk_step(step):
                vb = 1 + TT
                set_ = 4 * (T.fixed["turn"] % 2)
                for n in range(4):
                    banks(n)
                    if n >= 2:
                        act.wait_ge(vec, T.value("vec", vb + 2 + 2 * (n - 1)))
                    for a, b in ((0, RQK // 2), (RQK // 2, 0)):
                        A.activation(swap[a:a + RQK // 2, n % 2, :], bank[set_ + n][b:b + RQK // 2, :],
                                     ACT.Copy).then_inc(act_out, 1)

            def ret_out(step):
                act.wait_ge(vec, T.value("vec", TT + 6))
                A.activation(small[:, 72:76], small[:, 64:68], ACT.Sqrt, scale=1.0 / RV, bias=eps_t[:, 0:1])\
                    .then_inc(act_out, 1)

            def ret_turn(step):
                half = T.var("half")
                for n in range(4):
                    act.wait_ge(evacuated, T.value("turn", n + 1, 4))
                    hi(n, sg[:, n, :], half * 4 + n)

            def g_step(step):
                in_place(lambda n: sg[:, n, :], ACT.Silu)

            def gb_step(step):
                half = T.var("half")
                in_place(lambda n: m_t[:, half * 4 + n, :], ACT.Sigmoid)

            def ga_step(step):
                half = T.var("half")
                in_place(lambda n: ga_t[:, half * 4 + n, :], ACT.Sigmoid)

            def cb_step(step):
                half = T.var("half")
                split_vec(lambda n: tmp2[:, n % 2, :], lambda n: half * 4 + n,
                          lambda n: 8 * (n // 2) + 6 + n % 2 + 1)

            def merge(step):
                j = step.args["j"]
                split_vec(lambda n: ga_t[:, 4 * j + n, :], lambda n: 8 + n if j == 0 else n, lambda n: n + 1)

            def up(step):
                vb = 1 + TT if step.args["stats"] else 0
                split_vec(lambda n: up_t[:, n, :], lambda n: 4 * step.args["j"] + n, lambda n: vb + n + 1)

            def x_step(step):
                pass

            kinds = {"prep": prep, "norm": norm, "x": x_step, "gates": gates, "lru_gate": lru_gate,
                     "taps": taps, "conv": conv, "input_gate": input_gate, "squares": squares,
                     "forget": forget, "first_head": attention, "attention": attention,
                     "fox_gate": fox_gate, "fq": lambda step: hi_parts(fq, q_hi), "fk": lambda step: hi_parts(fk, k_hi),
                     "renorm": renorm, "trig": trig, "qk": qk_step, "ret_out": ret_out,
                     "rates": rates, "gate_mul": gate_mul,
                     "ret_turn": ret_turn, "g": g_step, "gb": gb_step, "ga": ga_step, "cb": cb_step,
                     "merge": merge, "up": up, "final": final}

            def emit(step):
                split_ahead(step)
                if step.kind in kinds and step.args.get("part") != "open":
                    join(step)
                    if step.args["stats"]:
                        statistics(step)
                    kinds[step.kind](step)

            T.walk(act, steps, emit)

        @block.vector
        def _(dve):
            T = Tally()
            V = nc.vector

            def split_ahead(step):
                for n, slot in split_slots(T, step):
                    dve.wait_ge(hi_ready, T.value("chunk", n + 1))
                    V.tensor_tensor(w_lo[:, slot, :], w_raw[:, slot, :], w_hi[:, slot, :].bitcast(F32),
                                    ALU.subtract).then_inc(lo_ready, 1)

            def join(step):
                wait(dve, evacuated, T.value("turn", -4 if step.args.get("beside") else 0, 4))
                for s, name in ((vec, "vec"), (a_lo, "a_lo"), (act_out, "act_out"), (a_hi, "a_hi")):
                    wait(dve, s, T.value(name))

            def banks(n, plus=0):
                dve.wait_ge(bank_ready, T.value("turn", 4 * plus + n + 1, 4))

            def got(n):
                dve.wait_ge(vec, T.value("vec", n))

            def read(n):
                dve.wait_ge(evacuated, T.value("turn", n + 1, 4))

            def acted(n):
                dve.wait_ge(act_out, T.value("act_out", n))

            def the_bank(n):
                return bank[4 * (T.fixed["turn"] % 2) + n]

            def evacuate(tile):
                for n in range(4):
                    banks(n)
                    V.tensor_tensor(tile(n), the_bank(n)[:, :], rms[:, :], ALU.mult).then_inc(evacuated, 1)

            def split_lo(tile, slot):
                for n in range(4):
                    dve.wait_ge(a_hi, T.value("a_hi", n + 1))
                    V.tensor_tensor(y_lo[:, slot(n), :], tile(n), y_hi[:, slot(n), :].bitcast(F32),
                                    ALU.subtract).then_inc(a_lo, 1)

            def statistics():
                dve.wait_ge(sumsq_read, T.value("stats", 1))
                V.reciprocal(rms[:, :], rms[:, :]).then_inc(vec, 1)
                for t in range(TT):
                    got(1 + t)
                    V.tensor_tensor_reduce(junk[:, :], rms[:, t * P:t * P + P], ident[:, :], 1.0, 0.0,
                                           ALU.mult, ALU.add, rms_col[:, t:t + 1]).then_inc(vec, 1)
                got(1 + TT)

            def prep(step):
                V.memset(ones_b[:, :], 1.0).then_inc(consts_ready, 1)
                V.memset(ones[:, :], 1.0).then_inc(consts_ready, 1)
                V.memset(eps_t[:, :], EPS).then_inc(consts_ready, 1)
                V.memset(u_pad[:, :, 0:CONV1 - 1], 0.0).then_inc(consts_ready, 1)
                dve.wait_ge(inputs_in, 64)
                V.tensor_copy(mask_b[:, :], junk[:, :]).then_inc(consts_ready, 1)
                V.tensor_copy(ident_b[:, :], ident[:, :]).then_inc(consts_ready, 1)
                dve.wait_ge(consts_ready, CONSTS)
                first_lo(0)

            def first_lo(c):
                dve.wait_ge(hi_ready, c + 1)
                V.tensor_tensor(w_lo[:, c, :], w_raw[:, c, :], w_hi[:, c, :].bitcast(F32),
                                ALU.subtract).then_inc(lo_ready, 1)

            def rates(step):
                count = [0]

                def link(ins):
                    count[0] += 1
                    ins.then_inc(rates_v, 1)
                    dve.wait_ge(rates_v, count[0])

                a = vec_t[:, V_AP:V_AP + LT]
                c0, c1, c2, c3 = (small[:, LT * n:LT * n + LT] for n in range(4))
                link(V.scalar_tensor_tensor(out=c0, in0=a, scalar=-1.0, in1=a, op0=ALU.mult, op1=ALU.max))
                dve.wait_ge(rates_a, 1)
                link(V.tensor_scalar(c1, c0, 2.0, None, ALU.add))
                link(V.reciprocal(c1, c1))
                link(V.tensor_tensor(c0, c0, c1, ALU.mult))
                link(V.tensor_tensor(c1, c0, c0, ALU.mult))
                link(V.tensor_scalar(c2, c1, ATANH[0], None, ALU.mult))
                for c in ATANH[1:] + [1.0]:
                    link(V.scalar_tensor_tensor(out=c2, in0=c2, scalar=c, in1=c1 if c < 1 else c0,
                                                op0=ALU.add, op1=ALU.mult))
                link(V.tensor_scalar(c3, a, -1.0, 0.0, ALU.mult, ALU.max))
                link(V.scalar_tensor_tensor(out=c3, in0=c2, scalar=2.0, in1=c3, op0=ALU.mult, op1=ALU.add))
                link(V.tensor_scalar(rate[:, :], c3, LRU_C / 2, None, ALU.mult))
                link(V.tensor_scalar(rate_m2[:, :], c3, -LRU_C, None, ALU.mult))
                assert count[0] == RATES_V, count

            def gain_column(step, k):
                g = step.args["gain"]
                if isinstance(g, int):
                    return vec_t[:, g + k:g + k + 1]
                base = V_LAYER + {"next": L_COLS + L_MIX, "mlp": L_MLP}[g] + k
                return vec_t[:, bass.ds(T.var("layer") * L_COLS + base, 1)]

            def lo_of_h(k, i, gain):
                dve.wait_ge(a_hi, T.value("a_hi", i + 1))
                V.scalar_tensor_tensor(out=h_lo[:, k, :], in0=x[:, k, :], scalar=gain,
                                       in1=h_hi[:, k, :].bitcast(F32), op0=ALU.mult,
                                       op1=ALU.subtract).then_inc(a_lo, 1)

            def add_square(k, square, last):
                acted(square)
                if k == 0:
                    V.tensor_copy(sumsq[:, :], xsq[:, 0, :]).then_inc(vec, 1)
                else:
                    got(last)
                    V.tensor_tensor(sumsq[:, :], sumsq[:, :], xsq[:, k % 2, :], ALU.add)\
                        .then_inc(vec, 1)

            def norm(step):
                first = T.fixed["turn"] == 0
                if step.args["part"] == 1 and not isinstance(step.args["gain"], int):
                    for i in range(DT // 2):
                        add_square(DT // 2 + i, i + 1, i)
                    for i in range(DT // 2):
                        lo_of_h(DT // 2 + i, i, gain_column(step, DT // 2 + i))
                    return
                for i in range(DT // 2):
                    k = step.args["part"] * DT // 2 + i
                    lo_of_h(k, i, gain_column(step, k))
                    add_square(k, i + 1, i)
                    if first and k < AHEAD - 1:
                        first_lo(k + 1)

            def x_step(step):
                evacuate(lambda n: u_pad[:, n, CONV1 - 1:])

            def conv(step):
                b = step.args["b"]
                for tap in range(1, CONV1):
                    for n in range(4):
                        if tap > 1:
                            got(4 * (tap - 2) + n + 1)
                        col = V_CW + (CONV1 - 1 - tap) * LT + 4 * b + n
                        at = CONV1 - 1 - tap
                        V.scalar_tensor_tensor(out=xc[:, 4 * b + n, :], in0=u_pad[:, n, at:at + SEQ],
                                               scalar=vec_t[:, col:col + 1], in1=xc[:, 4 * b + n, :],
                                               op0=ALU.mult, op1=ALU.add).then_inc(vec, 1)
                split_lo(lambda n: xc[:, 4 * b + n, :], lambda n: xc_slot(b, n))

            def input_gate(step):
                blk = 4 * step.args["b"] + 2 * step.args["half"]
                acted(4)
                V.scalar_tensor_tensor(out=g_d, in0=g_d, scalar=1.0, in1=g_t, op0=ALU.add,
                                       op1=ALU.mult).then_inc(vec, 1)
                got(1)
                V.scalar_tensor_tensor(out=g_t, in0=g_d, scalar=2.0, in1=g_d, op0=ALU.subtract,
                                       op1=ALU.mult).then_inc(vec, 1)
                V.tensor_tensor(g_i, g_i, xc[:, blk:blk + 2, :], ALU.mult).then_inc(vec, 1)
                got(2)
                V.tensor_scalar(g_d, g_d, -1.0, 1.0, ALU.mult, ALU.add).then_inc(vec, 1)

            def scan(step):
                blk = 4 * step.args["b"] + 2 * step.args["half"]
                V.tensor_tensor(g_i, g_i, g_t, ALU.mult).then_inc(vec, 1)
                got(1)
                for q in range(2):
                    V.tensor_tensor_scan(xc[:, blk + q, :], g_d[:, q, :], g_i[:, q, :], 0.0,
                                         ALU.mult, ALU.add).then_inc(vec, 1)

            def times_and_split(tile, other, slot):
                for n in range(4):
                    V.tensor_tensor(tile(n), tile(n), other(n), ALU.mult).then_inc(vec, 1)
                split_lo(tile, slot)

            def lru_gate(step):
                evacuate(lambda n: gate_t(step.args["b"], n))

            def gate_mul(step):
                b = step.args["b"]
                times_and_split(lambda n: gate_t(b, n), lambda n: xc[:, 4 * b + n, :], lambda n: 4 * b + n)

            def residual(step):
                j = step.args["j"]
                for n in range(4):
                    banks(n)
                    V.tensor_tensor(x[:, 4 * j + n, :], the_bank(n)[:, :], x[:, 4 * j + n, :], ALU.add)\
                        .then_inc(evacuated, 1)

            def forget(step):
                count = [1 + TT]

                def link(ins):
                    count[0] += 1
                    ins.then_inc(vec, 1)
                    got(count[0])

                banks(3)
                for g in range(TT):
                    rows, cols = slice(32 * g, 32 * g + 32), slice(P * g, P * g + P)
                    V.tensor_tensor(quarter(0)[rows, :], the_bank(0)[rows, cols], rms[rows, cols], ALU.mult)\
                        .then_inc(evacuated, 1)
                read(3)
                f0, f1, f2, f3 = (quarter(n) for n in range(4))
                link(V.tensor_scalar(f0, f0, vec_t[:, V_BF:V_BF + 1], None, ALU.add))
                link(V.scalar_tensor_tensor(out=f1, in0=f0, scalar=-1.0, in1=f0, op0=ALU.mult, op1=ALU.max))
                acted(1)
                link(V.tensor_scalar(f2, f1, 2.0, None, ALU.add))
                link(V.reciprocal(f2, f2))
                link(V.tensor_tensor(f1, f1, f2, ALU.mult))
                link(V.tensor_tensor(f2, f1, f1, ALU.mult))
                link(V.tensor_scalar(f3, f2, ATANH[0], None, ALU.mult))
                for c in ATANH[1:] + [1.0]:
                    link(V.scalar_tensor_tensor(out=f3, in0=f3, scalar=c, in1=f2 if c < 1 else f1,
                                                op0=ALU.add, op1=ALU.mult))
                link(V.tensor_scalar(f0, f0, 0.0, None, ALU.min))
                link(V.scalar_tensor_tensor(out=f1, in0=f3, scalar=-2.0, in1=f0, op0=ALU.mult, op1=ALU.add))
                for g in range(TT):
                    V.tensor_copy(ft(1)[:, P * g:P * g + P], f1[32 * g:32 * g + HEADS, :]).then_inc(vec, 1)
                count[0] += TT
                link(V.memset(ft(2), 1.0))
                link(V.tensor_tensor_scan(ft(0), ft(2), ft(1), 0.0, ALU.mult, ALU.add))
                link(V.tensor_copy(cum_part(0), ft(0)))
                link(V.tensor_tensor(ft(0), ft(0), cum_part(0), ALU.subtract))
                link(V.tensor_copy(cum_part(1), ft(0)))
                link(V.tensor_tensor(ft(0), ft(0), cum_part(1), ALU.subtract))
                link(V.tensor_copy(cum_part(2), ft(0)))
                assert count[0] == step.incs["vec"], count

            def fq_step(step):
                for n in range(4):
                    banks(n)
                    V.scalar_tensor_tensor(out=fq[:, n, :], in0=the_bank(n)[:, :], scalar=-HD ** -0.5,
                                           in1=rms[:, :], op0=ALU.mult, op1=ALU.mult).then_inc(evacuated, 1)
                lo_parts(fq, q_hi, q_lo)

            def fk_step(step):
                evacuate(lambda n: fk[:, n, :])
                lo_parts(fk, k_hi, k_lo)

            def lo_parts(raw, part_hi, part_lo):
                for n in range(4):
                    acted(n + 1)
                    V.tensor_tensor(part_lo[:, n, :], raw[:, n, :], part_hi[:, n, :].bitcast(F32),
                                    ALU.subtract).then_inc(vec, 1)

            def v_step(step):
                to = v_tok if step.args["to"] == "fox" else rv
                for t in range(TT):
                    banks(t)
                    V.tensor_scalar(to[:, t, :], the_bank(t)[:, :], rms_col[:, t:t + 1], None, ALU.mult)\
                        .then_inc(evacuated, 1)

            def attention(step):
                def heads(count, plus=0):
                    return T.value("halves", plus, count * HEADS // 2)

                def maxima(hh):
                    sm = 32 * (hh % 2)
                    if hh >= 2:
                        dve.wait_ge(exp_ready, heads(4, 4 * (hh - 1)))
                    for t in range(TT):
                        dve.wait_ge(scores_ready, heads(4, 4 * hh + t + 1))
                        V.tensor_reduce(small[:, sm + 4 + t:sm + 5 + t], bank[t][:, 0:P * (t + 1)], AX_X, ALU.min)\
                            .then_inc(max_ready, 1)

                def normalise(hh):
                    sm = 32 * (hh % 2)
                    dve.wait_ge(exp_ready, heads(4, 4 * hh + 4))
                    V.reciprocal(small[:, sm + 12:sm + 16], small[:, sm + 8:sm + 12]).then_inc(probs_ready, 1)
                    dve.wait_ge(probs_ready, heads(5, 5 * hh + 1))
                    for t in range(TT):
                        at = P * t * (t + 1) // 2
                        p_t = probs[:, hh % 2, at:at + P * (t + 1)]
                        V.tensor_scalar(p_t, p_t, small[:, sm + 12 + t:sm + 13 + t], None, ALU.mult)\
                            .then_inc(probs_ready, 1)

                def copies(hh):
                    if hh:
                        dve.wait_ge(o_ready, heads(1, hh))
                    dve.wait_ge(turned, heads(3, 3 * hh + 3))
                    at, n = tri(2)[0], 3 * P
                    V.tensor_copy(probs_t[:, at:at + n], bank[6][:, 0:n]).then_inc(turned_vec, 1)

                def output(hh):
                    rows = slice(HD * (hh % 2), HD * (hh % 2) + HD)
                    dve.wait_ge(o_ready, heads(1, hh + 1))
                    V.tensor_copy(fq[rows, hh // 2, :], bank[7][rows, :]).then_inc(o_copied, 1)

                if step.kind == "first_head":
                    maxima(0)
                    normalise(0)
                    return
                if step.kind == "last_head":
                    output(HEADS // 2 - 1)
                    dve.wait_ge(o_copied, heads(1, HEADS // 2))
                    return
                for hh in range(HEADS // 2):
                    if hh + 1 < HEADS // 2:
                        maxima(hh + 1)
                    if hh:
                        output(hh - 1)
                    copies(hh)
                    if hh + 1 < HEADS // 2:
                        normalise(hh + 1)

            def fox_gate(step):
                half = T.var("half")
                evacuate(lambda n: fox_t[:, n, :])
                acted(4)
                times_and_split(lambda n: fox_t[:, n, :], lambda n: fq[:, n, :], lambda n: half * 4 + n)

            def renorm(step):
                half = DT // 2
                for i in range(half):
                    add_square(half + i, i + 1, i)
                acted(half + 1)
                V.reciprocal(rms[:, :], rms[:, :]).then_inc(vec, 1)
                got(half + 1)

                def scaled(k):
                    V.scalar_tensor_tensor(out=x[:, k, :], in0=x[:, k, :], scalar=vec_t[:, V_FG + k:V_FG + k + 1],
                                           in1=rms[:, :], op0=ALU.mult, op1=ALU.mult).then_inc(vec, 1)

                scaled(0)
                for k in range(DT):
                    if k + 1 < DT:
                        scaled(k + 1)
                    lo_of_h(k, k, vec_t[:, V_LAYER + L_MIX + k:V_LAYER + L_MIX + k + 1])
                    add_square(k, half + 1 + k + 1, half + 1 + 2 * k + 1)

            def squares(step):
                for k in range(DT // 2):
                    add_square(k, k + 1, k)

            def final(step):
                acted(1)
                V.reciprocal(rms[:, :], rms[:, :]).then_inc(vec, 1)
                got(1)
                for k in range(DT):
                    V.scalar_tensor_tensor(out=x[:, k, :], in0=x[:, k, :], scalar=vec_t[:, V_NF + k:V_NF + k + 1],
                                           in1=rms[:, :], op0=ALU.mult, op1=ALU.mult).then_inc(out_ready, 1)

            def trig(step):
                count = [0]

                def link(ins):
                    count[0] += 1
                    ins.then_inc(vec, 1)
                    got(count[0])

                angle, k_t, r_s, r_c = (area(SEQ * n, SEQ) for n in range(4))
                dve.wait_ge(decay_in, 32)
                link(V.tensor_copy(cos_t, sin_t.bitcast(I32)))
                link(V.tensor_scalar(angle, cos_t, pcol[:, 0:1], None, ALU.mult))

                def reduce(out, quarter):
                    link(V.tensor_scalar(k_t, angle, 1 / (2 * math.pi), quarter, ALU.mult, ALU.add))
                    link(V.tensor_scalar(k_t, k_t, MAGIC, None, ALU.add))
                    link(V.tensor_scalar(k_t, k_t, MAGIC, None, ALU.subtract))
                    for n, part in enumerate(two_pi_parts()):
                        link(V.scalar_tensor_tensor(out=out, in0=k_t, scalar=-part, in1=out if n else angle,
                                                    op0=ALU.mult, op1=ALU.add))
                top = 3.1415925
                reduce(r_s, 0.0)
                link(V.tensor_scalar(r_s, r_s, top, -top, ALU.min, ALU.max))
                reduce(r_c, 0.25)
                link(V.tensor_scalar(r_c, r_c, math.pi / 2, top, ALU.add, ALU.min))
                link(V.tensor_scalar(r_c, r_c, -top, None, ALU.max))
                assert count[0] == 19, count

            def qk_step(step):
                vb = 1 + TT
                V.tensor_tensor(cos_r, cos_t, rms[:, :], ALU.mult).then_inc(vec, 1)
                V.tensor_tensor(sin_r, sin_t, rms[:, :], ALU.mult).then_inc(vec, 1)
                got(vb + 2)
                for n in range(4):
                    acted(2 * n + 2)
                    V.tensor_tensor(swap[:, n % 2, :], swap[:, n % 2, :], sin_r, ALU.mult).then_inc(vec, 1)
                    V.tensor_tensor(qk[:, n, :], the_bank(n)[:, :], cos_r, ALU.mult).then_inc(evacuated, 1)
                    got(vb + 2 + 2 * n + 1)
                    read(n)
                    V.tensor_tensor(qk[:, n, :], qk[:, n, :], swap[:, n % 2, :], ALU.add).then_inc(vec, 1)

            def ret_scores(step):
                hh = step.args["hh"]
                half = T.var("half")
                for j in range(TT):
                    at, n = tri(j)
                    banks(j)
                    V.scalar_tensor_tensor(out=st[:, hh, at:at + n], in0=the_bank(j)[:, 0:n],
                                           scalar=RQK ** -0.5, in1=decay[:, half * 2 + hh, 0:n],
                                           op0=ALU.mult, op1=ALU.mult).then_inc(evacuated, 1)

            def ret_out(step):
                hh = step.args["hh"]
                for t in range(TT):
                    banks(t)
                    V.bn_stats(small[:, 32 + 6 * t:38 + 6 * t], the_bank(t)[:, 0:RV]).then_inc(vec, 1)
                parts = small[:, 32:32 + 6 * TT].rearrange("p (t s) -> p t s", s=6)
                diff, mean, var = small[:, 56:60], small[:, 60:64], small[:, 64:68]
                got(TT)
                V.tensor_tensor(diff, parts[:, :, 1], parts[:, :, 4], ALU.subtract).then_inc(vec, 1)
                V.tensor_tensor(mean, parts[:, :, 1], parts[:, :, 4], ALU.add).then_inc(vec, 1)
                V.tensor_tensor(var, parts[:, :, 2], parts[:, :, 5], ALU.add).then_inc(vec, 1)
                got(TT + 1)
                V.scalar_tensor_tensor(out=diff, in0=diff, scalar=RV / 4, in1=diff, op0=ALU.mult,
                                       op1=ALU.mult).then_inc(vec, 1)
                got(TT + 2)
                V.tensor_scalar(mean, mean, 0.5, None, ALU.mult).then_inc(vec, 1)
                got(TT + 4)
                V.tensor_tensor(var, var, diff, ALU.add).then_inc(vec, 1)
                acted(1)
                V.reciprocal(small[:, 76:80], small[:, 72:76]).then_inc(vec, 1)
                got(TT + 7)
                for t in range(TT):
                    V.tensor_scalar(st[:, hh, t * RV:t * RV + RV], the_bank(t)[:, 0:RV],
                                    small[:, 60 + t:61 + t], small[:, 76 + t:77 + t],
                                    ALU.subtract, ALU.mult).then_inc(evacuated, 1)

            def layer_column(at):
                return vec_t[:, bass.ds(T.var("layer") * L_COLS + at, 1)]

            def ret_turn(step):
                half = T.var("half")
                for n in range(4):
                    banks(n)
                    col = vec_t[:, bass.ds(T.var("layer") * L_COLS + (half * 4 + (V_LAYER + L_RN + n)), 1)]
                    V.scalar_tensor_tensor(out=sg[:, n, :], in0=the_bank(n)[:, :], scalar=col, in1=sg[:, n, :],
                                           op0=ALU.mult, op1=ALU.mult).then_inc(evacuated, 1)
                split_lo(lambda n: sg[:, n, :], lambda n: half * 4 + n)

            def g_step(step):
                evacuate(lambda n: sg[:, n, :])

            def gb_step(step):
                half = T.var("half")
                evacuate(lambda n: m_t[:, half * 4 + n, :])

            def ga_step(step):
                half = T.var("half")
                evacuate(lambda n: ga_t[:, half * 4 + n, :])

            def ret_proj(step):
                half = T.var("half")
                for n in range(4):
                    banks(n)
                    m = m_t[:, half * 4 + n, :]
                    V.tensor_tensor(m, the_bank(n)[:, :], m, ALU.mult).then_inc(evacuated, 1)

            def cc_step(step):
                V.memset(z_pad[:, :, 0:CONV2 - 1], 0.0).then_inc(vec, 1)
                evacuate(lambda n: z_pad[:, n, CONV2 - 1:])

            def cu_step(step):
                for n in range(4):
                    banks(n)
                    if n >= 2:
                        got(n - 1)
                    V.tensor_tensor(tmp2[:, n % 2, :], the_bank(n)[:, :], rms[:, :], ALU.mult).then_inc(evacuated, 1)
                    read(n)
                    z = z_pad[:, n, CONV2 - 1:]
                    V.tensor_tensor(z, z, tmp2[:, n % 2, :], ALU.mult).then_inc(vec, 1)

            def cb_step(step):
                half = T.var("half")
                for pair in range(2):
                    vb = 8 * pair
                    if pair:
                        dve.wait_ge(a_lo, T.value("a_lo", 2))
                    for tap in range(CONV2):
                        for q in range(2):
                            n = 2 * pair + q
                            col = vec_t[:, bass.ds(T.var("layer") * L_COLS + (
                                half * 4 + (V_LAYER + L_CW + (CONV2 - 1 - tap) * DT + n)), 1)]
                            z = z_pad[:, n, CONV2 - 1 - tap:CONV2 - 1 - tap + SEQ]
                            if tap == 0:
                                V.tensor_scalar(tmp2[:, q, :], z, col, None, ALU.mult).then_inc(vec, 1)
                            else:
                                got(vb + 2 * tap - 2 + q + 1)
                                V.scalar_tensor_tensor(out=tmp2[:, q, :], in0=z, scalar=col, in1=tmp2[:, q, :],
                                                       op0=ALU.mult, op1=ALU.add).then_inc(vec, 1)
                    for q in range(2):
                        n = 2 * pair + q
                        banks(n)
                        got(vb + 4 + q + 1)
                        V.tensor_tensor(tmp2[:, q, :], the_bank(n)[:, :], tmp2[:, q, :], ALU.mult)\
                            .then_inc(evacuated, 1)
                    for q in range(2):
                        read(2 * pair + q)
                        V.tensor_tensor(tmp2[:, q, :], tmp2[:, q, :], rms[:, :], ALU.mult).then_inc(vec, 1)
                    for q in range(2):
                        n = 2 * pair + q
                        dve.wait_ge(a_hi, T.value("a_hi", n + 1))
                        V.tensor_tensor(y_lo[:, half * 4 + n, :], tmp2[:, q, :],
                                        y_hi[:, half * 4 + n, :].bitcast(F32), ALU.subtract).then_inc(a_lo, 1)

            def merge(step):
                j = step.args["j"]
                for n in range(4):
                    banks(n)
                    g = ga_t[:, 4 * j + n, :]
                    V.tensor_tensor(g, the_bank(n)[:, :], g, ALU.mult).then_inc(evacuated, 1)
                for n in range(4):
                    read(n)
                    g = ga_t[:, 4 * j + n, :]
                    V.tensor_tensor(g, g, m_t[:, 4 * j + n, :], ALU.add).then_inc(vec, 1)
                split_lo(lambda n: ga_t[:, 4 * j + n, :], lambda n: 8 + n if j == 0 else n)

            def up(step):
                evacuate(lambda n: up_t[:, n, :])
                for n in range(4):
                    read(n)
                    V.scalar_tensor_tensor(out=up_t[:, n, :], in0=up_t[:, n, :], scalar=0.0, in1=up_t[:, n, :],
                                           op0=ALU.max, op1=ALU.mult).then_inc(vec, 1)
                split_lo(lambda n: up_t[:, n, :], lambda n: 4 * step.args["j"] + n)

            kinds = {"prep": prep, "norm": norm, "x": x_step, "lru_gate": lru_gate,
                     "residual": residual, "forget": forget, "fq": fq_step,
                     "fk": fk_step, "v": v_step,
                     "first_head": attention, "attention": attention, "last_head": attention,
                     "fox_gate": fox_gate, "renorm": renorm, "trig": trig,
                     "rates": rates, "gate_mul": gate_mul, "conv": conv, "input_gate": input_gate,
                     "scan": scan, "squares": squares,
                     "qk": qk_step, "ret_scores": ret_scores, "ret_out": ret_out, "ret_turn": ret_turn,
                     "g": g_step, "gb": gb_step, "ret_proj": ret_proj, "cc": cc_step, "cu": cu_step,
                     "cb": cb_step, "ga": ga_step, "merge": merge, "up": up, "final": final}

            def emit(step):
                split_ahead(step)
                if step.kind not in kinds or step.args.get("part") == "open":
                    return
                join(step)
                if step.args["stats"]:
                    statistics()
                kinds[step.kind](step)

            T.walk(dve, steps, emit)



def order_of_weights(lru_w_in, lru_wa, lru_wx, lru_w_out, fox_w_in, fox_w_out, w_in, w_conv_out,
                     w_ret_out, w_o, w_up, w_down):
    def group(w, columns, rows=None):
        w = w[rows] if rows is not None else w
        cols = np.concatenate([w[:, a:a + n] for a, n in columns], axis=1)
        return cols.reshape(-1, KT, P, 512).transpose(0, 2, 1, 3).reshape(-1, P, CW)

    out = []
    for kind, args in flat_order():
        b = args.get("b", 0)
        half = args.get("half", 0)
        layer = args.get("layer", 0)
        j = args.get("j", 0)
        rows = {"open": slice(0, D // 2), "close": slice(D // 2, D)}.get(args.get("part"))
        if kind == "x":
            out.append(group(lru_w_in, [(512 * b, 512)], rows))
        elif kind == "gates":
            blocks = slice(4 * b + 2 * half, 4 * b + 2 * half + 2)
            both = np.concatenate([lru_wa[blocks], lru_wx[blocks]])
            out.append(np.zeros((1, P, CW), np.float32))
            out[-1][0, :, 0:4 * P] = both.transpose(1, 0, 2).reshape(P, 4 * P)
        elif kind == "lru_gate":
            out.append(group(lru_w_in, [(LRU_W + 512 * b, 512)], rows))
        elif kind == "residual" and args["k"] == "lru":
            out.append(group(lru_w_out, [(512 * j, 512)], rows or slice(512 * b, 512 * b + 512)))
        elif kind == "residual" and "layer" not in args:
            out.append(group(fox_w_out, [(512 * j, 512)]))
        elif kind == "residual" and args["k"] == "m":
            out.append(group(w_o[layer], [(512 * j, 512)]))
        elif kind == "residual":
            q = args["quarter"]
            out.append(group(w_down[layer], [(512 * j, 512)], slice(1024 * q, 1024 * q + 1024)))
        elif kind == "forget":
            w = np.zeros((D, P), fox_w_in.dtype)
            for g in range(TT):
                w[:, 32 * g:32 * g + HEADS] = fox_w_in[:, 4 * D:]
            out.append(w.reshape(DT, P, P).transpose(1, 0, 2).reshape(1, P, CW))
        elif kind in ("fq", "fk", "fox_gate") or (kind == "v" and "layer" not in args):
            at = {"fq": 0, "fk": D, "v": 2 * D, "fox_gate": 3 * D}[kind]
            out.append(group(fox_w_in, [(at + 512 * half, 512)], rows))
        elif kind == "qk":
            out.append(group(w_in[layer], [(CQ + 256 * half, 256), (CK + 256 * half, 256)]))
        elif kind in ("v", "g", "gb", "cc", "cu", "cb", "ga"):
            at = {"v": CV, "g": CG, "gb": CGB, "cc": CC, "cu": CU, "cb": CB, "ga": CGA}[kind]
            out.append(group(w_in[layer], [(at + 512 * half, 512)]))
        elif kind == "ret_proj":
            out.append(group(w_ret_out[layer], [(512 * half, 512)]))
        elif kind == "merge":
            out.append(group(w_conv_out[layer], [(512 * j, 512)]))
        elif kind == "up":
            out.append(group(w_up[layer], [(1024 * args["quarter"] + 512 * j, 512)]))
    out.append(np.zeros((AHEAD, P, CW), np.float32))
    return np.concatenate(out)


def flat_order():
    def walk(items, env):
        for item in items:
            if isinstance(item, Loop):
                for i in range(item.count):
                    yield from walk(item.body, {**env, item.name: i})
            else:
                yield item.kind, {**env, **item.args}
    return walk(schedule(), {})


def shape_constants():
    out = np.zeros((P, K_COLS), np.float32)
    half = RQK // 2
    inv = np.float32(ROPE_BASE) ** (-np.arange(half, dtype=np.float32) / np.float32(half))
    out[:, K_INVF] = np.tile(inv, 2)
    out[:, K_SIGN] = np.repeat([-1.0, 1.0], half)
    out[:, K_IDENT:K_IDENT + P] = np.eye(P)
    row, col = np.arange(P)[:, None], np.arange(P)[None, :]
    out[:, K_MASK:K_MASK + P] = np.where(col > row, 1e30, 0.0)
    rel = (np.arange(SEQ)[None, :] - np.arange(P)[:, None]).astype(np.float64)
    for h in range(RH):
        log_gamma = np.log1p(-(2.0 ** (-5.0 - h)))
        out[:, K_DECAY + h * SEQ:K_DECAY + (h + 1) * SEQ] = np.where(
            rel >= 0, np.exp(log_gamma * np.maximum(rel, 0)), 0.0)
    return out


def kernel(**inputs):
    from concourse import bacc
    from concourse.bass_utils import run_bass_kernel_spmd

    a = {k: np.asarray(v) for k, v in inputs.items()}

    def columns(*vectors):
        return np.concatenate([v.reshape(-1, P).T for v in vectors], axis=1)

    b_f = np.zeros((P, 1), np.float32)
    for g in range(TT):
        b_f[32 * g:32 * g + HEADS, 0] = a["fox_b_f"][0]
    vecs = [columns(a["norm_g"][0], a["norm_g"][1], a["final_g"], *a["lru_conv_w"][0], a["lru_conv_b"][0],
                    a["lru_ba"][0], a["lru_bx"][0], a["lru_a_param"][0]), b_f]
    for i in range(LAYERS):
        vecs.append(columns(a["norm_mix_2"][i], a["norm_mlp_2"][i], *a["conv_w_2"][i], a["ret_norm_2"][i]))
    vecs.append(columns(a["norm_final_2"]))
    arrays = {
        "stream": order_of_weights(a["lru_w_in"][0], a["lru_wa"][0], a["lru_wx"][0], a["lru_w_out"][0],
                                   a["fox_w_in"][0], a["fox_w_out"][0], a["w_in_2"], a["w_conv_out_2"],
                                   a["w_ret_out_2"], a["w_o_2"], a["w_up_2"], a["w_down_2"]),
        "x_t": np.ascontiguousarray(a["x"][0].T),
        "vecs": np.ascontiguousarray(np.concatenate(vecs, axis=1)),
        "consts": shape_constants(),
        "positions": a["positions_2"][0],
    }
    assert arrays["vecs"].shape[1] == V_COLS
    nc = bacc.Bacc("TRN2", target_bir_lowering=False, num_devices=1)
    args = [nc.dram_tensor(f"in_{k}", v.shape, mybir.dt.from_np(v.dtype), kind="ExternalInput").ap()
            for k, v in arrays.items()]
    out = nc.dram_tensor("out_t", (D, SEQ), F32, kind="ExternalOutput").ap()
    scratch = nc.dram_tensor("cum_parts", (3, HEADS, SEQ), BF16).ap()
    build(nc, *args, out, scratch)
    r = run_bass_kernel_spmd(nc, [{f"in_{k}": v for k, v in arrays.items()}], core_ids=[0])
    return np.ascontiguousarray(r.results[0]["out_t"].T)[None]
```
